# Optimizing a Trainium2 kernel written in Bass

```python
import math
import jax, jax.numpy as jnp
from jax import lax
import numpy as np

D_MODEL = 1024
BATCH = 1
SEQ = 256
DEPTH = 2

HEAD_DIM = 64
N_HEADS = D_MODEL // HEAD_DIM
D_FF = 4 * D_MODEL
DECAY_LORA = 64
AAA_LORA = 64
GATE_LORA = 160
N_SHIFT_MIX = 6
BLOCK_Q = 128
N_A_LAYERS = DEPTH // 2
N_B_LAYERS = DEPTH - N_A_LAYERS
NORM_EPS = 1e-6
GN_EPS = 64e-5


def rmsnorm(x, g, eps=NORM_EPS):
    xf = x.astype(jnp.float32)
    y = xf * lax.rsqrt(jnp.mean(xf * xf, axis=-1, keepdims=True) + eps)
    return (y * g.astype(jnp.float32)).astype(x.dtype)

def to_heads(t):
    b, s, _ = t.shape
    return t.reshape(b, s, N_HEADS, HEAD_DIM)

def rwkv7_time_mix(h, mu, w_rkv, w0, w1, w2, a0, a1, a2, g1, g2,
                   k_k, k_a, r_k, lnx_w, lnx_b, w_o):
    B, T, D = h.shape
    f32 = jnp.float32
    x_prev = jnp.pad(h[:, :-1], ((0, 0), (1, 0), (0, 0)))
    xx = x_prev - h
    xs = h[None] + xx[None] * mu[:, None, None, :]
    x_r, x_w, x_k, x_v, x_a, x_g = xs[0], xs[1], xs[2], xs[3], xs[4], xs[5]
    rkv = jnp.einsum('pbtd,pde->pbte', jnp.stack([x_r, x_k, x_v]), w_rkv)
    r, k, v = rkv[0], rkv[1], rkv[2]
    w = -jax.nn.softplus(-(w0 + jnp.tanh(x_w @ w1) @ w2)) - 0.5
    decay = jnp.exp(-jnp.exp(w.astype(f32)))
    a = jax.nn.sigmoid(a0 + (x_a @ a1) @ a2)
    g = jax.nn.sigmoid(x_g @ g1) @ g2
    kk = to_heads((k * k_k).astype(f32))
    kk = kk / jnp.maximum(jnp.linalg.norm(kk, axis=-1, keepdims=True), 1e-12)
    k = k * (1.0 + (a - 1.0) * k_a)

    r_h = to_heads(r).astype(f32)
    k_h = to_heads(k).astype(f32)
    v_h = to_heads(v).astype(f32)
    a_h = to_heads(a).astype(f32)
    w_h = to_heads(decay)
    b_h = kk * a_h

    def step(S, inp):
        r_t, w_t, k_t, v_t, kk_t, b_t = inp
        sa = jnp.einsum('bhvk,bhk->bhv', S, -kk_t)
        S = (S * w_t[:, :, None, :] + sa[..., None] * b_t[:, :, None, :]
             + v_t[..., None] * k_t[:, :, None, :])
        y_t = jnp.einsum('bhvk,bhk->bhv', S, r_t)
        return S, y_t

    tm = lambda t: jnp.moveaxis(t, 1, 0)
    S0 = jnp.zeros((B, N_HEADS, HEAD_DIM, HEAD_DIM), f32)
    _, y = lax.scan(step, S0, (tm(r_h), tm(w_h), tm(k_h), tm(v_h), tm(kk), tm(b_h)))
    y = jnp.moveaxis(y, 0, 1)

    mean = jnp.mean(y, axis=-1, keepdims=True)
    var = jnp.mean(jnp.square(y - mean), axis=-1, keepdims=True)
    y = (y - mean) * lax.rsqrt(var + GN_EPS)
    y = y.reshape(B, T, D) * lnx_w.astype(f32) + lnx_b.astype(f32)
    bonus = jnp.sum(r_h * k_h * r_k.astype(f32), axis=-1, keepdims=True) * v_h
    y = (y + bonus.reshape(B, T, D)).astype(h.dtype) * g
    return y @ w_o

def shared_kv(x, kv_norm_g, kv_w, kv_f_bias, k_norm_g):
    D = x.shape[-1]
    h = rmsnorm(x, kv_norm_g)
    proj = h @ kv_w
    k = to_heads(proj[..., :D])
    v = to_heads(proj[..., D:2 * D])
    f_logit = (proj[..., 2 * D:] + kv_f_bias).astype(jnp.float32)
    k = rmsnorm(k, k_norm_g)
    log_f = jax.nn.log_sigmoid(f_logit)
    c = jnp.cumsum(jnp.transpose(log_f, (0, 2, 1)), axis=-1)
    return jnp.transpose(k, (0, 2, 1, 3)), jnp.transpose(v, (0, 2, 1, 3)), c

def forgetting_attention(q, k, v, c):
    T = q.shape[2]
    scale = 1.0 / math.sqrt(HEAD_DIM)
    outs = []
    for s in range(0, T, BLOCK_Q):
        e = s + BLOCK_Q
        logits = jnp.einsum('bhqd,bhkd->bhqk', q[:, :, s:e], k[:, :, :e]).astype(jnp.float32) * scale
        logits = logits + (c[:, :, s:e, None] - c[:, :, None, :e])
        causal = jnp.arange(s, e)[:, None] >= jnp.arange(e)[None, :]
        logits = jnp.where(causal, logits, -jnp.inf)
        p = jax.nn.softmax(logits, axis=-1).astype(v.dtype)
        outs.append(jnp.einsum('bhqk,bhkd->bhqd', p, v[:, :, :e]))
    return jnp.concatenate(outs, axis=2)

def fox_layer(h, w_q, q_norm_g, w_o, k_sh, v_sh, c_sh):
    B, T, D = h.shape
    q = rmsnorm(to_heads(h @ w_q), q_norm_g)
    q = jnp.transpose(q, (0, 2, 1, 3))
    o = forgetting_attention(q, k_sh, v_sh, c_sh)
    o = jnp.transpose(o, (0, 2, 1, 3)).reshape(B, T, D)
    return o @ w_o

def sq_relu_mlp(h, w_in, w_out):
    return jnp.square(jax.nn.relu(h @ w_in)) @ w_out

def first_inputs(seed: int = 0) -> dict:
    key = jax.random.key(seed)
    ks = iter(jax.random.split(key, 40))
    D, H, N, F = D_MODEL, N_HEADS, HEAD_DIM, D_FF
    nA, nB = N_A_LAYERS, N_B_LAYERS
    nrm = lambda shape, s: s * jax.random.normal(next(ks), shape, jnp.float32)
    gain = lambda shape: 1.0 + nrm(shape, 0.05)
    decay_base = jnp.linspace(-6.5, -1.5, D, dtype=jnp.float32)
    inp = {}
    inp["x"] = jax.random.normal(next(ks), (BATCH, SEQ, D), jnp.float32)
    inp["rwkv_norm_g"] = gain((nA, D))
    inp["rwkv_mu"] = jax.random.uniform(next(ks), (nA, N_SHIFT_MIX, D), jnp.float32)
    inp["rwkv_w_rkv"] = nrm((nA, 3, D, D), D ** -0.5)
    inp["rwkv_w0"] = decay_base[None] + nrm((nA, D), 0.1)
    inp["rwkv_w1"] = nrm((nA, D, DECAY_LORA), D ** -0.5)
    inp["rwkv_w2"] = nrm((nA, DECAY_LORA, D), 0.1 * DECAY_LORA ** -0.5)
    inp["rwkv_a0"] = nrm((nA, D), 0.1)
    inp["rwkv_a1"] = nrm((nA, D, AAA_LORA), D ** -0.5)
    inp["rwkv_a2"] = nrm((nA, AAA_LORA, D), 0.1 * AAA_LORA ** -0.5)
    inp["rwkv_g1"] = nrm((nA, D, GATE_LORA), D ** -0.5)
    inp["rwkv_g2"] = nrm((nA, GATE_LORA, D), GATE_LORA ** -0.5)
    inp["rwkv_k_k"] = 0.85 + nrm((nA, D), 0.05)
    inp["rwkv_k_a"] = 1.0 + nrm((nA, D), 0.05)
    inp["rwkv_r_k"] = nrm((nA, H, N), 0.1)
    inp["rwkv_lnx_w"] = gain((nA, D))
    inp["rwkv_lnx_b"] = nrm((nA, D), 0.02)
    inp["rwkv_w_o"] = nrm((nA, D, D), 0.5 * D ** -0.5)
    inp["kv_norm_g"] = gain((D,))
    inp["kv_w"] = nrm((D, 2 * D + H), D ** -0.5)
    inp["kv_f_bias"] = jax.random.uniform(next(ks), (H,), jnp.float32, 0.5, 3.0)
    inp["k_norm_g"] = gain((H, N))
    inp["attn_norm_g"] = gain((nB, D))
    inp["attn_w_q"] = nrm((nB, D, D), D ** -0.5)
    inp["q_norm_g"] = gain((nB, H, N))
    inp["attn_w_o"] = nrm((nB, D, D), 0.5 * D ** -0.5)
    inp["mlp_norm_g"] = gain((DEPTH, D))
    inp["mlp_w_in"] = nrm((DEPTH, D, F), D ** -0.5)
    inp["mlp_w_out"] = nrm((DEPTH, F, D), 0.5 * F ** -0.5)
    return inp

def first_block(x, rwkv_norm_g, rwkv_mu, rwkv_w_rkv, rwkv_w0, rwkv_w1, rwkv_w2,
              rwkv_a0, rwkv_a1, rwkv_a2, rwkv_g1, rwkv_g2, rwkv_k_k, rwkv_k_a,
              rwkv_r_k, rwkv_lnx_w, rwkv_lnx_b, rwkv_w_o,
              kv_norm_g, kv_w, kv_f_bias, k_norm_g,
              attn_norm_g, attn_w_q, q_norm_g, attn_w_o,
              mlp_norm_g, mlp_w_in, mlp_w_out):
    k_sh = v_sh = c_sh = None
    for layer in range(DEPTH):
        if layer < N_A_LAYERS:
            i = layer
            h = rmsnorm(x, rwkv_norm_g[i])
            x = x + rwkv7_time_mix(h, rwkv_mu[i], rwkv_w_rkv[i], rwkv_w0[i], rwkv_w1[i],
                                   rwkv_w2[i], rwkv_a0[i], rwkv_a1[i], rwkv_a2[i],
                                   rwkv_g1[i], rwkv_g2[i], rwkv_k_k[i], rwkv_k_a[i],
                                   rwkv_r_k[i], rwkv_lnx_w[i], rwkv_lnx_b[i], rwkv_w_o[i])
        else:
            j = layer - N_A_LAYERS
            h = rmsnorm(x, attn_norm_g[j])
            x = x + fox_layer(h, attn_w_q[j], q_norm_g[j], attn_w_o[j], k_sh, v_sh, c_sh)
        x = x + sq_relu_mlp(rmsnorm(x, mlp_norm_g[layer]), mlp_w_in[layer], mlp_w_out[layer])
        if layer == N_A_LAYERS - 1:
            k_sh, v_sh, c_sh = shared_kv(x, kv_norm_g, kv_w, kv_f_bias, k_norm_g)
    return x


N_MIXERS = 2
NEG = -1e30
D_FF_2 = 4 * D_MODEL
RET_HEADS = 4
RET_DK = D_MODEL // RET_HEADS
RET_DV = 2 * RET_DK
RET_CHUNK = 128
RET_THETA = 10000.0
RET_IN = 2 * RET_HEADS * RET_DK + 2 * RET_HEADS * RET_DV
MOBA_HEADS = 8
MOBA_DH = D_MODEL // MOBA_HEADS
MOBA_BLOCK = 256
MOBA_TOPK = 3
MOBA_QCHUNK = 8
ROPE_THETA = 500000.0
ROPE_DIM = MOBA_DH // 4
MOBA_IN = 3 * MOBA_HEADS * MOBA_DH


def rms_norm(x, g):
    xf = x.astype(jnp.float32)
    y = xf * lax.rsqrt(jnp.mean(xf * xf, axis=-1, keepdims=True) + NORM_EPS)
    return (y * g.astype(jnp.float32)).astype(x.dtype)

def sq_relu_mlp_2(x, w_up, w_down):
    h = jax.nn.relu(x @ w_up)
    return (h * h) @ w_down

def retnet_rotary(x, pos):
    d = x.shape[-1]
    freq = 1.0 / (RET_THETA ** jnp.linspace(0.0, 1.0, d // 2, dtype=jnp.float32))
    ang = pos[:, None].astype(jnp.float32) * freq[None, :]
    cos, sin = jnp.cos(ang), jnp.sin(ang)
    x1 = x[..., 0::2].astype(jnp.float32)
    x2 = x[..., 1::2].astype(jnp.float32)
    y = jnp.stack([x1 * cos - x2 * sin, x1 * sin + x2 * cos], axis=-1)
    return y.reshape(x.shape).astype(x.dtype)

def partial_rope(x, pos):
    half = ROPE_DIM // 2
    inv = ROPE_THETA ** (-jnp.arange(0, ROPE_DIM, 2, dtype=jnp.float32) / ROPE_DIM)
    ang = pos[:, None].astype(jnp.float32) * inv[None, :]
    cos, sin = jnp.cos(ang), jnp.sin(ang)
    x1 = x[..., :half].astype(jnp.float32)
    x2 = x[..., half:ROPE_DIM].astype(jnp.float32)
    rot = jnp.concatenate([x1 * cos - x2 * sin, x2 * cos + x1 * sin], axis=-1)
    return jnp.concatenate([rot.astype(x.dtype), x[..., ROPE_DIM:]], axis=-1)

def retention(h, w_in, w_out):
    B, S, _ = h.shape
    H, DK, DV, L = RET_HEADS, RET_DK, RET_DV, RET_CHUNK
    C = S // L
    q, k, v, g = jnp.split(h @ w_in, [H * DK, 2 * H * DK, 2 * H * DK + H * DV], axis=-1)
    q = q.reshape(B, S, H, DK).transpose(0, 2, 1, 3)
    k = k.reshape(B, S, H, DK).transpose(0, 2, 1, 3)
    v = v.reshape(B, S, H, DV).transpose(0, 2, 1, 3)
    pos = jnp.arange(S)
    q = retnet_rotary(q, pos)
    k = retnet_rotary(k, pos) * (DK ** -0.5)

    log_gamma = jnp.log(1.0 - 2.0 ** (-5.0 - jnp.arange(H, dtype=jnp.float32)))
    idx = jnp.arange(L, dtype=jnp.float32)
    diff = idx[:, None] - idx[None, :]
    d_intra = jnp.where(diff >= 0, jnp.exp(log_gamma[:, None, None] * jnp.maximum(diff, 0.0)), 0.0)
    q_decay = jnp.exp(log_gamma[:, None] * (idx + 1.0))[None, :, :, None]
    k_decay = jnp.exp(log_gamma[:, None] * (L - 1.0 - idx))[None, :, :, None]
    chunk_decay = jnp.exp(log_gamma * L)[None, :, None, None]

    qc = q.reshape(B, H, C, L, DK)
    kc = k.reshape(B, H, C, L, DK)
    vc = v.reshape(B, H, C, L, DV)
    scores = jnp.einsum('bhcid,bhcjd->bhcij', qc, kc).astype(jnp.float32) * d_intra[None, :, None]
    o_intra = jnp.einsum('bhcij,bhcje->bhcie', scores, vc)

    def step(state, inp):
        q_c, k_c, v_c = inp
        cross = jnp.einsum('bhid,bhde->bhie', q_c, state) * q_decay
        state = state * chunk_decay + jnp.einsum('bhjd,bhje->bhde', k_c * k_decay, v_c)
        return state, cross

    init = jnp.zeros((B, H, DK, DV), jnp.float32)
    xs = (qc.transpose(2, 0, 1, 3, 4), kc.transpose(2, 0, 1, 3, 4), vc.transpose(2, 0, 1, 3, 4))
    _, o_cross = lax.scan(step, init, xs)
    o = (o_intra + o_cross.transpose(1, 2, 0, 3, 4)).reshape(B, H, S, DV)
    o = o * lax.rsqrt(jnp.mean(o * o, axis=-1, keepdims=True) + NORM_EPS)
    o = o.transpose(0, 2, 1, 3).reshape(B, S, H * DV)
    o = o * jax.nn.silu(g.astype(jnp.float32))
    return o.astype(h.dtype) @ w_out

def moba_attention(h, w_in, w_out):
    B, S, _ = h.shape
    H, Dh, BS, QC = MOBA_HEADS, MOBA_DH, MOBA_BLOCK, MOBA_QCHUNK
    nb = -(-S // BS)
    Sp = nb * BS
    K_SEL = min(MOBA_TOPK, nb)
    q, k, v = jnp.split(h @ w_in, 3, axis=-1)
    q = q.reshape(B, S, H, Dh).transpose(0, 2, 1, 3)
    k = k.reshape(B, S, H, Dh).transpose(0, 2, 1, 3)
    v = v.reshape(B, S, H, Dh).transpose(0, 2, 1, 3)
    pos = jnp.arange(S)
    q = partial_rope(q, pos) * (Dh ** -0.5)
    k = partial_rope(k, pos)
    pad = ((0, 0), (0, 0), (0, Sp - S), (0, 0))
    q, k, v = jnp.pad(q, pad), jnp.pad(k, pad), jnp.pad(v, pad)
    qb = q.reshape(B, H, nb, BS, Dh)
    kb = k.reshape(B, H, nb, BS, Dh)
    vb = v.reshape(B, H, nb, BS, Dh)

    causal = jnp.tril(jnp.ones((BS, BS), dtype=bool))
    s_own = jnp.einsum('bhnid,bhnjd->bhnij', qb, kb).astype(jnp.float32)
    s_own = jnp.where(causal, s_own, NEG)
    m_own = jnp.max(s_own, axis=-1)
    p_own = jnp.exp(s_own - m_own[..., None])
    l_own = jnp.sum(p_own, axis=-1)
    o_own = jnp.einsum('bhnij,bhnjd->bhnid', p_own, vb)
    m_own, l_own = m_own.reshape(B, H, Sp), l_own.reshape(B, H, Sp)
    o_own = o_own.reshape(B, H, Sp, Dh)

    k_mean = jnp.mean(kb.astype(jnp.float32), axis=3)
    gate = jnp.einsum('bhsd,bhnd->bhsn', q.astype(jnp.float32), k_mean)
    q_blk = jnp.arange(Sp) // BS
    past = jnp.arange(nb)[None, :] < q_blk[:, None]
    gate = jnp.where(past, gate, NEG)
    _, sel = lax.top_k(gate, K_SEL)
    valid = sel < q_blk[:, None]

    nq = Sp // QC
    q_ch = q.reshape(B, H, nq, QC, Dh).transpose(2, 0, 1, 3, 4)
    sel_ch = sel.reshape(B, H, nq, QC, K_SEL).transpose(2, 0, 1, 3, 4)
    val_ch = valid.reshape(B, H, nq, QC, K_SEL).transpose(2, 0, 1, 3, 4)
    bi = jnp.arange(B)[:, None, None, None]
    hi = jnp.arange(H)[None, :, None, None]

    def attend_selected(args):
        qc, sc, vc = args
        k_sel = kb[bi, hi, sc]
        v_sel = vb[bi, hi, sc]
        s = jnp.einsum('bhqd,bhqkjd->bhqkj', qc, k_sel).astype(jnp.float32)
        s = jnp.where(vc[..., None], s, NEG)
        m = jnp.max(s, axis=(3, 4))
        p = jnp.exp(s - m[..., None, None])
        l = jnp.sum(p, axis=(3, 4))
        o = jnp.einsum('bhqkj,bhqkjd->bhqd', p, v_sel)
        return m, l, o

    m_sel, l_sel, o_sel = lax.map(attend_selected, (q_ch, sel_ch, val_ch))
    m_sel = m_sel.transpose(1, 2, 0, 3).reshape(B, H, Sp)
    l_sel = l_sel.transpose(1, 2, 0, 3).reshape(B, H, Sp)
    o_sel = o_sel.transpose(1, 2, 0, 3, 4).reshape(B, H, Sp, Dh)

    m = jnp.maximum(m_own, m_sel)
    a = jnp.exp(m_own - m)
    b = jnp.exp(m_sel - m)
    o = (o_own * a[..., None] + o_sel * b[..., None]) / (l_own * a + l_sel * b)[..., None]
    o = o[:, :, :S].transpose(0, 2, 1, 3).reshape(B, S, H * Dh)
    return o.astype(h.dtype) @ w_out

def second_inputs(seed: int = 0) -> dict:
    key = jax.random.key(seed)
    ks = jax.random.split(key, 32)
    f32 = jnp.float32

    def w(k, shape):
        return jax.random.normal(k, shape, f32) * (shape[0] ** -0.5)

    def gain(k):
        return 1.0 + 0.05 * jax.random.normal(k, (D_MODEL,), f32)

    return {
        "x": jax.random.normal(ks[0], (BATCH, SEQ, D_MODEL), f32),
        "ln_mix_pre_0": gain(ks[1]),
        "ln_mix_post_0": gain(ks[2]),
        "w_in_0": w(ks[3], (D_MODEL, RET_IN)),
        "w_out_0": w(ks[4], (RET_HEADS * RET_DV, D_MODEL)),
        "ln_mlp_pre_0": gain(ks[5]),
        "ln_mlp_post_0": gain(ks[6]),
        "w_up_0": w(ks[7], (D_MODEL, D_FF_2)),
        "w_down_0": w(ks[8], (D_FF_2, D_MODEL)),
        "ln_mix_pre_1": gain(ks[9]),
        "ln_mix_post_1": gain(ks[10]),
        "w_in_1": w(ks[11], (D_MODEL, MOBA_IN)),
        "w_out_1": w(ks[12], (MOBA_HEADS * MOBA_DH, D_MODEL)),
        "ln_mlp_pre_1": gain(ks[13]),
        "ln_mlp_post_1": gain(ks[14]),
        "w_up_1": w(ks[15], (D_MODEL, D_FF_2)),
        "w_down_1": w(ks[16], (D_FF_2, D_MODEL)),
    }

def second_block(x, ln_mix_pre_0, ln_mix_post_0, w_in_0, w_out_0, ln_mlp_pre_0, ln_mlp_post_0, w_up_0, w_down_0,
              ln_mix_pre_1, ln_mix_post_1, w_in_1, w_out_1, ln_mlp_pre_1, ln_mlp_post_1, w_up_1, w_down_1):
    mixers = (retention, moba_attention)
    layers = (
        (ln_mix_pre_0, ln_mix_post_0, w_in_0, w_out_0, ln_mlp_pre_0, ln_mlp_post_0, w_up_0, w_down_0),
        (ln_mix_pre_1, ln_mix_post_1, w_in_1, w_out_1, ln_mlp_pre_1, ln_mlp_post_1, w_up_1, w_down_1),
    )
    h = x
    for i in range(DEPTH):
        pre, post, w_in, w_out, mpre, mpost, w_up, w_down = layers[i]
        h = h + rms_norm(mixers[i % N_MIXERS](rms_norm(h, pre), w_in, w_out), post)
        h = h + rms_norm(sq_relu_mlp_2(rms_norm(h, mpre), w_up, w_down), mpost)
    return h


def setup_inputs(seed=0):
    out = dict(first_inputs(seed))
    for name, value in second_inputs(seed + 1).items():
        if name != "x":
            out[name + "_2"] = value
    return out


def reference(
    x, rwkv_norm_g, rwkv_mu, rwkv_w_rkv, rwkv_w0, rwkv_w1, rwkv_w2, rwkv_a0, rwkv_a1, rwkv_a2,
    rwkv_g1, rwkv_g2, rwkv_k_k, rwkv_k_a, rwkv_r_k, rwkv_lnx_w, rwkv_lnx_b, rwkv_w_o, kv_norm_g,
    kv_w, kv_f_bias, k_norm_g, attn_norm_g, attn_w_q, q_norm_g, attn_w_o, mlp_norm_g, mlp_w_in,
    mlp_w_out, ln_mix_pre_0_2, ln_mix_post_0_2, w_in_0_2, w_out_0_2, ln_mlp_pre_0_2,
    ln_mlp_post_0_2, w_up_0_2, w_down_0_2, ln_mix_pre_1_2, ln_mix_post_1_2, w_in_1_2, w_out_1_2,
    ln_mlp_pre_1_2, ln_mlp_post_1_2, w_up_1_2, w_down_1_2,
):
    x = first_block(
        x, rwkv_norm_g, rwkv_mu, rwkv_w_rkv, rwkv_w0, rwkv_w1, rwkv_w2, rwkv_a0, rwkv_a1,
        rwkv_a2, rwkv_g1, rwkv_g2, rwkv_k_k, rwkv_k_a, rwkv_r_k, rwkv_lnx_w, rwkv_lnx_b,
        rwkv_w_o, kv_norm_g, kv_w, kv_f_bias, k_norm_g, attn_norm_g, attn_w_q, q_norm_g,
        attn_w_o, mlp_norm_g, mlp_w_in, mlp_w_out,
    )
    return second_block(
        x, ln_mix_pre_0_2, ln_mix_post_0_2, w_in_0_2, w_out_0_2, ln_mlp_pre_0_2,
        ln_mlp_post_0_2, w_up_0_2, w_down_0_2, ln_mix_pre_1_2, ln_mix_post_1_2, w_in_1_2,
        w_out_1_2, ln_mlp_pre_1_2, ln_mlp_post_1_2, w_up_1_2, w_down_1_2,
    )


_drawn_inputs = setup_inputs


def setup_inputs(seed=0):
    import zlib

    import numpy as np

    out = dict(_drawn_inputs(seed))
    spreads = {}
    factors = {'rwkv_w1': 8.0,
     'rwkv_w2': 8.0,
     'rwkv_a0': 2.977,
     'rwkv_a1': 3.052,
     'rwkv_a2': 3.171,
     'rwkv_k_k': 4.025,
     'rwkv_lnx_w': 2.787,
     'rwkv_lnx_b': 5.155,
     'kv_norm_g': 2.99,
     'k_norm_g': 5.84,
     'attn_norm_g': 5.918,
     'q_norm_g': 6.089,
     'ln_mlp_post_1_2': 2.787,
     'ln_mix_post_1_2': 2.904}
    for name, (base, spread) in spreads.items():
        noise = np.random.default_rng([zlib.crc32(name.encode()), seed]).standard_normal(out[name].shape)
        drawn = base * np.exp(spread * noise) if base else spread * noise
        out[name] = __import__('jax').numpy.asarray(drawn.astype(out[name].dtype))
    for name, factor in factors.items():
        out[name] = (out[name] * factor).astype(out[name].dtype)
    return out
```

```python
from contextlib import ExitStack

import numpy as np

import concourse.bass as bass
from concourse import mybir

F32 = mybir.dt.float32
F32R = mybir.dt.float32r
ACT = mybir.ActivationFunctionType
ALU = mybir.AluOpType
AXX = mybir.AxisListType.X

P = 128
D = 1024
T = 256
FF = 4096
MT = T // P
KT = D // P
RAW_RING, SPLIT_RING = 4, 2
UK, UN = 4, 512
NH = 16
HD = 64
LORA, GATE = 64, 160
RET_H, RET_DV = 4, 512
MOBA_H, MOBA_D = 8, 128
ROPE = 32
NORM_EPS, GN_EPS = 1e-6, 64e-5
NEG = -1e30

GEMMS = [("r", 8, 2), ("k", 8, 2), ("v", 8, 2), ("rwo", 8, 2), ("mlp0", 0, 0),
         ("fk", 8, 2), ("fv", 8, 2), ("fq", 8, 2), ("fo", 8, 2), ("mlp1", 0, 0),
         ("rq", 8, 2), ("rk", 8, 2), ("rv", 8, 4), ("rg", 8, 4), ("reo", 16, 2), ("mlp2", 0, 0),
         ("mq", 8, 2), ("mk", 8, 2), ("mv", 8, 2), ("mo", 8, 2), ("mlp3", 0, 0)]
READER = {"r": "act", "k": "act", "v": "act", "rwo": "sum", "fk": "act", "fv": "act", "fq": "act",
          "fo": "sum", "rq": "dve", "rk": "dve", "rv": "act", "rg": "act", "reo": "sum",
          "mq": "act", "mk": "act", "mv": "act", "mo": "sum"}
MLP_STEPS = FF // UN
MLP_UNITS = 4 * MLP_STEPS


def plan():
    u0, chunk0, u, g = {}, {}, 0, 0
    readers = []
    for name, kt, nn in GEMMS:
        u0[name], chunk0[name] = u, g
        if kt == 0:
            u += MLP_UNITS
            continue
        readers += [READER[name]] * nn
        u += nn * kt // UK
        g += nn
    read_count, counts = [], {"act": 0, "dve": 0, "sum": 0}
    for r in readers:
        counts[r] += 2
        read_count.append((r, counts[r]))
    return u0, chunk0, read_count, u


U0, CHUNK0, READ_COUNT, UNITS = plan()

VECS = ["rwkv_norm_g", "mu0", "mu1", "mu2", "mu3", "mu4", "mu5", "w0", "a0", "k_k", "k_a", "r_k",
        "kv_norm_g", "k_norm_g", "attn_norm_g", "q_norm_g", "mlp_norm_g0", "mlp_norm_g1",
        "ln_mix_pre_0", "ln_mlp_pre_0", "ln_mix_pre_1", "ln_mlp_pre_1"]
ROWS = ["lnx_w", "lnx_b", "ln_mix_post_0", "ln_mlp_post_0", "ln_mix_post_1", "ln_mlp_post_1"]

TURNS = [("rwkv", "rwkv_norm_g", 8, True, 0), ("rwo", None, 8, False, 0), ("mlp0", "mlp_norm_g0", 8, True, 0),
         ("kv", "kv_norm_g", 8, True, 0), ("attn", "attn_norm_g", 8, False, 1), ("fo", None, 8, False, 0),
         ("mlp1", "mlp_norm_g1", 8, True, 0), ("ret", "ln_mix_pre_0", 8, True, 0), ("reo", None, 16, False, 0),
         ("mlp2", "ln_mlp_pre_0", 8, True, 0), ("moba", "ln_mix_pre_1", 8, True, 0), ("mo", None, 8, False, 0),
         ("mlp3", "ln_mlp_pre_1", 8, True, 0)]
TI = {t[0]: i for i, t in enumerate(TURNS)}


def turn_counts():
    turned, split, normed, b, s, n = [], [], [], 0, 0, 0
    for name, _, kt, norm, _ in TURNS:
        turned.append(b)
        split.append(s)
        normed.append(n)
        b += kt // 2
        s += kt // 2 if name != "rwkv" else 0
        n += 1 if norm else 0
    return turned, split, normed


TURNED0, SPLIT0, NORM0 = turn_counts()
RESIDUALS = {"rwkv": 0, "mlp0": 4, "kv": 8, "mlp1": 12, "ret": 16, "mlp2": 20, "moba": 24, "mlp3": 28}


def constants():
    f = np.float32
    i = np.arange(P)
    c = {"ident": np.eye(P, dtype=f)}
    strict = (i[:, None] < i[None, :]).astype(f)
    incl = (i[:, None] <= i[None, :]).astype(f)
    c["pair_masks"] = np.concatenate([strict, incl, strict, incl], 1)
    lm = []
    for m in (1, 2, 4, 8, 16, 32, 64):
        b = i // m
        lm.append(((b[:, None] % 2 == 1) & (b[None, :] == b[:, None] - 1)).astype(f))
    c["first_mask"] = -lm[0].T
    c["level_masks"] = np.concatenate(lm[1:], 1)
    c["head_window"] = np.zeros((P, 142), f)
    c["head_window"][i, 14 + i // HD] = 1.0
    c["head_spread"] = (i[:, None] == np.arange(D)[None, :] // HD).astype(f)
    c["head_blocks"] = (i[:, None] // HD == i[None, :] // HD).astype(f)
    c["head_halves"] = np.stack([(i // HD == 0), (i // HD == 1)], 1).astype(f)
    causal = np.where(i[:, None] >= i[None, :], 0.0, NEG).astype(f)
    c["causal"] = np.concatenate([causal, np.zeros((P, P), f), causal], 1)
    h = np.arange(RET_H, dtype=f)
    lg = np.log(1.0 - 2.0 ** (-5.0 - h.astype(np.float64)))
    t = np.arange(T)
    diff = t[None, None, :] - i[:, None, None]
    dec = np.where(diff >= 0, np.exp(lg[None, :, None] * np.maximum(diff, 0)) / 16.0, 0.0)
    c["ret_decay"] = dec.reshape(P, RET_H * T).astype(f)
    freq = (1.0 / (f(10000.0) ** np.linspace(0.0, 1.0, P, dtype=f))).astype(f)
    ang = (np.arange(T, dtype=f)[None, :] * freq[:, None]).astype(f).astype(np.float64)
    c["ret_cos"], c["ret_sin"] = np.cos(ang).astype(f), np.sin(ang).astype(f)
    inv = (f(500000.0) ** (-np.arange(0, ROPE, 2, dtype=f) / f(ROPE))).astype(f)
    a2 = (np.arange(T, dtype=f)[None, :] * inv[:, None]).astype(f).astype(np.float64)
    c["rope_cos"] = np.concatenate([np.cos(a2), np.cos(a2)], 0).astype(f)
    c["rope_sin"] = np.concatenate([-np.sin(a2), np.sin(a2)], 0).astype(f)
    perm = np.zeros((P, ROPE), f)
    j = np.arange(ROPE)
    perm[(j + ROPE // 2) % ROPE, j] = 1.0
    c["rope_swap"] = perm
    return c


CONST_KEEP = ["ident", "pair_masks", "first_mask", "level_masks", "head_window", "head_blocks", "head_halves", "causal"]
CONST_RET = ["ret_decay", "ret_cos", "ret_sin"]
CONST_ROPE = ["rope_cos", "rope_sin", "rope_swap"]


def build(nc, a, out):
    with ExitStack() as ctx:
        def sb(name, shape, dt=F32):
            return ctx.enter_context(nc.sbuf_tensor(name, shape, dt))

        def sem(name):
            return ctx.enter_context(nc.semaphore(name))

        X = sb("X", [P, MT, D])
        raw = sb("raw", [P, RAW_RING, UK, UN])
        whi = sb("whi", [P, SPLIT_RING, UK, UN], F32R)
        wlo = sb("wlo", [P, SPLIT_RING, UK, UN], F32R)
        XH = sb("XH", [P, 2 * KT, T], F32R)
        XL = sb("XL", [P, 2 * KT, T], F32R)
        vecs = sb("vecs", [P, len(VECS), KT])
        keep = {n: sb(f"c_{n}", list(a[n].shape)) for n in CONST_KEEP if n != "causal"}
        ident = keep["ident"]
        small = sb("small", [P, 128])
        att_nmax = sb("att_nmax", [P, 4, MT])
        att_sum = sb("att_sum", [P, NH, MT])
        ret_sums = sb("ret_sums", [P, RET_H * MT])
        NA = 24320
        arena = sb("arena", [P, NA])
        psum = [ctx.enter_context(nc.psum_tensor(f"bank{i}", [P, 512], F32)) for i in range(8)]

        def at(off, *dims):
            n = int(np.prod(dims))
            assert off + n <= NA, (off, dims)
            v = arena[:, off:off + n]
            names = "abcd"[:len(dims)]
            if len(dims) == 1:
                return v
            return v.rearrange(f"p ({' '.join(names)}) -> p {' '.join(names)}", **dict(zip(names, dims)))

        def gain(name, k):
            i = VECS.index(name)
            return vecs[:, i, k:k + 1]

        def bank_kt(b):
            return psum[b][:, :].rearrange("p (a t) -> p a t", a=2)

        norm_ss, norm_ms, norm_rstd = small[:, 0:2], small[:, 2:4], small[:, 4:6]
        norm_sd = small[:, 6:8]
        post_ss = small[:, 8:12].rearrange("p (m n) -> p m n", m=2)
        post_ms, post_sd, post_rstd = small[:, 12:14], small[:, 14:16], small[:, 16:18]
        bonus = small[:, 32:64]
        state_scale = small[:, 64:72]
        gn_mean, gn_var = small[:, 72:88], small[:, 88:104]

        XN, JUNK = at(4096, MT, D), at(6144, D)
        RELU = at(8240, MT, UN)
        hT, xxT = at(0, KT, T), at(2048, KT, T)
        XM = [at(4096, KT, T), at(6144, KT, T)]
        w1s, a1s, g1s = at(8192, KT, LORA), at(8704, KT, LORA), at(9216, KT, GATE)
        w2s, a2s, g2a, g2b = at(10496, D), at(11520, D), at(12544, D), at(13568, D)
        rT, kT, V, G = at(14592, KT, T), at(16640, KT, T), at(18688, MT, D), at(20736, MT, D)
        tw, ta, sga, sgb = at(22784, T), at(23040, T), at(23296, T), at(23552, T)
        sT, aT, lwT = at(0, KT, T), at(2080, KT, T), at(4128, KT, T)
        LW = P + 1
        Lx = at(6176, KT * 2, LW)
        E1, E2 = at(8240, KT * 2, LW), at(0, KT * 2, LW)
        kkT, sqT, rn = at(10496, KT, T), at(12544, KT, T), at(22784, T)
        AR = at(4128, KT * 2, 2, P)
        BE = aT
        Y = at(0, MT, D)
        M = [at(8240 + 2048 * l, 4, 512) for l in range(2)]
        TI_ = [at(12336 + 512 * l, 4, P) for l in range(2)]
        TT_ = [at(13360 + 512 * l, 4, P) for l in range(2)]
        PM = [at(14384 + 512 * l, 4, P) for l in range(2)]
        PAD = at(15408, 2, 4, P)
        SA = [at(22784 + 256 * l, 256) for l in range(2)]
        S0 = at(23296, KT, P)
        YC, YQ, LNROW = at(8240, D), at(10288, D), at(12336, 2, D)
        ones, mids = at(24064, P), small[:, 104:120].unsqueeze(2)
        SPREAD = at(23040, KT, P)
        fK, fKP, fV, fQ = at(0, KT, T), at(8240, NH, T), at(12336, MT, D), at(14384, KT, T)
        fSQ, negc, frn = at(16432, KT, T), at(18480, T), at(18736, T)
        wf, fz, fl = at(18992, KT, NH), at(19120, T), at(19376, T)
        fc, fbias = at(19632, T), at(7600, 1)
        fL, fE, fPT = at(19888, 2, 384), at(20656, 2, 384), at(21424, 2, 384)
        fO, fCAUSAL = at(22192, MT, D), at(7200, 384)
        rDEC, rCOS, rSIN = at(0, RET_H, T), at(1024, T), at(1280, T)
        rQ, rK = at(1536, RET_H, 2, T), at(7168, RET_H, 2, T)
        rV, rG = at(9216, MT, 2 * D), at(13312, MT, 2 * D)
        rA, rB = [at(17408 + 512 * i, 2, T) for i in range(2)], [at(18432 + 512 * i, 2, T) for i in range(2)]
        rPT = at(19456, 2, 384)
        POST = at(20224, 2, D)
        PTMP = at(22272, 2, UN)
        mQ, mCOS, mSIN, mSWAP, mCAUSAL = at(0, KT, T), at(2048, T), at(2304, T), at(2560, ROPE), at(2592, 384)
        mTMP, mTMP2 = at(2976, 2, T), at(3488, 2, T)
        mK, mV = at(7168, KT, T), at(9216, MT, D)
        mL, mE, mPT = at(11264, 2, 384), at(12032, 2, 384), at(12800, 2, 384)
        mO = at(13568, MT, D)

        raw_landed = [sem(f"raw_landed{i}") for i in range(RAW_RING)]
        hi_done, lo_done, unit_used = sem("hi_done"), sem("lo_done"), sem("unit_used")
        acc_read = {"act": sem("acc_read_act"), "dve": sem("acc_read_dve")}
        spread_in = sem("spread_in")
        x_in, ident_in, const_in, vecs_in, lora_in = sem("x_in"), sem("ident_in"), sem("const_in"), sem("vecs_in"), sem("lora_in")
        lnrow_in, fox_in, ret_in, moba_in = sem("lnrow_in"), sem("fox_in"), sem("ret_in"), sem("moba_in")
        post_in, out_done = sem("post_in"), sem("out_done")
        ss_done, ms_done, sd_done, rstd_done, xn_ready = (sem(n) for n in (
            "ss_done", "ms_done", "sd_done", "rstd_done", "xn_ready"))
        turned, turned_hi, turned_lo, hT_ready = sem("turned"), sem("turned_hi"), sem("turned_lo"), sem("hT_ready")
        residual = sem("residual")
        pss_done, pms_done, psd_done, prstd_done, ptmp_done = (sem(n) for n in (
            "pss_done", "pms_done", "psd_done", "prstd_done", "ptmp_done"))
        relu_done, square_done, h_turned, h_hi, h_lo = (sem(n) for n in (
            "relu_done", "square_done", "h_turned", "h_hi", "h_lo"))
        dve_step, act_step, pool_step = sem("dve_step"), sem("act_step"), sem("pool_step")
        mixed, mix_hi, mix_lo, lora1, lora1_act, lora2, lora2_read = (sem(n) for n in (
            "mixed", "mix_hi", "mix_lo", "lora1", "lora1_act", "lora2", "lora2_read"))
        lw_ready, centred, exps_ready, sq_ready, sums_ready, sums_ms, sums_sd, rn_ready, rn_spread, spread_read = (
            sem(n) for n in ("lw_ready", "centred", "exps_ready", "sq_ready", "sums_ready", "sums_ms", "sums_sd",
                             "rn_ready", "rn_spread", "spread_read"))
        bonus_prod, bonus_sum, bonus_read, prepared, scale_ready = (sem(n) for n in (
            "bonus_prod", "bonus_sum", "bonus_read", "prepared", "scale_ready"))
        padded, pair_prod, pair_masked, first_ready, first_turned, inv_ready, half_prod, half_masked, step_prod, \
            rhs_prod, rhs_ready, sa_prod, sa_ready, y_prod, y_ready, keys_turned, keys_ready, state_prod, \
            state_ready = (sem(n) for n in (
                "padded", "pair_prod", "pair_masked", "first_ready", "first_turned", "inv_ready", "half_prod",
                "half_masked", "step_prod", "rhs_prod", "rhs_ready", "sa_prod", "sa_ready", "y_prod", "y_ready",
                "keys_turned", "keys_ready", "state_prod", "state_ready"))
        doubled = sem("doubled")
        y_centred, y_squared, gn_ms, gn_sd, y_done = (sem(n) for n in (
            "y_centred", "y_squared", "gn_ms", "gn_sd", "y_done"))
        f_prod, f_z, f_abs, f_ln, negc_ready, zeroed = (sem(n) for n in (
            "f_prod", "f_z", "f_abs", "f_ln", "negc_ready", "zeroed"))
        logits, masked, maxed, expd, e_turned, pt_ready, av_prod, att_recip, att_out = (sem(n) for n in (
            "logits", "masked", "maxed", "expd", "e_turned", "pt_ready", "av_prod", "att_recip", "att_out"))
        rope_swapped, rope_cos, roped = sem("rope_swapped"), sem("rope_cos"), sem("roped")
        rotated, scores, decayed, ret_prod, ret_ss, ret_ms, ret_sd, ret_out = (sem(n) for n in (
            "rotated", "scores", "decayed", "ret_prod", "ret_ss", "ret_ms", "ret_sd", "ret_out"))

        block = ctx.enter_context(nc.Block())

        def raw_full(u):
            return 16 * (u // RAW_RING + 1)

        @block.sync
        def _(sp):
            sent = [0]

            def load_unit(name, u, row):
                if u >= RAW_RING:
                    sp.wait_ge(lo_done, u - RAW_RING + 1)
                sp.dma_start(raw[:, u % RAW_RING].rearrange("p k n -> p (k n)"), a["w_" + name][row])\
                    .then_inc(raw_landed[u % RAW_RING], 16)

            sp.dma_start(X[:, :, :], a["x"]).then_inc(x_in, 16)
            sp.dma_start(vecs[:, :, :].rearrange("p v k -> p (v k)"), a["vecs"]).then_inc(vecs_in, 16)
            sp.dma_start(ident[:, :], a["ident"]).then_inc(ident_in, 16)
            load_unit("r", 0, 0)
            load_unit("r", 1, 1)
            for n, dst in (("w1", w1s), ("a1", a1s), ("g1", g1s)):
                sp.dma_start(dst.rearrange("p k n -> p (k n)"), a[n]).then_inc(lora_in, 16)
            for n, dst, k in (("w2", w2s, LORA), ("a2", a2s, LORA), ("g2a", g2a, P), ("g2b", g2b, GATE - P)):
                sp.dma_start(dst[0:k, :], a[n]).then_inc(lora_in, 16)
            for n in CONST_KEEP[1:-1]:
                sp.dma_start(keep[n][:, :], a[n]).then_inc(const_in, 16)
            for name, kt, nn in GEMMS:
                if kt:
                    for i in range(nn * kt // UK):
                        u = U0[name] + i
                        if u >= 2:
                            load_unit(name, u, i)
                    continue
                b = U0[name]
                for i in range(2):
                    load_unit(name, b + i, i)
                with sp.Fori(1, MLP_STEPS) as j:
                    for i in range(UK):
                        slot = (i - 2) % RAW_RING
                        sp.wait_ge(lo_done, j * 4 + (b - 2 + i - RAW_RING + 1))
                        sp.dma_start(raw[:, slot].rearrange("p k n -> p (k n)"),
                                     a["w_" + name][bass.ds(j * 4 + (i - 2), 1)].rearrange("u p n -> (u p) n"))\
                            .then_inc(raw_landed[slot], 16)
                for i in range(MLP_UNITS - 2, MLP_UNITS):
                    load_unit(name, b + i, i)
            for i in range(4):
                m, h = i % 2, i // 2
                sp.wait_ge(residual, 28 + i + 1)
                sp.dma_start(out[0, m * P:(m + 1) * P, h * UN:(h + 1) * UN], X[:, m, h * UN:(h + 1) * UN])\
                    .then_inc(out_done, 16)
            sp.wait_ge(out_done, 64)

        @block.scalar
        def _(act):
            done = [0]
            steps = [0]

            def hi_unit(u):
                act.wait_ge(raw_landed[u % RAW_RING], raw_full(u))
                if u >= SPLIT_RING:
                    act.wait_ge(unit_used, u - SPLIT_RING + 1)
                act.activation(whi[:, u % SPLIT_RING], raw[:, u % RAW_RING], ACT.Copy).then_inc(hi_done, 1)

            def hi_upto(n):
                while done[0] < min(n, UNITS):
                    hi_unit(done[0])
                    done[0] += 1

            def stats(n):
                for m in range(MT):
                    act.activation(JUNK, X[:, m], ACT.Square, accum_out=norm_ss[:, m:m + 1]).then_inc(ss_done, 1)
                    act.wait_ge(ss_done, MT * n + m + 1)
                act.wait_ge(ms_done, n + 1)
                act.activation(norm_sd, norm_ms, ACT.Sqrt).then_inc(sd_done, 1)

            def norm(name):
                n = NORM0[TI[name]]
                if RESIDUALS[name]:
                    act.wait_ge(residual, RESIDUALS[name])
                else:
                    act.wait_ge(x_in, 16)
                stats(n)

            def turn_hi(name):
                i = TI[name]
                _, g, kt, _, half = TURNS[i]
                for b in range(kt // 2):
                    act.wait_ge(turned, TURNED0[i] + b + 1)
                    src = bank_kt(4 + b % 4)
                    if g is None:
                        act.activation(XH[:, half * KT + 2 * b:half * KT + 2 * b + 2], src, ACT.Copy)\
                            .then_inc(turned_hi, 1)
                        continue
                    for j in range(2):
                        k = 2 * b + j
                        ins = act.activation(XH[:, half * KT + k], src[:, j], ACT.Copy, scale=gain(g, k))
                    ins.then_inc(turned_hi, 1)

            def read_chunk(name, n, put):
                g, kt = CHUNK0[name] + n, dict((q[0], q[1]) for q in GEMMS)[name]
                ue = U0[name] + (n + 1) * kt // UK
                hi_upto(ue + 1)
                act.wait_ge(unit_used, ue)
                for j in range(2):
                    put(n, j, psum[(g % 2) * 2 + j]).then_inc(acc_read["act"], 1)

            def by_feature(dst):
                return lambda n, j, b: act.activation(
                    dst[:, 4 * n + 2 * j:4 * n + 2 * j + 2], b[:, :].rearrange("p (a t) -> p a t", a=2), ACT.Copy)

            def by_token(dst, func=ACT.Copy):
                return lambda n, j, b: act.activation(dst[:, j, n * UN:(n + 1) * UN], b[:, :], func)

            def mlp(i):
                b, name = U0[f"mlp{i}"], f"mlp{i}"
                s0 = MLP_STEPS * i

                def relu(q):
                    for m in range(MT):
                        act.activation(RELU[:, m], psum[m][:, :], ACT.Relu).then_inc(relu_done, 1)

                def hidden_hi(q):
                    for k in range(2):
                        act.wait_ge(h_turned, 2 * q + k + 1)
                        act.activation(XH[:, KT + 2 * k:KT + 2 * k + 2], bank_kt(6 + k), ACT.Copy).then_inc(h_hi, 1)

                hi_upto(b + 2)
                act.wait_ge(unit_used, b + 2)
                relu(s0)
                with act.Fori(1, MLP_STEPS) as j:
                    for n in range(UK):
                        slot = (n - 2) % RAW_RING
                        act.wait_ge(raw_landed[slot], (j + (b // RAW_RING + (1 if n >= 2 else 0))) * 16)
                        act.wait_ge(unit_used, j * 4 + (b - 2 + n - SPLIT_RING + 1))
                        act.activation(whi[:, slot % SPLIT_RING], raw[:, slot], ACT.Copy).then_inc(hi_done, 1)
                        if n == 1:
                            hidden_hi(j + (s0 - 1))
                    act.wait_ge(unit_used, j * 4 + b)
                    relu(j + s0)
                done[0] = b + MLP_UNITS - 2
                hi_upto(b + MLP_UNITS)
                hidden_hi(s0 + MLP_STEPS - 1)

            def post_norm(i, ue, bank0):
                hi_upto(ue + 1)
                act.wait_ge(unit_used, ue)
                for m in range(MT):
                    for n in range(2):
                        act.activation(PJUNK, psum[bank0 + 2 * n + m][:, :], ACT.Square,
                                       accum_out=post_ss[:, m, n:n + 1]).then_inc(pss_done, 1)
                        act.wait_ge(pss_done, 4 * i + 2 * m + n + 1)
                act.wait_ge(pms_done, i + 1)
                act.activation(post_sd, post_ms, ACT.Sqrt).then_inc(psd_done, 1)

            PJUNK = JUNK[:, 0:UN]

            def head_squares(i, src):
                act.activation(sqT if i == 0 else fSQ, src, ACT.Square).then_inc(sq_ready, 1)

            def head_roots(i):
                act.wait_ge(sums_ms, i + 1)
                r = rn if i == 0 else frn
                act.activation(r, r, ACT.Sqrt).then_inc(sums_sd, 1)

            def attention(a0, heads, scale, L, E, PT):
                for h in range(heads + 1):
                    if h < heads:
                        act.wait_ge(maxed, a0 + h + 1)
                        if h >= 2:
                            act.wait_ge(e_turned, a0 + h - 1)
                        for m in range(MT):
                            c0, c1 = (0, P) if m == 0 else (P, 3 * P)
                            ins = act.activation(E[:, h % 2, c0:c1], L[:, h % 2, c0:c1], ACT.Exp,
                                                 bias=att_nmax[:, h % 4, m:m + 1],
                                                 accum_out=att_sum[:, h % 16, m:m + 1])
                        ins.then_inc(expd, 1)
                    if h >= 1:
                        g = h - 1
                        act.wait_ge(e_turned, a0 + g + 1)
                        if g >= 2:
                            act.wait_ge(av_prod, a0 + g - 1)
                        act.activation(PT[:, g % 2], psum[2 + g % 2][:, 0:384], ACT.Copy).then_inc(pt_ready, 1)

            act.wait_ge(vecs_in, 16)
            norm("rwkv")
            hi_upto(2)
            for b in range(4):
                act.wait_ge(turned, b + 1)
                for j in range(2):
                    k = 2 * b + j
                    ins = act.activation(hT[:, k], bank_kt(4 + b)[:, j], ACT.Copy, scale=gain("rwkv_norm_g", k))
                ins.then_inc(hT_ready, 1)

            def mix_to_hi(j, order, half):
                act.wait_ge(mixed, order + 1)
                if j == 2:
                    act.wait_ge(unit_used, U0["k"])
                act.activation(XH[:, half * KT:(half + 1) * KT], XM[order % 2], ACT.Copy).then_inc(mix_hi, 1)

            mix_to_hi(0, 0, 0)
            read_chunk("r", 0, by_feature(rT))
            mix_to_hi(1, 2, 1)
            read_chunk("r", 1, by_feature(rT))
            act.wait_ge(lora1, 1)
            act.activation(tw[0:LORA, :], psum[4][0:LORA, 0:T], ACT.Tanh).then_inc(lora1_act, 1)
            read_chunk("k", 0, by_feature(kT))
            mix_to_hi(2, 4, 0)
            read_chunk("k", 1, by_feature(kT))
            act.wait_ge(lora1, 2)
            act.activation(ta[0:LORA, :], psum[5][0:LORA, 0:T], ACT.Copy).then_inc(lora1_act, 1)
            read_chunk("v", 0, by_token(V))
            read_chunk("v", 1, by_token(V))
            act.wait_ge(lora1, 3)
            act.activation(sga, psum[6][:, 0:T], ACT.Sigmoid).then_inc(lora1_act, 1)
            act.activation(sgb[0:GATE - P, :], psum[7][0:GATE - P, 0:T], ACT.Sigmoid).then_inc(lora1_act, 1)
            for b in range(4):
                act.wait_ge(lora2, b + 1)
                act.activation(G[:, b // 2, (b % 2) * UN:(b % 2 + 1) * UN], psum[4 + b][:, :], ACT.Copy)\
                    .then_inc(lora2_read, 1)
            for q, (dst, bias) in enumerate(((sT, "w0"), (aT, "a0"))):
                for b in range(4):
                    act.wait_ge(lora2, 4 + 4 * q + b + 1)
                    for j in range(2):
                        ins = act.activation(dst[:, 2 * b + j], bank_kt(4 + b)[:, j], ACT.Sigmoid,
                                             bias=gain(bias, 2 * b + j))
                    ins.then_inc(lora2_read, 1)
                if q == 0:
                    act.wait_ge(lora2_read, 8)
                    act.activation(lwT, sT, ACT.Copy, scale=-float(np.exp(-0.5))).then_inc(lw_ready, 1)
            act.wait_ge(prepared, 1)
            head_squares(0, kkT)
            head_roots(0)
            act.wait_ge(centred, 1)
            act.activation(E1, Lx, ACT.Exp).then_inc(exps_ready, 1)
            act.activation(E2, Lx, ACT.Exp, scale=-1.0).then_inc(exps_ready, 1)
            act.activation(state_scale, state_scale, ACT.Exp).then_inc(scale_ready, 1)
            for r in range(4):
                c = r // 2
                for l in range(2):
                    gi = 2 * r + l
                    act.wait_ge(first_turned, gi + 1)
                    act.activation(TI_[l], psum[2 + l][:, :].rearrange("p (h s) -> p h s", h=4), ACT.Copy)\
                        .then_inc(inv_ready, 1)
                for l in range(2):
                    act.wait_ge(rhs_prod, 2 * r + l + 1)
                    act.activation(SA[l], psum[6 + l][:, 0:256], ACT.Copy, scale=-1.0).then_inc(rhs_ready, 1)
                for l in range(2):
                    act.wait_ge(sa_prod, 2 * r + l + 1)
                    act.activation(SA[l], psum[6 + l][:, 0:256], ACT.Copy).then_inc(sa_ready, 1)
                for l in range(2):
                    q = (2 * r + l) % 4
                    act.wait_ge(y_prod, 2 * r + l + 1)
                    act.activation(Y[:, c, q * 256:(q + 1) * 256], psum[6 + l][:, 0:256], ACT.Copy)\
                        .then_inc(y_ready, 1)
                if c == 0:
                    for l in range(2):
                        act.wait_ge(keys_turned, 2 * r + l + 1)
                        act.activation(PM[l], psum[l][:, :].rearrange("p (h s) -> p h s", h=4), ACT.Copy)\
                            .then_inc(keys_ready, 1)
            for c in range(2):
                act.wait_ge(y_centred, c + 1)
                act.activation(YQ, YC, ACT.Square).then_inc(y_squared, 1)
                act.wait_ge(gn_ms, c + 1)
                act.activation(gn_var, gn_var, ACT.Sqrt).then_inc(gn_sd, 1)
            turn_hi("rwo")
            hi_upto(U0["rwo"] + 4 + 1)
            norm("mlp0")
            turn_hi("mlp0")
            mlp(0)
            hi_upto(U0["fk"] + 1)
            norm("kv")
            turn_hi("kv")
            turn_hi("attn")
            read_chunk("fk", 0, by_feature(fK))
            read_chunk("fk", 1, by_feature(fK))
            act.wait_ge(acc_read["act"], READ_COUNT[CHUNK0["fk"] + 1][1])
            head_squares(1, fK)
            read_chunk("fv", 0, by_token(fV))
            act.wait_ge(f_z, 1)
            act.activation(fl[0:NH, :], fz[0:NH, :], ACT.Abs).then_inc(f_abs, 1)
            act.wait_ge(f_abs, 1)
            act.activation(fl[0:NH, :], fl[0:NH, :], ACT.Exp, scale=-1.0).then_inc(f_abs, 1)
            act.wait_ge(f_abs, 2)
            act.activation(fl[0:NH, :], fl[0:NH, :], ACT.Ln, bias=1.0).then_inc(f_ln, 1)
            head_roots(1)
            read_chunk("fv", 1, by_token(fV))
            read_chunk("fq", 0, by_feature(fQ))
            read_chunk("fq", 1, by_feature(fQ))
            act.wait_ge(acc_read["act"], READ_COUNT[CHUNK0["fq"] + 1][1])
            act.wait_ge(sums_ready, 2)
            head_squares(2, fQ)
            head_roots(2)
            attention(0, NH, 1.0 / 8, fL, fE, fPT)
            hi_upto(U0["fo"] + 2)
            turn_hi("fo")
            hi_upto(U0["fo"] + 4 + 1)
            norm("mlp1")
            turn_hi("mlp1")
            mlp(1)
            hi_upto(U0["rq"] + 1)
            norm("ret")
            turn_hi("ret")
            hi_upto(U0["rv"])
            for n in range(4):
                read_chunk("rv", n, by_token(rV))
            for n in range(4):
                read_chunk("rg", n, by_token(rG, ACT.Silu))
            for h in range(RET_H):
                for m in range(MT):
                    act.wait_ge(ret_prod, 2 * h + m + 1)
                    act.activation(PJUNK, psum[4 + (2 * h + m) % 4][:, :], ACT.Square,
                                   accum_out=ret_sums[:, 2 * h + m:2 * h + m + 1]).then_inc(ret_ss, 1)
                    act.wait_ge(ret_ss, 2 * h + m + 1)
                act.wait_ge(ret_ms, h + 1)
                act.activation(ret_sums[:, 2 * h:2 * h + 2], ret_sums[:, 2 * h:2 * h + 2], ACT.Sqrt).then_inc(ret_sd, 1)
            hi_upto(U0["reo"] + 2)
            turn_hi("reo")
            post_norm(0, U0["reo"] + 8, 2 * (CHUNK0["reo"] % 2))
            norm("mlp2")
            turn_hi("mlp2")
            mlp(2)
            post_norm(1, U0["mlp2"] + MLP_UNITS, 2)
            norm("moba")
            turn_hi("moba")
            read_chunk("mq", 0, by_feature(mQ))
            read_chunk("mq", 1, by_feature(mQ))
            read_chunk("mk", 0, by_feature(mK))
            read_chunk("mk", 1, by_feature(mK))
            read_chunk("mv", 0, by_token(mV))
            read_chunk("mv", 1, by_token(mV))
            attention(NH, MOBA_H, MOBA_D ** -0.5, mL, mE, mPT)
            hi_upto(U0["mo"] + 2)
            turn_hi("mo")
            post_norm(2, U0["mo"] + 4, 2 * (CHUNK0["mo"] % 2))
            norm("mlp3")
            turn_hi("mlp3")
            mlp(3)
            post_norm(3, U0["mlp3"] + MLP_UNITS, 2)

        @block.vector
        def _(dve):
            done = [0]
            steps = [0]

            def step(ins):
                steps[0] += 1
                ins.then_inc(dve_step, 1)
                dve.wait_ge(dve_step, steps[0])

            def lo_unit(u):
                dve.wait_ge(hi_done, u + 1)
                dve.tensor_tensor(wlo[:, u % SPLIT_RING], raw[:, u % RAW_RING],
                                  whi[:, u % SPLIT_RING].bitcast(F32), ALU.subtract).then_inc(lo_done, 1)

            def lo_upto(n):
                while done[0] < min(n, UNITS):
                    lo_unit(done[0])
                    done[0] += 1

            def norm(name):
                n = NORM0[TI[name]]
                if RESIDUALS[name]:
                    dve.wait_ge(residual, RESIDUALS[name])
                else:
                    dve.wait_ge(x_in, 16)
                dve.wait_ge(ss_done, MT * (n + 1))
                dve.tensor_scalar(norm_ms, norm_ss, 1.0 / D, NORM_EPS, ALU.mult, ALU.add).then_inc(ms_done, 1)
                dve.wait_ge(sd_done, n + 1)
                dve.reciprocal(norm_rstd, norm_sd).then_inc(rstd_done, 1)
                dve.wait_ge(rstd_done, n + 1)
                for m in range(MT):
                    dve.tensor_scalar(XN[:, m], X[:, m], norm_rstd[:, m:m + 1], None, ALU.mult).then_inc(xn_ready, 1)

            def turn_lo(name):
                i = TI[name]
                _, g, kt, _, half = TURNS[i]
                for b in range(kt // 2):
                    dve.wait_ge(turned_hi, SPLIT0[i] + b + 1)
                    src = bank_kt(4 + b % 4)
                    k = half * KT + 2 * b
                    if g is None:
                        dve.tensor_tensor(XL[:, k:k + 2], src, XH[:, k:k + 2].bitcast(F32), ALU.subtract)\
                            .then_inc(turned_lo, 1)
                        continue
                    for j in range(2):
                        ins = dve.scalar_tensor_tensor(XL[:, k + j], src[:, j], gain(g, 2 * b + j),
                                                       XH[:, k + j].bitcast(F32), ALU.mult, ALU.subtract)
                    ins.then_inc(turned_lo, 1)

            def residual_chunks(name):
                for n in range(2):
                    g, kt = CHUNK0[name] + n, 8
                    ue = U0[name] + (n + 1) * kt // UK
                    lo_upto(ue + 1)
                    dve.wait_ge(unit_used, ue)
                    for m in range(MT):
                        x = X[:, m, n * UN:(n + 1) * UN]
                        dve.tensor_tensor(x, x, psum[(g % 2) * 2 + m][:, :], ALU.add).then_inc(residual, 1)

            def mlp(i, before, plain):
                b = U0[f"mlp{i}"]
                s0 = MLP_STEPS * i

                def hidden_lo(q):
                    for k in range(2):
                        dve.wait_ge(h_hi, 2 * q + k + 1)
                        dve.tensor_tensor(XL[:, KT + 2 * k:KT + 2 * k + 2], bank_kt(6 + k),
                                          XH[:, KT + 2 * k:KT + 2 * k + 2].bitcast(F32), ALU.subtract)\
                            .then_inc(h_lo, 1)

                lo_upto(b + 2)
                with dve.Fori(1, MLP_STEPS) as j:
                    for n in range(UK):
                        slot = (n - 2) % RAW_RING
                        dve.wait_ge(hi_done, j * 4 + (b - 2 + n + 1))
                        dve.tensor_tensor(wlo[:, slot % SPLIT_RING], raw[:, slot],
                                          whi[:, slot % SPLIT_RING].bitcast(F32), ALU.subtract).then_inc(lo_done, 1)
                        if n == 1:
                            hidden_lo(j + (s0 - 1))
                done[0] = b + MLP_UNITS - 2
                lo_upto(b + MLP_UNITS)
                hidden_lo(s0 + MLP_STEPS - 1)
                if plain:
                    lo_upto(b + MLP_UNITS + 1)
                    dve.wait_ge(unit_used, b + MLP_UNITS)
                    for n in range(2):
                        for m in range(MT):
                            x = X[:, m, n * UN:(n + 1) * UN]
                            dve.tensor_tensor(x, x, psum[2 + 2 * n + m][:, :], ALU.add).then_inc(residual, 1)

            def post_norm(i, ue, bank0, row):
                lo_upto(ue + 1)
                dve.wait_ge(pss_done, 4 * (i + 1))
                step(dve.tensor_tensor(post_ms, post_ss[:, :, 0], post_ss[:, :, 1], ALU.add))
                dve.tensor_scalar(post_ms, post_ms, 1.0 / D, NORM_EPS, ALU.mult, ALU.add).then_inc(pms_done, 1)
                dve.wait_ge(psd_done, i + 1)
                step(dve.reciprocal(post_rstd, post_sd))
                if i % 2 == 0:
                    dve.wait_ge(post_in, 16 * (i + 2))
                for n in range(2):
                    for m in range(MT):
                        tmp, x = PTMP[:, m], X[:, m, n * UN:(n + 1) * UN]
                        step(dve.scalar_tensor_tensor(tmp, psum[bank0 + 2 * n + m][:, :], post_rstd[:, m:m + 1],
                                                      POST[:, row, n * UN:(n + 1) * UN], ALU.mult, ALU.mult))
                        dve.tensor_tensor(x, x, tmp, ALU.add).then_inc(residual, 1)

            def head_sums(i, scale, eps):
                r = rn if i == 0 else frn
                dve.wait_ge(sums_ready, i + 1)
                dve.tensor_scalar(r, psum[4][:, 0:T], scale, eps, ALU.mult, ALU.add).then_inc(sums_ms, 1)
                dve.wait_ge(sums_sd, i + 1)
                if i == 0:
                    step(dve.tensor_scalar(r, r, 1e-12, None, ALU.max))
                dve.reciprocal(r, r).then_inc(rn_ready, 1)

            def attention(a0, heads, scale, L, CAUSAL, V_, dh, O):
                per = 512 // (MT * dh)
                for h in range(heads + 4):
                    if h < heads:
                        dve.wait_ge(logits, a0 + h + 1)
                        if h >= 2:
                            dve.wait_ge(expd, a0 + h - 1)
                        dve.scalar_tensor_tensor(L[:, h % 2], psum[h % 2][:, 0:384], scale, CAUSAL,
                                                 ALU.mult, ALU.add).then_inc(masked, 1)
                        dve.wait_ge(masked, a0 + h + 1)
                        for m in range(MT):
                            c0, c1 = (0, P) if m == 0 else (P, 3 * P)
                            ins = dve.tensor_reduce(att_nmax[:, h % 4, m:m + 1], L[:, h % 2, c0:c1], AXX, ALU.max,
                                                    negate=True)
                        ins.then_inc(maxed, 1)
                    g = h - 4
                    if g >= 0 and g % per == per - 1:
                        h0 = g - per + 1
                        dve.wait_ge(expd, a0 + g + 1)
                        s = att_sum[:, h0:g + 1]
                        step(dve.reciprocal(s, s))
                        dve.wait_ge(av_prod, a0 + g + 1)
                        src = psum[4 + (g // per) % 2][:, :].rearrange("p (h m d) -> p m h d", h=per, m=MT)
                        for m in range(MT):
                            ins = dve.tensor_tensor(
                                O[:, m, h0 * dh:(g + 1) * dh].rearrange("p (h d) -> p h d", h=per), src[:, m],
                                s[:, :, m:m + 1].broadcast_to((P, per, dh)), ALU.mult)
                        ins.then_inc(att_out, 1)

            norm("rwkv")
            lo_upto(2)
            dve.wait_ge(hT_ready, 4)
            dve.tensor_tensor(xxT[:, :, 1:T], hT[:, :, 0:T - 1], hT[:, :, 1:T], ALU.subtract)
            step(dve.tensor_scalar(xxT[:, :, 0:1], hT[:, :, 0:1], -1.0, None, ALU.mult))

            def mix(order, mu):
                for k in range(KT):
                    ins = dve.scalar_tensor_tensor(XM[order % 2][:, k], xxT[:, k], gain(f"mu{mu}", k), hT[:, k],
                                                   ALU.mult, ALU.add)
                ins.then_inc(mixed, 1)

            def mix_to_lo(j, order, half):
                dve.wait_ge(mix_hi, j + 1)
                s = slice(half * KT, (half + 1) * KT)
                dve.tensor_tensor(XL[:, s], XM[order % 2], XH[:, s].bitcast(F32), ALU.subtract).then_inc(mix_lo, 1)

            mix(0, 0)
            mix_to_lo(0, 0, 0)
            mix(1, 1)
            lo_upto(3)
            mix(2, 2)
            mix_to_lo(1, 2, 1)
            lo_upto(5)
            dve.wait_ge(lora1, 1)
            mix(3, 4)
            lo_upto(7)
            mix(4, 3)
            mix_to_lo(2, 4, 0)
            lo_upto(9)
            dve.wait_ge(lora1, 2)
            mix(5, 5)
            lo_upto(13)
            dve.wait_ge(lw_ready, 1)
            dve.memset(Lx[:, :, 0:1], 0.0)
            step(dve.memset(ones, 1.0))
            lw16 = lwT.rearrange("p k (c t) -> p (k c) t", c=2)
            for q in range(2 * KT):
                ins = dve.tensor_tensor_scan(Lx[:, q, 1:LW], ones, lw16[:, q], 0.0, ALU.mult, ALU.add)
            step(ins)
            Lc = Lx.rearrange("p (k c) t -> p k c t", c=2)
            step(dve.tensor_copy(mids, Lx[:, :, HD:HD + 1]))
            mid2 = mids.rearrange("p (k c) o -> p k (c o)", c=2)
            step(dve.tensor_tensor(state_scale, Lc[:, :, 0, P], mid2[:, :, 0], ALU.subtract))
            step(dve.tensor_tensor(state_scale, state_scale, mid2[:, :, 1], ALU.add))
            dve.tensor_tensor(Lx, Lx, mids.broadcast_to((P, 2 * KT, LW)), ALU.subtract).then_inc(centred, 1)
            dve.wait_ge(lora2, 12)
            for p in range(KT):
                ins = dve.tensor_scalar(kkT[:, p], kT[:, p], gain("k_k", p), None, ALU.mult)
            ins.then_inc(prepared, 1)
            head_sums(0, 1.0, 0.0)
            for p in range(KT):
                ins = dve.tensor_scalar(sqT[:, p], aT[:, p], 1.0, gain("k_a", p), ALU.subtract, ALU.mult)
            step(ins)
            step(dve.scalar_tensor_tensor(kT, sqT, 1.0, kT, ALU.add, ALU.mult))
            for p in range(KT):
                ins = dve.scalar_tensor_tensor(sqT[:, p], rT[:, p], gain("r_k", p), kT[:, p], ALU.mult, ALU.mult)
            ins.then_inc(bonus_prod, 1)
            for b in range(4):
                dve.wait_ge(rn_spread, b + 1)
                k2 = kkT[:, 2 * b:2 * b + 2]
                ins = dve.tensor_tensor(k2, k2, bank_kt(4 + b), ALU.mult)
                ins.then_inc(spread_read, 1)
            dve.wait_ge(spread_read, 4)
            step(dve.tensor_tensor(aT, kkT, aT, ALU.mult))
            dve.wait_ge(exps_ready, 2)
            kk16 = kkT.rearrange("p k (c t) -> p (k c) t", c=2)
            r16 = rT.rearrange("p k (c t) -> p (k c) t", c=2)
            k16 = kT.rearrange("p k (c t) -> p (k c) t", c=2)
            b16 = BE.rearrange("p k (c t) -> p (k c) t", c=2)
            dve.tensor_tensor(AR[:, :, 0], kk16, E1[:, :, 0:P], ALU.mult)
            dve.tensor_tensor(AR[:, :, 1], r16, E1[:, :, 1:LW], ALU.mult)
            dve.tensor_tensor(b16, b16, E2[:, :, 1:LW], ALU.mult)
            dve.tensor_tensor(k16, k16, E2[:, :, 1:LW], ALU.mult).then_inc(prepared, 1)
            dve.wait_ge(prepared, 2)
            dve.wait_ge(bonus_sum, 1)
            dve.tensor_copy(bonus, psum[7][:, 0:32]).then_inc(bonus_read, 1)
            for l in range(2):
                for blk in range(4):
                    ins = dve.memset(M[l][HD:P, :, blk * P:blk * P + HD], 0.0)
            step(ins)
            dve.wait_ge(scale_ready, 1)
            dve.wait_ge(const_in, 16 * (len(CONST_KEEP) - 2))
            first4 = keep["first_mask"][:, :].unsqueeze(1).broadcast_to((P, 4, P))
            ident4 = ident[:, :].unsqueeze(1).broadcast_to((P, 4, P))
            pm = keep["pair_masks"]
            for r in range(4):
                c = r // 2
                for l in range(2):
                    gi = 2 * r + l
                    for h in range(4):
                        b = psum[4 * l + h]
                        dve.wait_ge(pair_prod, 4 * gi + h + 1)
                        dve.tensor_tensor(M[l][0:HD, h], b[0:HD, :], pm[0:HD, :], ALU.mult)
                        dve.tensor_tensor(M[l][HD:P, h].rearrange("p (b t) -> p b t", b=4)[:, :, HD:P],
                                          b[HD:P, :].rearrange("p (b t) -> p b t", b=4)[:, :, HD:P],
                                          pm[HD:P, :].rearrange("p (b t) -> p b t", b=4)[:, :, HD:P],
                                          ALU.mult).then_inc(pair_masked, 1)
                    dve.wait_ge(pair_masked, 4 * gi + 4)
                    step(dve.tensor_tensor(TT_[l], M[l][:, :, 0:P], first4, ALU.mult))
                    dve.tensor_tensor(TT_[l], TT_[l], ident4, ALU.add).then_inc(first_ready, 1)
                for i in range(6):
                    lm = keep["level_masks"][:, i * P:(i + 1) * P].unsqueeze(1).broadcast_to((P, 4, P))
                    for l in range(2):
                        n = 12 * r + 2 * i + l
                        dve.wait_ge(half_prod, n + 1)
                        dve.tensor_tensor(PM[l], psum[l][:, :].rearrange("p (h s) -> p h s", h=4), lm, ALU.mult)\
                            .then_inc(half_masked, 1)
                    for l in range(2):
                        n = 12 * r + 2 * i + l
                        dve.wait_ge(step_prod, n + 1)
                        if i < 5:
                            dve.tensor_tensor(TI_[l], TI_[l], psum[2 + l][:, :].rearrange("p (h s) -> p h s", h=4),
                                              ALU.subtract)
                        dve.tensor_tensor(TT_[l], TT_[l], psum[4 + l][:, :].rearrange("p (h s) -> p h s", h=4),
                                          ALU.subtract).then_inc(doubled, 1)
                if c == 0:
                    for l in range(2):
                        p0 = 2 * (2 * r + l)
                        dve.wait_ge(state_prod, 2 * r + l + 1)
                        for pp in range(2):
                            dve.scalar_tensor_tensor(S0[:, p0 + pp], psum[2 + l][:, pp * P:(pp + 1) * P],
                                                     state_scale[:, p0 + pp:p0 + pp + 1], keep["head_blocks"][:, :],
                                                     ALU.mult, ALU.mult).then_inc(state_ready, 1)
            dve.wait_ge(y_ready, 8)
            for c in range(2):
                y = Y[:, c].rearrange("p (h d) -> p h d", h=NH)
                yc = YC.rearrange("p (h d) -> p h d", h=NH)
                vv = V[:, c].rearrange("p (h d) -> p h d", h=NH)
                wide = (P, NH, HD)
                step(dve.tensor_reduce(gn_mean, y, AXX, ALU.add))
                step(dve.tensor_scalar(gn_mean, gn_mean, 1.0 / HD, None, ALU.mult))
                dve.tensor_tensor(yc, y, gn_mean.unsqueeze(2).broadcast_to(wide), ALU.subtract).then_inc(y_centred, 1)
                dve.wait_ge(y_squared, c + 1)
                step(dve.tensor_reduce(gn_var, YQ.rearrange("p (h d) -> p h d", h=NH), AXX, ALU.add))
                dve.tensor_scalar(gn_var, gn_var, 1.0 / HD, GN_EPS, ALU.mult, ALU.add).then_inc(gn_ms, 1)
                dve.wait_ge(gn_sd, c + 1)
                step(dve.reciprocal(gn_var, gn_var))
                step(dve.tensor_tensor(yc, yc, gn_var.unsqueeze(2).broadcast_to(wide), ALU.mult))
                dve.wait_ge(lnrow_in, 32)
                step(dve.tensor_tensor(YC, YC, LNROW[:, 0], ALU.mult))
                dve.tensor_tensor(YC, YC, LNROW[:, 1], ALU.add)
                bs = bonus.rearrange("p (c h) -> p c h", c=2)[:, c].unsqueeze(2).broadcast_to(wide)
                step(dve.tensor_tensor(y, vv, bs, ALU.mult))
                step(dve.tensor_tensor(YC, YC, Y[:, c], ALU.add))
                dve.tensor_tensor(Y[:, c], YC, G[:, c], ALU.mult).then_inc(y_done, 1)
            turn_lo("rwo")
            residual_chunks("rwo")
            norm("mlp0")
            turn_lo("mlp0")
            mlp(0, 4, True)
            norm("kv")
            turn_lo("kv")
            turn_lo("attn")
            lo_upto(U0["fv"] + 1)
            dve.wait_ge(f_prod, 1)
            dve.wait_ge(fox_in, 16 * 3)
            dve.tensor_scalar(fz[0:NH, :], psum[4][0:NH, 0:T], fbias[0:NH, :], None, ALU.add).then_inc(f_z, 1)
            lo_upto(U0["fv"] + 3)
            head_sums(1, 1.0 / HD, NORM_EPS)
            dve.wait_ge(f_ln, 1)
            step(dve.scalar_tensor_tensor(fz[0:NH, :], fz[0:NH, :], 0.0, fl[0:NH, :], ALU.min, ALU.subtract))
            step(dve.memset(fl, 1.0))
            step(dve.tensor_tensor_scan(fc[0:NH, :], fl[0:NH, :], fz[0:NH, :], 0.0, ALU.mult, ALU.add))
            dve.wait_ge(zeroed, 2)
            dve.tensor_scalar(negc[0:NH, :], fc[0:NH, :], -8.0, None, ALU.mult).then_inc(negc_ready, 1)
            lo_upto(U0["fq"] + 1)
            for b in range(4):
                dve.wait_ge(rn_spread, 4 + b + 1)
                for j in range(2):
                    p = 2 * b + j
                    for f in range(2):
                        s = slice(f * HD, (f + 1) * HD)
                        ins = dve.scalar_tensor_tensor(fKP[s, 2 * p + f], bank_kt(4 + b)[s, j],
                                                       gain("k_norm_g", p)[s], fK[s, p], ALU.mult, ALU.mult)
                ins.then_inc(spread_read, 1)
            lo_upto(U0["fo"] + 1)
            head_sums(2, 1.0 / HD, NORM_EPS)
            for b in range(4):
                dve.wait_ge(rn_spread, 8 + b + 1)
                for j in range(2):
                    p = 2 * b + j
                    ins = dve.scalar_tensor_tensor(fQ[:, p], bank_kt(4 + b)[:, j], gain("q_norm_g", p), fQ[:, p],
                                                   ALU.mult, ALU.mult)
                ins.then_inc(spread_read, 1)
            attention(0, NH, 1.0 / 8, fL, fCAUSAL, fV, HD, fO)
            lo_upto(U0["fo"] + 2)
            turn_lo("fo")
            residual_chunks("fo")
            norm("mlp1")
            turn_lo("mlp1")
            mlp(1, 12, True)
            norm("ret")
            turn_lo("ret")
            dve.wait_ge(ret_in, 16 * 3)
            cos2 = rCOS.unsqueeze(1).broadcast_to((P, 2, T))
            sin2 = rSIN.unsqueeze(1).broadcast_to((P, 2, T))
            for i, (name, dst) in enumerate((("rq", rQ), ("rk", rK))):
                for n in range(2):
                    g = CHUNK0[name] + n
                    ue = U0[name] + 2 * (n + 1)
                    lo_upto(ue + 1)
                    dve.wait_ge(unit_used, ue)
                    for j in range(2):
                        h, s = 2 * n + j, j
                        src = bank_kt((g % 2) * 2 + j)
                        dve.tensor_tensor(rA[s], src, cos2, ALU.mult)
                        ins = dve.tensor_tensor(rB[s], src, sin2, ALU.mult)
                        ins.then_inc(acc_read["dve"], 1)
                        dve.wait_ge(acc_read["dve"], READ_COUNT[g][1] - 1 + j)
                        dve.tensor_tensor(dst[:, h, 0], rA[s][:, 0], rB[s][:, 1], ALU.subtract)
                        dve.tensor_tensor(dst[:, h, 1], rB[s][:, 0], rA[s][:, 1], ALU.add).then_inc(rotated, 1)
            lo_upto(U0["reo"])
            for h in range(RET_H):
                dve.wait_ge(scores, h + 1)
                if h >= 2:
                    dve.wait_ge(ret_prod, 2 * (h - 1))
                d = rDEC[:, h]
                dve.tensor_tensor(rPT[:, h % 2, 0:T], psum[h % 2][:, 0:T], d, ALU.mult)
                dve.tensor_tensor(rPT[:, h % 2, T:T + P], psum[h % 2][:, T:T + P], d[:, 0:P], ALU.mult)\
                    .then_inc(decayed, 1)
                dve.wait_ge(ret_ss, 2 * h + 2)
                s = ret_sums[:, 2 * h:2 * h + 2]
                dve.tensor_scalar(s, s, 1.0 / RET_DV, NORM_EPS, ALU.mult, ALU.add).then_inc(ret_ms, 1)
                dve.wait_ge(ret_sd, h + 1)
                step(dve.reciprocal(s, s))
                if h == 0:
                    dve.wait_ge(acc_read["act"], READ_COUNT[CHUNK0["rg"] + 3][1])
                for m in range(MT):
                    gt = rG[:, m, h * RET_DV:(h + 1) * RET_DV]
                    dve.scalar_tensor_tensor(gt, psum[4 + (2 * h + m) % 4][:, :], s[:, m:m + 1], gt, ALU.mult,
                                             ALU.mult).then_inc(ret_out, 1)
            lo_upto(U0["reo"] + 2)
            turn_lo("reo")
            post_norm(0, U0["reo"] + 8, 0, 0)
            norm("mlp2")
            turn_lo("mlp2")
            mlp(2, 20, False)
            post_norm(1, U0["mlp2"] + MLP_UNITS, 2, 1)
            norm("moba")
            turn_lo("moba")
            dve.wait_ge(moba_in, 16 * 4)
            for i, (name, src) in enumerate((("mq", mQ), ("mk", mK))):
                lo_upto(U0["mk"] + 5)
                dve.wait_ge(acc_read["act"], READ_COUNT[CHUNK0[name] + 1][1])
                for b in range(4):
                    s = slice(2 * b, 2 * b + 2)
                    x = src[0:ROPE, s]
                    dve.wait_ge(rope_swapped, 4 * i + b + 1)
                    step(dve.tensor_tensor(mTMP[0:ROPE], bank_kt(4 + b)[0:ROPE],
                                           mSIN[0:ROPE].unsqueeze(1).broadcast_to((ROPE, 2, T)), ALU.mult))
                    step(dve.tensor_tensor(mTMP2[0:ROPE], x, mCOS[0:ROPE].unsqueeze(1).broadcast_to((ROPE, 2, T)),
                                           ALU.mult))
                    dve.tensor_tensor(x, mTMP[0:ROPE], mTMP2[0:ROPE], ALU.add).then_inc(roped, 1)
                    dve.wait_ge(roped, 4 * i + b + 1)
            lo_upto(U0["mo"] + 1)
            attention(NH, MOBA_H, MOBA_D ** -0.5, mL, mCAUSAL, mV, MOBA_D, mO)
            lo_upto(U0["mo"] + 2)
            turn_lo("mo")
            post_norm(2, U0["mo"] + 4, 0, 0)
            norm("mlp3")
            turn_lo("mlp3")
            mlp(3, 28, False)
            post_norm(3, U0["mlp3"] + MLP_UNITS, 2, 1)

        @block.gpsimd
        def _(pool):
            def squares(i):
                s0 = MLP_STEPS * i

                def one(q):
                    for m in range(MT):
                        pool.wait_ge(relu_done, 2 * q + m + 1)
                        pool.tensor_tensor(RELU[:, m], RELU[:, m], RELU[:, m], ALU.mult).then_inc(square_done, 1)

                with pool.Fori(0, MLP_STEPS) as j:
                    one(j + s0)

            pool.wait_ge(const_in, 16 * (len(CONST_KEEP) - 2))
            pool.wait_ge(lora2, 12)
            pool.dma_start(SPREAD.rearrange("p k f -> p (k f)"), a["head_spread"]).then_inc(spread_in, 16)
            pool.wait_ge(prepared, 2)
            for gi in range(8):
                c, p0 = gi // 4, 2 * (gi % 4)
                if gi >= 1:
                    pool.wait_ge(pair_prod, 4 * gi)
                for s, src in enumerate((BE, kT)):
                    for f in range(2):
                        pool.tensor_scalar(PAD[:, s].rearrange("p (q f) t -> p f q t", f=2)[:, f],
                                           src[:, p0:p0 + 2, c * P:(c + 1) * P], keep["head_halves"][:, f:f + 1], 1.0,
                                           ALU.mult, ALU.mult).then_inc(padded, 1)
            pool.wait_ge(y_ready, 8)
            for i in range(2):
                pool.dma_start(LNROW[:, i], a[ROWS[i]].partition_broadcast(P)).then_inc(lnrow_in, 16)
            squares(0)
            pool.dma_start(wf.rearrange("p k n -> p (k n)"), a["wf"]).then_inc(fox_in, 16)
            pool.dma_start(fbias[0:NH, :], a["f_bias"]).then_inc(fox_in, 16)
            pool.dma_start(fCAUSAL, a["causal"]).then_inc(fox_in, 16)
            pool.dma_start(SPREAD.rearrange("p k f -> p (k f)"), a["head_spread"]).then_inc(spread_in, 16)
            pool.memset(negc, 0.0).then_inc(zeroed, 1)
            pool.wait_ge(h_lo, 2 * MLP_STEPS)
            pool.memset(fKP, 0.0).then_inc(zeroed, 1)
            squares(1)
            for n, dst in (("ret_decay", at(0, RET_H * T)), ("ret_cos", rCOS), ("ret_sin", rSIN)):
                pool.dma_start(dst, a[n]).then_inc(ret_in, 16)
            for i in range(2):
                pool.dma_start(POST[:, i], a[ROWS[2 + i]].partition_broadcast(P)).then_inc(post_in, 16)
            squares(2)
            for n, dst, k in (("rope_cos", mCOS, ROPE), ("rope_sin", mSIN, ROPE), ("rope_swap", mSWAP, P),
                              ("causal", mCAUSAL, P)):
                pool.dma_start(dst[0:k], a[n]).then_inc(moba_in, 16)
            pool.wait_ge(residual, 24)
            for i in range(2):
                pool.dma_start(POST[:, i], a[ROWS[4 + i]].partition_broadcast(P)).then_inc(post_in, 16)
            squares(3)

        @block.tensor
        def _(pe):
            def turn(name, src):
                i = TI[name]
                kt = TURNS[i][2]
                for b in range(kt // 2):
                    if b >= 4:
                        pe.wait_ge(turned_lo, SPLIT0[i] + b - 3)
                    for j in range(2):
                        for m in range(MT):
                            k = 2 * b + j
                            ins = pe.transpose(psum[4 + b % 4][:, j * T + m * P:j * T + (m + 1) * P],
                                               src[:, m, k * P:(k + 1) * P], ident[:, :])
                    ins.then_inc(turned, 1)

            def norm_turn(name):
                pe.wait_ge(xn_ready, MT * (NORM0[TI[name]] + 1))
                turn(name, XN)

            def passes(out_, x, w, xs, ws, start, stop_=False):
                (xh, xl), (wh, wl) = x, w
                pe.matmul(out_, xh[xs], wh[ws], start=start, stop=False)
                pe.matmul(out_, xh[xs], wl[ws], start=False, stop=False)
                return pe.matmul(out_, xl[xs], wh[ws], start=False, stop=stop_)

            def chunk(name, n, form, half=0, kts=KT, ready=None):
                g = CHUNK0[name] + n
                if g >= 2 and READ_COUNT[g - 2][0] != "sum":
                    who, c = READ_COUNT[g - 2]
                    pe.wait_ge(acc_read[who], c)
                for kg in range(kts // UK):
                    u = U0[name] + n * (kts // UK) + kg
                    if ready is not None and n == 0:
                        ready(kg)
                    pe.wait_ge(lo_done, u + 1)
                    s = u % SPLIT_RING
                    for k in range(UK):
                        kt = kg * UK + k
                        first, last = kt == 0, kt == kts - 1
                        x = half * KT + kt
                        if form == "token":
                            for m in range(MT):
                                ins = passes(psum[(g % 2) * 2 + m][:, :], (XH, XL), (whi, wlo),
                                             (slice(None), x, slice(m * P, (m + 1) * P)),
                                             (slice(None), s, k), first, last)
                        else:
                            for f in range(UK):
                                o = psum[(g % 2) * 2 + f // 2][:, (f % 2) * T:(f % 2 + 1) * T]
                                ins = passes(o, (whi, wlo), (XH, XL),
                                             (slice(None), s, k, slice(f * P, (f + 1) * P)),
                                             (slice(None), x), first and f % 2 == 0, last and f % 2 == 1)
                    ins.then_inc(unit_used, 1)

            def split_ready(name):
                return lambda kg: pe.wait_ge(turned_lo, SPLIT0[TI[name]] + 2 * (kg + 1))

            def mlp(i):
                b, name = U0[f"mlp{i}"], f"mlp{i}"
                s0 = MLP_STEPS * i

                def up(u, q, kg):
                    for k in range(UK):
                        kt = kg * UK + k
                        for m in range(MT):
                            ins = passes(psum[m][:, :], (XH, XL), (whi, wlo),
                                         (slice(None), kt, slice(m * P, (m + 1) * P)), (slice(None), u, k),
                                         kt == 0, kt == KT - 1)
                    ins.then_inc(unit_used, 1)

                def hidden_turn(q):
                    pe.wait_ge(square_done, q * 2 + 2)
                    for k in range(2):
                        for j in range(2):
                            for m in range(MT):
                                f = 2 * k + j
                                ins = pe.transpose(psum[6 + k][:, j * T + m * P:j * T + (m + 1) * P],
                                                   RELU[:, m, f * P:(f + 1) * P], ident[:, :])
                        ins.then_inc(h_turned, 1)

                def down(u, n, first, last):
                    for k in range(UK):
                        for m in range(MT):
                            ins = passes(psum[2 + 2 * n + m][:, :], (XH, XL), (whi, wlo),
                                         (slice(None), KT + k, slice(m * P, (m + 1) * P)), (slice(None), u, k),
                                         first and k == 0, last and k == UK - 1)
                    ins.then_inc(unit_used, 1)

                for kg in range(2):
                    pe.wait_ge(turned_lo, SPLIT0[TI[name]] + 2 * (kg + 1))
                    pe.wait_ge(lo_done, b + kg + 1)
                    up(kg, s0, kg)

                def body(j, first):
                    pe.wait_ge(relu_done, (j + s0) * 2)
                    pe.wait_ge(lo_done, j * 4 + (b - 1))
                    up(0, j, 0)
                    hidden_turn(j + (s0 - 1))
                    pe.wait_ge(lo_done, j * 4 + b)
                    up(1, j, 1)
                    pe.wait_ge(h_lo, (j + s0) * 2)
                    for n in range(2):
                        pe.wait_ge(lo_done, j * 4 + (b + n + 1))
                        down(n, n, first, False)

                body(1, True)
                with pe.Fori(2, MLP_STEPS) as j:
                    body(j, False)
                q = s0 + MLP_STEPS - 1
                hidden_turn(q)
                pe.wait_ge(h_lo, 2 * (q + 1))
                for n in range(2):
                    pe.wait_ge(lo_done, b + MLP_UNITS - 1 + n)
                    down(n, n, False, True)

            def head_sums(i, sq):
                pe.wait_ge(sq_ready, i + 1)
                for p in range(KT):
                    ins = pe.matmul(psum[4][:, 0:T], keep["head_window"][:, 14 - 2 * p:14 - 2 * p + P], sq[:, p],
                                    start=(p == 0), stop=(p == KT - 1))
                ins.then_inc(sums_ready, 1)

            def head_spread(i, r):
                pe.wait_ge(rn_ready, i + 1)
                pe.wait_ge(spread_in, 16 if i == 0 else 32)
                for p in range(KT):
                    ins = pe.matmul(psum[4 + p // 2][:, (p % 2) * T:(p % 2 + 1) * T], SPREAD[:, p], r,
                                    start=(p % 2 == 0), stop=(p % 2 == 1))
                    if p % 2:
                        ins.then_inc(rn_spread, 1)

            def attention(a0, heads, dh, q_of, k_of, bias, E, PT, V_):
                per = 512 // (MT * dh)
                for h in range(heads + 3):
                    if h < heads:
                        if h >= 2:
                            pe.wait_ge(masked, a0 + h - 1)
                        for m in range(MT):
                            c0, n = (0, P) if m == 0 else (P, T)
                            o = psum[h % 2][:, c0:c0 + n]
                            ins = pe.matmul(o, q_of(h)[:, m * P:(m + 1) * P], k_of(h)[:, 0:n], start=(m == 0),
                                            stop=(not bias and m == 1))
                            if bias:
                                ins = pe.matmul(o, ident[:, h:h + 1].broadcast_to((P, P)), negc[:, 0:n],
                                                start=False, stop=(m == 1))
                        ins.then_inc(logits, 1)
                    g = h - 1
                    if 0 <= g < heads:
                        pe.wait_ge(expd, a0 + g + 1)
                        if g >= 2:
                            pe.wait_ge(pt_ready, a0 + g - 1)
                        for s in range(3):
                            ins = pe.transpose(psum[2 + g % 2][:, s * P:(s + 1) * P], E[:, g % 2, s * P:(s + 1) * P],
                                               ident[:, :])
                        ins.then_inc(e_turned, 1)
                    g = h - 3
                    if g >= 0:
                        pe.wait_ge(pt_ready, a0 + g + 1)
                        if g % per == 0 and g // per >= 2:
                            pe.wait_ge(att_out, a0 // 4 + g // per - 1)
                        o = psum[4 + (g // per) % 2][:, (g % per) * MT * dh:(g % per + 1) * MT * dh]
                        v = V_[:, :, g * dh:(g + 1) * dh]
                        pt = PT[:, g % 2]
                        pe.matmul(o[:, 0:dh], pt[:, 0:P], v[:, 0], start=(g % per == 0), stop=False)
                        pe.matmul(o[:, dh:2 * dh], pt[:, P:2 * P], v[:, 0], start=False, stop=False)
                        pe.matmul(o[:, dh:2 * dh], pt[:, 2 * P:3 * P], v[:, 1], start=False,
                                  stop=(g % per == per - 1)).then_inc(av_prod, 1)

            pe.wait_ge(ident_in, 16)
            norm_turn("rwkv")
            mix_wait = [lambda kg, j=j: pe.wait_ge(mix_lo, j + 1) for j in range(3)]

            def lora_in1(order, w, n, bank):
                for k in range(KT):
                    ins = pe.matmul(psum[bank][0:min(n, P), 0:T], w[:, k, 0:min(n, P)], XM[order % 2][:, k],
                                    start=(k == 0), stop=(k == KT - 1))
                if n > P:
                    for k in range(KT):
                        ins = pe.matmul(psum[bank + 1][0:n - P, 0:T], w[:, k, P:n], XM[order % 2][:, k],
                                        start=(k == 0), stop=(k == KT - 1))
                ins.then_inc(lora1, 1)

            chunk("r", 0, "feature", 0, ready=mix_wait[0])
            chunk("r", 1, "feature", 0)
            pe.wait_ge(lora_in, 16 * 7)
            pe.wait_ge(mixed, 2)
            lora_in1(1, w1s, LORA, 4)
            chunk("k", 0, "feature", 1, ready=mix_wait[1])
            chunk("k", 1, "feature", 1)
            pe.wait_ge(mixed, 4)
            lora_in1(3, a1s, LORA, 5)
            chunk("v", 0, "token", 0, ready=mix_wait[2])
            chunk("v", 1, "token", 0)
            pe.wait_ge(mixed, 6)
            lora_in1(5, g1s, GATE, 6)
            pe.wait_ge(lora1_act, 4)
            for b in range(4):
                m, n = b // 2, b % 2
                pe.matmul(psum[4 + b][:, :], sga[:, m * P:(m + 1) * P], g2a[:, n * UN:(n + 1) * UN], start=True,
                          stop=False)
                pe.matmul(psum[4 + b][:, :], sgb[0:GATE - P, m * P:(m + 1) * P], g2b[0:GATE - P, n * UN:(n + 1) * UN],
                          start=False, stop=True).then_inc(lora2, 1)
            for q, (w2, t1) in enumerate(((w2s, tw), (a2s, ta))):
                for b in range(4):
                    pe.wait_ge(lora2_read, 4 * q + b + 1)
                    for j in range(2):
                        p = 2 * b + j
                        ins = pe.matmul(psum[4 + b][:, j * T:(j + 1) * T], w2[0:LORA, p * P:(p + 1) * P],
                                        t1[0:LORA, :], start=(j == 0), stop=(j == 1))
                    ins.then_inc(lora2, 1)
            pe.wait_ge(lora2_read, 12)
            pe.wait_ge(const_in, 16 * (len(CONST_KEEP) - 2))
            head_sums(0, sqT)
            head_spread(0, rn)
            pe.wait_ge(bonus_prod, 1)
            pe.wait_ge(spread_read, 4)
            for q in range(2 * KT):
                c, p = q // KT, q % KT
                ins = pe.matmul(psum[7][:, 16 * c + 2 * p:16 * c + 2 * p + 2], sqT[:, p, c * P:(c + 1) * P],
                                keep["head_window"][:, 14:16], start=(q == 0), stop=(q == 2 * KT - 1))
            ins.then_inc(bonus_sum, 1)
            pe.wait_ge(prepared, 2)
            pe.wait_ge(bonus_read, 1)
            for r in range(4):
                c = r // 2
                if r:
                    pe.wait_ge(y_ready, 2 * r)
                    pe.wait_ge(state_ready, 4 * min(r, 2))
                for l in range(2):
                    gi = 2 * r + l
                    p0 = 2 * (gi % 4)
                    pe.wait_ge(padded, 4 * (gi + 1))
                    for h in range(4):
                        ar = AR[:, (p0 + h // 2) * 2 + c]
                        for s in range(2):
                            ins = pe.matmul(psum[4 * l + h][:, s * T:(s + 1) * T], PAD[:, s, h], ar, start=(s == 0),
                                            stop=(s == 1))
                        ins.then_inc(pair_prod, 1)
                pe.wait_ge(pair_masked, 4 * (2 * r + 2))
                for l in range(2):
                    gi = 2 * r + l
                    pe.wait_ge(first_ready, gi + 1)
                    for h in range(4):
                        ins = pe.transpose(psum[2 + l][:, h * P:(h + 1) * P], TT_[l][:, h], ident[:, :])
                    ins.then_inc(first_turned, 1)
                for i in range(6):
                    for l in range(2):
                        if i == 0:
                            pe.wait_ge(inv_ready, 2 * r + l + 1)
                        else:
                            pe.wait_ge(doubled, 12 * r + 2 * (i - 1) + l + 1)
                        for h in range(4):
                            ins = pe.matmul(psum[l][:, h * P:(h + 1) * P], M[l][:, h, 0:P], TI_[l][:, h],
                                            start=(h == 0), stop=(h == 3))
                        ins.then_inc(half_prod, 1)
                    for l in range(2):
                        pe.wait_ge(half_masked, 12 * r + 2 * i + l + 1)
                        if i < 5:
                            for h in range(4):
                                pe.matmul(psum[2 + l][:, h * P:(h + 1) * P], TT_[l][:, h], PM[l][:, h],
                                          start=(h == 0), stop=(h == 3))
                        for h in range(4):
                            ins = pe.matmul(psum[4 + l][:, h * P:(h + 1) * P], PM[l][:, h], TT_[l][:, h],
                                            start=(h == 0), stop=(h == 3))
                        ins.then_inc(step_prod, 1)

                def carried(l, p0, which):
                    for pp in range(2):
                        pe.matmul(psum[6 + l][:, pp * P:(pp + 1) * P], AR[:, (p0 + pp) * 2 + c, which],
                                  S0[:, p0 + pp], start=(pp == 0), stop=False)

                for l in range(2):
                    p0 = 2 * ((2 * r + l) % 4)
                    if c:
                        carried(l, p0, 0)
                    for h in range(4):
                        hd = (2 * p0 + h) * HD
                        ins = pe.matmul(psum[6 + l][:, h * HD:(h + 1) * HD], M[l][:, h, 2 * P:3 * P],
                                        V[:, c, hd:hd + HD], start=(c == 0 and h == 0), stop=(h == 3))
                    ins.then_inc(rhs_prod, 1)
                for l in range(2):
                    pe.wait_ge(rhs_ready, 2 * r + l + 1)
                    pe.wait_ge(doubled, 12 * r + 10 + l + 1)
                    for h in range(4):
                        ins = pe.matmul(psum[6 + l][:, h * HD:(h + 1) * HD], TT_[l][:, h],
                                        SA[l][:, h * HD:(h + 1) * HD], start=(h == 0), stop=(h == 3))
                    ins.then_inc(sa_prod, 1)
                for l in range(2):
                    p0 = 2 * ((2 * r + l) % 4)
                    pe.wait_ge(sa_ready, 2 * r + l + 1)
                    if c:
                        carried(l, p0, 1)
                    for h in range(4):
                        hd = (2 * p0 + h) * HD
                        o = psum[6 + l][:, h * HD:(h + 1) * HD]
                        pe.matmul(o, M[l][:, h, P:2 * P], SA[l][:, h * HD:(h + 1) * HD], start=(c == 0 and h == 0),
                                  stop=False)
                        ins = pe.matmul(o, M[l][:, h, 3 * P:4 * P], V[:, c, hd:hd + HD], start=False,
                                        stop=(h == 3))
                    ins.then_inc(y_prod, 1)
                if c == 0:
                    for l in range(2):
                        p0 = 2 * (2 * r + l)
                        for s, src in enumerate((BE, kT)):
                            for pp in range(2):
                                k = (2 * s + pp) * P
                                ins = pe.transpose(psum[l][:, k:k + P], src[:, p0 + pp, 0:P], ident[:, :])
                        ins.then_inc(keys_turned, 1)
                    for l in range(2):
                        p0 = 2 * (2 * r + l)
                        pe.wait_ge(keys_ready, 2 * r + l + 1)
                        for pp in range(2):
                            o = psum[2 + l][:, pp * P:(pp + 1) * P]
                            pe.matmul(o, PM[l][:, pp], SA[l][:, pp * P:(pp + 1) * P], start=(pp == 0), stop=False)
                            ins = pe.matmul(o, PM[l][:, 2 + pp], V[:, 0, (p0 + pp) * P:(p0 + pp + 1) * P],
                                            start=False, stop=(pp == 1))
                        ins.then_inc(state_prod, 1)
            pe.wait_ge(y_done, 2)
            turn("rwo", Y)
            for n in range(2):
                chunk("rwo", n, "token", ready=split_ready("rwo"))
            norm_turn("mlp0")
            mlp(0)
            norm_turn("kv")
            pe.wait_ge(turned_lo, SPLIT0[TI["attn"]])
            turn("attn", XN)
            chunk("fk", 0, "feature", ready=split_ready("kv"))
            chunk("fk", 1, "feature")
            pe.wait_ge(fox_in, 16 * 3)
            pe.wait_ge(turned_lo, SPLIT0[TI["fo"]])
            for part in (XH, XL):
                for k in range(KT):
                    ins = pe.matmul(psum[4][0:NH, 0:T], wf[:, k], part[:, k].bitcast(F32),
                                    start=(part is XH and k == 0), stop=(part is XL and k == KT - 1))
            ins.then_inc(f_prod, 1)
            chunk("fv", 0, "token")
            pe.wait_ge(f_z, 1)
            head_sums(1, fSQ)
            chunk("fv", 1, "token")
            head_spread(1, frn)
            chunk("fq", 0, "feature", 1)
            chunk("fq", 1, "feature", 1)
            pe.wait_ge(spread_read, 8)
            head_sums(2, fSQ)
            head_spread(2, frn)
            pe.wait_ge(spread_read, 12)
            pe.wait_ge(negc_ready, 1)
            attention(0, NH, HD, lambda h: fQ[:, h // 2], lambda h: fKP[:, h], True, fE, fPT, fV)
            pe.wait_ge(att_out, 4)
            turn("fo", fO)
            for n in range(2):
                chunk("fo", n, "token", ready=split_ready("fo"))
            norm_turn("mlp1")
            mlp(1)
            norm_turn("ret")
            for name in ("rq", "rk"):
                for n in range(2):
                    chunk(name, n, "feature", ready=split_ready("ret"))
            for name in ("rv", "rg"):
                for n in range(4):
                    chunk(name, n, "token")
            pe.wait_ge(acc_read["act"], READ_COUNT[CHUNK0["rg"] + 3][1])
            pe.wait_ge(rotated, 2 * RET_H)
            for h in range(RET_H + 1):
                if h < RET_H:
                    if h >= 2:
                        pe.wait_ge(decayed, h - 1)
                    for m in range(MT):
                        o = psum[h % 2][:, 0:T] if m == 0 else psum[h % 2][:, T:T + P]
                        for e in range(2):
                            ins = pe.matmul(o, rK[:, h, e, m * P:(m + 1) * P], rQ[:, h, e, m * P:T],
                                            start=(m == 0 and e == 0), stop=(m == 1 and e == 1))
                    ins.then_inc(scores, 1)
                g = h - 1
                if g >= 0:
                    pe.wait_ge(decayed, g + 1)
                    if g >= 2:
                        pe.wait_ge(ret_out, 2 * (g - 1))
                    v = rV[:, :, g * RET_DV:(g + 1) * RET_DV]
                    pt = rPT[:, g % 2]
                    b = 4 + (2 * g) % 4
                    pe.matmul(psum[b][:, :], pt[:, 0:P], v[:, 0], start=True, stop=True).then_inc(ret_prod, 1)
                    pe.matmul(psum[b + 1][:, :], pt[:, P:2 * P], v[:, 0], start=True, stop=False)
                    pe.matmul(psum[b + 1][:, :], pt[:, 2 * P:3 * P], v[:, 1], start=False, stop=True)\
                        .then_inc(ret_prod, 1)
            pe.wait_ge(ret_out, 8)
            turn("reo", rG)
            for n in range(2):
                chunk("reo", n, "token", kts=2 * KT, ready=split_ready("reo"))
            norm_turn("mlp2")
            mlp(2)
            norm_turn("moba")
            for name in ("mq", "mk"):
                for n in range(2):
                    chunk(name, n, "feature", ready=split_ready("moba"))
            for i, (name, src) in enumerate((("mq", mQ), ("mk", mK))):
                pe.wait_ge(acc_read["act"], READ_COUNT[CHUNK0[name] + 1][1])
                pe.wait_ge(moba_in, 16 * 4)
                for b in range(4):
                    if i:
                        pe.wait_ge(roped, b + 1)
                    for j in range(2):
                        ins = pe.matmul(psum[4 + b][0:ROPE, j * T:(j + 1) * T], mSWAP, src[:, 2 * b + j],
                                        start=(j == 0), stop=(j == 1))
                    ins.then_inc(rope_swapped, 1)
            for n in range(2):
                chunk("mv", n, "token")
            pe.wait_ge(acc_read["act"], READ_COUNT[CHUNK0["mv"] + 1][1])
            pe.wait_ge(roped, 8)
            attention(NH, MOBA_H, MOBA_D, lambda h: mQ[:, h], lambda h: mK[:, h], False, mE, mPT, mV)
            pe.wait_ge(att_out, 4 + 4)
            turn("mo", mO)
            for n in range(2):
                chunk("mo", n, "token", ready=split_ready("mo"))
            norm_turn("mlp3")
            mlp(3)


def pack(w):
    k, n = w.shape
    return w.reshape(k // 512, UK, P, n // UN, UN).transpose(3, 0, 2, 1, 4).reshape(-1, P, UK * UN)


def pack_mlp(w_in, w_out):
    up, down = pack(w_in), pack(w_out)
    units = [up[0], up[1]]
    for j in range(1, MLP_STEPS):
        units += [up[2 * j], up[2 * j + 1], down[j - 1], down[MLP_STEPS + j - 1]]
    units += [down[MLP_STEPS - 1], down[2 * MLP_STEPS - 1]]
    return np.stack(units)


def by_partition(w):
    return w.reshape(-1, P, w.shape[1]).transpose(1, 0, 2).reshape(P, -1)


def laid_out(i):
    f = {k: np.asarray(v) for k, v in i.items()}
    o = {"x": f["x"].reshape(MT, P, D).transpose(1, 0, 2)}
    per = {"rwkv_norm_g": f["rwkv_norm_g"][0], "w0": f["rwkv_w0"][0], "a0": f["rwkv_a0"][0],
           "k_k": f["rwkv_k_k"][0], "k_a": f["rwkv_k_a"][0], "r_k": f["rwkv_r_k"][0],
           "kv_norm_g": f["kv_norm_g"], "k_norm_g": f["k_norm_g"], "attn_norm_g": f["attn_norm_g"][0],
           "q_norm_g": f["q_norm_g"][0], "mlp_norm_g0": f["mlp_norm_g"][0], "mlp_norm_g1": f["mlp_norm_g"][1],
           "ln_mix_pre_0": f["ln_mix_pre_0_2"], "ln_mlp_pre_0": f["ln_mlp_pre_0_2"],
           "ln_mix_pre_1": f["ln_mix_pre_1_2"], "ln_mlp_pre_1": f["ln_mlp_pre_1_2"]}
    per |= {f"mu{m}": f["rwkv_mu"][0, m] for m in range(6)}
    o["vecs"] = np.stack([per[n].reshape(KT, P).T for n in VECS], 1).reshape(P, -1)
    rows = {"lnx_w": f["rwkv_lnx_w"][0], "lnx_b": f["rwkv_lnx_b"][0]}
    rows |= {n: f[n + "_2"] for n in ROWS[2:]}
    o |= {n: rows[n].reshape(1, D) for n in ROWS}
    o["w1"], o["a1"], o["g1"] = (by_partition(f[n][0]) for n in ("rwkv_w1", "rwkv_a1", "rwkv_g1"))
    o["w2"], o["a2"] = f["rwkv_w2"][0], f["rwkv_a2"][0]
    o["g2a"], o["g2b"] = f["rwkv_g2"][0, :P], f["rwkv_g2"][0, P:]
    o["wf"] = by_partition(f["kv_w"][:, 2 * D:])
    o["f_bias"] = f["kv_f_bias"].reshape(NH, 1)
    cols = np.arange(D).reshape(RET_H, P, 2).transpose(0, 2, 1).reshape(-1)
    ret, mo = f["w_in_0_2"], f["w_in_1_2"]
    w = {"r": f["rwkv_w_rkv"][0, 0], "k": f["rwkv_w_rkv"][0, 1], "v": f["rwkv_w_rkv"][0, 2],
         "rwo": f["rwkv_w_o"][0], "fk": f["kv_w"][:, :D], "fv": f["kv_w"][:, D:2 * D],
         "fq": f["attn_w_q"][0], "fo": f["attn_w_o"][0],
         "rq": ret[:, :D][:, cols], "rk": ret[:, D:2 * D][:, cols], "rv": ret[:, 2 * D:4 * D], "rg": ret[:, 4 * D:],
         "reo": f["w_out_0_2"], "mq": mo[:, :D], "mk": mo[:, D:2 * D], "mv": mo[:, 2 * D:], "mo": f["w_out_1_2"]}
    o |= {"w_" + n: pack(m) for n, m in w.items()}
    o["w_mlp0"] = pack_mlp(f["mlp_w_in"][0], f["mlp_w_out"][0])
    o["w_mlp1"] = pack_mlp(f["mlp_w_in"][1], f["mlp_w_out"][1])
    o["w_mlp2"] = pack_mlp(f["w_up_0_2"], f["w_down_0_2"])
    o["w_mlp3"] = pack_mlp(f["w_up_1_2"], f["w_down_1_2"])
    o |= constants()
    return {k: np.ascontiguousarray(v) for k, v in o.items()}


def kernel(**inputs):
    import concourse.bacc as bacc
    from concourse.bass_utils import run_bass_kernel_spmd

    nc = bacc.Bacc("TRN2", target_bir_lowering=False, num_devices=1)
    arrays = {f"in_{k}": v for k, v in laid_out(inputs).items()}
    a = {k[3:]: nc.dram_tensor(k, v.shape, mybir.dt.from_np(v.dtype), kind="ExternalInput").ap()
         for k, v in arrays.items()}
    out = nc.dram_tensor("out", (1, T, D), F32, kind="ExternalOutput").ap()
    build(nc, a, out)
    return run_bass_kernel_spmd(nc, [arrays], core_ids=[0]).results[0]["out"]
```

```python
from contextlib import ExitStack

import numpy as np

import concourse.bass as bass
from concourse import mybir

F32 = mybir.dt.float32
F32R = mybir.dt.float32r
ACT = mybir.ActivationFunctionType
ALU = mybir.AluOpType
AXX = mybir.AxisListType.X

P = 128
D = 1024
T = 256
FF = 4096
MT = T // P
KT = D // P
RAW_RING, SPLIT_RING = 4, 2
UK, UN = 4, 512
NH = 16
HD = 64
LORA, GATE = 64, 160
RET_H, RET_DV = 4, 512
MOBA_H, MOBA_D = 8, 128
ROPE = 32
NORM_EPS, GN_EPS = 1e-6, 64e-5
NEG = -1e30

GEMMS = [("k", 8, 2), ("v", 8, 2), ("r", 8, 2), ("rwo", 8, 2), ("mlp0", 0, 0),
         ("fk", 8, 2), ("fv", 8, 2), ("fq", 8, 2), ("fo", 8, 2), ("mlp1", 0, 0),
         ("rq", 8, 2), ("rk", 8, 2), ("rv", 8, 4), ("rg", 8, 4), ("reo", 16, 2), ("mlp2", 0, 0),
         ("mq", 8, 2), ("mk", 8, 2), ("mv", 8, 2), ("mo", 8, 2), ("mlp3", 0, 0)]
READER = {"r": "act", "k": "act", "v": "act", "rwo": "sum", "fk": "act", "fv": "act", "fq": "act",
          "fo": "sum", "rq": "dve", "rk": "dve", "rv": "act", "rg": "act", "reo": "sum",
          "mq": "act", "mk": "act", "mv": "act", "mo": "sum"}
MLP_STEPS = FF // UN
MLP_UNITS = 4 * MLP_STEPS


def plan():
    u0, chunk0, u, g = {}, {}, 0, 0
    readers = []
    for name, kt, nn in GEMMS:
        u0[name], chunk0[name] = u, g
        if kt == 0:
            u += MLP_UNITS
            continue
        readers += [READER[name]] * nn
        u += nn * kt // UK
        g += nn
    read_count, counts = [], {"act": 0, "dve": 0, "sum": 0}
    for r in readers:
        counts[r] += 2
        read_count.append((r, counts[r]))
    return u0, chunk0, read_count, u


U0, CHUNK0, READ_COUNT, UNITS = plan()

VECS = ["rwkv_norm_g", "mu0", "mu1", "mu2", "mu3", "mu4", "mu5", "w0", "a0", "k_k", "k_a", "r_k",
        "kv_norm_g", "k_norm_g", "attn_norm_g", "q_norm_g", "mlp_norm_g0", "mlp_norm_g1",
        "ln_mix_pre_0", "ln_mlp_pre_0", "ln_mix_pre_1", "ln_mlp_pre_1"]
ROWS = ["lnx_w", "lnx_b", "ln_mix_post_0", "ln_mlp_post_0", "ln_mix_post_1", "ln_mlp_post_1"]

TURNS = [("rwkv", "rwkv_norm_g", 8, True, 0), ("rwo", None, 8, False, 0), ("mlp0", "mlp_norm_g0", 8, True, 0),
         ("kv", "kv_norm_g", 8, True, 0), ("attn", "attn_norm_g", 8, False, 1), ("fo", None, 8, False, 0),
         ("mlp1", "mlp_norm_g1", 8, True, 0), ("ret", "ln_mix_pre_0", 8, True, 0), ("reo", None, 16, False, 0),
         ("mlp2", "ln_mlp_pre_0", 8, True, 0), ("moba", "ln_mix_pre_1", 8, True, 0), ("mo", None, 8, False, 0),
         ("mlp3", "ln_mlp_pre_1", 8, True, 0)]
TI = {t[0]: i for i, t in enumerate(TURNS)}


def turn_counts():
    turned, split, normed, b, s, n = [], [], [], 0, 0, 0
    for name, _, kt, norm, _ in TURNS:
        turned.append(b)
        split.append(s)
        normed.append(n)
        b += kt // 2
        s += kt // 2 if name != "rwkv" else 0
        n += 1 if norm else 0
    return turned, split, normed


TURNED0, SPLIT0, NORM0 = turn_counts()
RESIDUALS = {"rwkv": 0, "mlp0": 4, "kv": 8, "mlp1": 12, "ret": 16, "mlp2": 20, "moba": 24, "mlp3": 28}


RESIDUALS_AFTER_POST = [20, 24, 28, 32]


def constants():
    f = np.float32
    i = np.arange(P)
    c = {"ident": np.eye(P, dtype=f)}
    strict = (i[:, None] < i[None, :]).astype(f)
    incl = (i[:, None] <= i[None, :]).astype(f)
    c["pair_masks"] = np.concatenate([strict, incl, strict, incl], 1)
    lm = []
    for m in (1, 2, 4, 8, 16, 32, 64):
        b = i // m
        lm.append(((b[:, None] % 2 == 1) & (b[None, :] == b[:, None] - 1)).astype(f))
    c["first_mask"] = -lm[0].T
    c["level_masks"] = np.concatenate(lm[1:], 1)
    c["head_window"] = np.zeros((P, 142), f)
    c["head_window"][i, 14 + i // HD] = 1.0
    c["head_spread"] = (i[:, None] == np.arange(D)[None, :] // HD).astype(f)
    c["head_blocks"] = (i[:, None] // HD == i[None, :] // HD).astype(f)
    c["head_halves"] = np.stack([(i // HD == 0), (i // HD == 1)], 1).astype(f)
    causal = np.where(i[:, None] >= i[None, :], 0.0, NEG).astype(f)
    c["causal"] = np.concatenate([causal, np.zeros((P, P), f), causal], 1)
    h = np.arange(RET_H, dtype=f)
    lg = np.log(1.0 - 2.0 ** (-5.0 - h.astype(np.float64)))
    t = np.arange(T)
    diff = t[None, None, :] - i[:, None, None]
    dec = np.where(diff >= 0, np.exp(lg[None, :, None] * np.maximum(diff, 0)) / 16.0, 0.0)
    c["ret_decay"] = dec.reshape(P, RET_H * T).astype(f)
    freq = (1.0 / (f(10000.0) ** np.linspace(0.0, 1.0, P, dtype=f))).astype(f)
    ang = (np.arange(T, dtype=f)[None, :] * freq[:, None]).astype(f).astype(np.float64)
    c["ret_cos"], c["ret_sin"] = np.cos(ang).astype(f), np.sin(ang).astype(f)
    inv = (f(500000.0) ** (-np.arange(0, ROPE, 2, dtype=f) / f(ROPE))).astype(f)
    a2 = (np.arange(T, dtype=f)[None, :] * inv[:, None]).astype(f).astype(np.float64)
    c["rope_cos"] = np.concatenate([np.cos(a2), np.cos(a2)], 0).astype(f)
    c["rope_sin"] = np.concatenate([-np.sin(a2), np.sin(a2)], 0).astype(f)
    perm = np.zeros((P, ROPE), f)
    j = np.arange(ROPE)
    perm[(j + ROPE // 2) % ROPE, j] = 1.0
    c["rope_swap"] = perm
    return c


CONST_KEEP = ["ident", "pair_masks", "first_mask", "level_masks", "head_window", "head_blocks", "head_halves", "causal"]
CONST_RET = ["ret_decay", "ret_cos", "ret_sin"]
CONST_ROPE = ["rope_cos", "rope_sin", "rope_swap"]


def build(nc, a, out):
    with ExitStack() as ctx:
        def sb(name, shape, dt=F32):
            return ctx.enter_context(nc.sbuf_tensor(name, shape, dt))

        def sem(name):
            return ctx.enter_context(nc.semaphore(name))

        X = sb("X", [P, MT, D])
        raw = sb("raw", [P, RAW_RING, UK, UN])
        whi = sb("whi", [P, SPLIT_RING, UK, UN], F32R)
        wlo = sb("wlo", [P, SPLIT_RING, UK, UN], F32R)
        XH = sb("XH", [P, 2 * KT, T], F32R)
        XL = sb("XL", [P, 2 * KT, T], F32R)
        vecs = sb("vecs", [P, len(VECS), KT])
        keep = {n: sb(f"c_{n}", list(a[n].shape)) for n in CONST_KEEP if n != "causal"}
        ident = keep["ident"]
        small = sb("small", [P, 128])
        att_nmax = sb("att_nmax", [P, 4, MT])
        att_sum = sb("att_sum", [P, NH, MT])
        ret_sums = sb("ret_sums", [P, RET_H * MT])
        NA = 24320
        arena = sb("arena", [P, NA])
        psum = [ctx.enter_context(nc.psum_tensor(f"bank{i}", [P, 512], F32)) for i in range(8)]

        def at(off, *dims):
            n = int(np.prod(dims))
            assert off + n <= NA, (off, dims)
            v = arena[:, off:off + n]
            names = "abcd"[:len(dims)]
            if len(dims) == 1:
                return v
            return v.rearrange(f"p ({' '.join(names)}) -> p {' '.join(names)}", **dict(zip(names, dims)))

        def gain(name, k):
            i = VECS.index(name)
            return vecs[:, i, k:k + 1]

        def bank_kt(b):
            return psum[b][:, :].rearrange("p (a t) -> p a t", a=2)

        norm_ss = small[:, 18:22].rearrange("p (m n) -> p m n", m=2)
        norm_ms, norm_rstd = small[:, 2:4], small[:, 4:6]
        norm_sd = small[:, 6:8]
        post_ss = small[:, 8:12].rearrange("p (m n) -> p m n", m=2)
        post_ms, post_sd, post_rstd = small[:, 12:14], small[:, 14:16], small[:, 16:18]
        eps_col = small[:, 22:23]
        bonus = small[:, 32:64]
        state_scale = small[:, 64:72]
        gn_mean, gn_var = small[:, 72:80], small[:, 88:96]

        XN, JUNK = at(4096, MT, D), at(6144, 2, UN)
        RELU = at(8240, MT, UN)
        hT, xxT = at(0, KT, T), at(2048, KT, T)
        XM = [at(6144, KT, T), at(4096, KT, T)]
        w1s, a1s, g1s = at(8192, KT, LORA), at(8704, KT, LORA), at(9216, KT, GATE)
        w2s, a2s, g2a, g2b = at(10496, D), at(11520, D), at(12544, D), at(13568, D)
        rT, kT, V, G = at(14592, KT, T), at(16640, KT, T), at(18688, MT, D), at(20736, MT, D)
        tw, ta, sga, sgb = at(22784, T), at(23040, T), at(23296, T), at(23552, T)
        sT, aT, lwT = at(0, KT, T), at(2080, KT, T), at(4128, KT, T)
        LW = P + 1
        Lx = at(6176, KT * 2, LW)
        E1, E2 = at(8240, KT * 2, LW), at(0, KT * 2, LW)
        kkT, sqT, rn = at(10496, KT, T), at(12544, KT, T), at(22784, T)
        AR = at(4128, KT * 2, 2, P)
        BE = aT
        Y = at(0, MT, D)
        M = [at(8240 + 2048 * l, 4, 512) for l in range(2)]
        TI_ = [at(12336 + 512 * l, 4, P) for l in range(2)]
        TT_ = [at(13360 + 512 * l, 4, P) for l in range(2)]
        PM = [at(14384 + 512 * l, 4, P) for l in range(2)]
        PADS = [[at(1024, 2, 4, P), at(15408, 2, 4, P)],
                [raw[:, 2].rearrange("p (a s) (h t) -> p a s h t", a=2, h=4)[:, 1], at(15408, 2, 4, P)]]
        KKSQ = at(14592, KT, T)
        SA = [at(22784 + 256 * l, 256) for l in range(2)]
        S0 = at(23296, KT, P)
        BONUS = raw[:, 2].rearrange("p k (a t) -> p (k a) t", a=2)
        YQ = raw[:, 2, 0]
        LNROW = raw[:, 3].rearrange("p (i k) n -> p i (k n)", i=2)
        ones, mids = at(24064, P), small[:, 104:120].unsqueeze(2)
        SPREAD = at(23040, KT, P)
        fK, fKP, fV, fQ = at(0, KT, T), at(8240, NH, T), at(12336, MT, D), at(14384, KT, T)
        fSQ, negc, frn = at(16432, KT, T), at(18480, T), at(18736, T)
        wf, fz, fl = at(18992, KT, NH), at(19120, T), at(19376, T)
        fc, fbias = at(19632, T), at(7600, 1)
        fL, fE, fPT = at(19888, 2, 384), at(20656, 2, 384), at(21424, 2, 384)
        fO, fCAUSAL = at(22192, MT, D), at(7200, 384)
        rDEC, rCOS, rSIN = at(0, RET_H, T), at(1024, T), at(1280, T)
        rQ, rK = at(1536, RET_H, 2, T), at(7168, RET_H, 2, T)
        rV, rG = at(9216, MT, 2 * D), at(13312, MT, 2 * D)
        rA, rB = [at(17408 + 512 * i, 2, T) for i in range(2)], [at(18432 + 512 * i, 2, T) for i in range(2)]
        rPT = at(19456, 2, 384)
        POST = at(20224, 2, D)
        PTMP = at(22272, 2, UN)
        mQ, mCOS, mSIN, mSWAP, mCAUSAL = at(0, KT, T), at(2048, T), at(2304, T), at(2560, ROPE), at(2592, 384)
        mTMP, mTMP2 = at(2976, 2, T), at(3488, 2, T)
        mK, mV = at(7168, KT, T), at(9216, MT, D)
        mL, mE, mPT = at(11264, 2, 384), at(12032, 2, 384), at(12800, 2, 384)
        mO = at(13568, MT, D)

        raw_landed = [sem(f"raw_landed{i}") for i in range(RAW_RING)]
        hi_done, lo_done, unit_used = sem("hi_done"), sem("lo_done"), sem("unit_used")
        acc_read = {"act": sem("acc_read_act"), "dve": sem("acc_read_dve")}
        spread_in = sem("spread_in")
        x_in = [sem(f"x_in{i}") for i in range(4)]
        ident_in, const_in, vecs_in, lora_in = sem("ident_in"), sem("const_in"), sem("vecs_in"), sem("lora_in")
        lnrow_in, fox_in, ret_in, moba_in = sem("lnrow_in"), sem("fox_in"), sem("ret_in"), sem("moba_in")
        post_in, out_done = sem("post_in"), sem("out_done")
        ss_done, ms_done, sd_done, rstd_done, xn_ready = (sem(n) for n in (
            "ss_done", "ms_done", "sd_done", "rstd_done", "xn_ready"))
        xn_act = sem("xn_act")
        turned, turned_hi, turned_lo, hT_ready = sem("turned"), sem("turned_hi"), sem("turned_lo"), sem("hT_ready")
        residual, eps_ready = sem("residual"), sem("eps_ready")
        pss_done, pms_done, psd_done, prstd_done, ptmp_done = (sem(n) for n in (
            "pss_done", "pms_done", "psd_done", "prstd_done", "ptmp_done"))
        relu_done, square_done, h_turned, h_hi, h_lo = (sem(n) for n in (
            "relu_done", "square_done", "h_turned", "h_hi", "h_lo"))
        dve_step, act_step, pool_step = sem("dve_step"), sem("act_step"), sem("pool_step")
        first_mixed, first_hi, first_lo, mixed, mix_hi, mix_lo, lora1, lora1_act, lora2, lora2_read = (sem(n) for n in (
            "first_mixed", "first_hi", "first_lo", "mixed", "mix_hi", "mix_lo", "lora1", "lora1_act", "lora2", "lora2_read"))
        lw_ready, centred, exps_ready, sq_ready, sums_ready, sums_ms, sums_sd, rn_ready, rn_spread, spread_read = (
            sem(n) for n in ("lw_ready", "centred", "exps_ready", "sq_ready", "sums_ready", "sums_ms", "sums_sd",
                             "rn_ready", "rn_spread", "spread_read"))
        bonus_prod, bonus_sum, bonus_read, prepared, rho_ready, scale_ready = (sem(n) for n in (
            "bonus_prod", "bonus_sum", "bonus_read", "prepared", "rho_ready", "scale_ready"))
        padded, pair_prod, pair_masked, first_ready, first_turned, inv_ready, half_prod, half_masked, step_prod, \
            rhs_prod, rhs_ready, sa_prod, sa_ready, y_prod, y_ready, keys_turned, keys_ready, state_prod, \
            state_ready = (sem(n) for n in (
                "padded", "pair_prod", "pair_masked", "first_ready", "first_turned", "inv_ready", "half_prod",
                "half_masked", "step_prod", "rhs_prod", "rhs_ready", "sa_prod", "sa_ready", "y_prod", "y_ready",
                "keys_turned", "keys_ready", "state_prod", "state_ready"))
        doubled = sem("doubled")
        y_centred, y_squared, gn_ms, gn_sd, y_done, gate_ready = (sem(n) for n in (
            "y_centred", "y_squared", "gn_ms", "gn_sd", "y_done", "gate_ready"))
        f_prod, f_z, f_abs, f_ln, negc_ready, zeroed = (sem(n) for n in (
            "f_prod", "f_z", "f_abs", "f_ln", "negc_ready", "zeroed"))
        logits, masked, maxed, expd, e_turned, pt_ready, av_prod, att_recip, att_out = (sem(n) for n in (
            "logits", "masked", "maxed", "expd", "e_turned", "pt_ready", "av_prod", "att_recip", "att_out"))
        rope_swapped, rope_cos, roped = sem("rope_swapped"), sem("rope_cos"), sem("roped")
        rotated, scores, decayed, ret_prod, ret_ss, ret_ms, ret_sd, ret_out = (sem(n) for n in (
            "rotated", "scores", "decayed", "ret_prod", "ret_ss", "ret_ms", "ret_sd", "ret_out"))

        block = ctx.enter_context(nc.Block())

        def raw_full(u):
            return 16 * (u // RAW_RING + 1)

        @block.sync
        def _(sp):
            sent = [0]

            def load_unit(name, u, row):
                if u >= RAW_RING:
                    sp.wait_ge(lo_done, u - RAW_RING + 1)
                sp.dma_start(raw[:, u % RAW_RING].rearrange("p k n -> p (k n)"), a["w_" + name][row])\
                    .then_inc(raw_landed[u % RAW_RING], 16)

            for q in range(4):
                m, f = q % 2, q // 2
                sp.dma_start(X[:, m, f * UN:(f + 1) * UN], a["x"][:, m, f * UN:(f + 1) * UN]).then_inc(x_in[q], 16)
            sp.dma_start(vecs[:, :, :].rearrange("p v k -> p (v k)"), a["vecs"]).then_inc(vecs_in, 16)
            sp.dma_start(ident[:, :], a["ident"]).then_inc(ident_in, 16)
            load_unit("k", 0, 0)
            load_unit("k", 1, 1)
            for n, dst in (("w1", w1s), ("a1", a1s), ("g1", g1s)):
                sp.dma_start(dst.rearrange("p k n -> p (k n)"), a[n]).then_inc(lora_in, 16)
            for n, dst, k in (("w2", w2s, LORA), ("a2", a2s, LORA), ("g2a", g2a, P), ("g2b", g2b, GATE - P)):
                sp.dma_start(dst[0:k, :], a[n]).then_inc(lora_in, 16)
            for n in CONST_KEEP[1:-1]:
                sp.dma_start(keep[n][:, :], a[n]).then_inc(const_in, 16)
            for name, kt, nn in GEMMS:
                if kt:
                    for i in range(nn * kt // UK):
                        u = U0[name] + i
                        if name == "rwo" and i == 2:
                            sp.wait_ge(gn_ms, 4)
                        if name == "rwo" and i == 3:
                            sp.wait_ge(gate_ready, 4)
                        if u >= 2:
                            load_unit(name, u, i)
                    continue
                b = U0[name]
                for i in range(2):
                    load_unit(name, b + i, i)
                with sp.Fori(1, MLP_STEPS) as j:
                    for i in range(UK):
                        slot = (i - 2) % RAW_RING
                        sp.wait_ge(lo_done, j * 4 + (b - 2 + i - RAW_RING + 1))
                        sp.dma_start(raw[:, slot].rearrange("p k n -> p (k n)"),
                                     a["w_" + name][bass.ds(j * 4 + (i - 2), 1)].rearrange("u p n -> (u p) n"))\
                            .then_inc(raw_landed[slot], 16)
                for i in range(MLP_UNITS - 2, MLP_UNITS):
                    load_unit(name, b + i, i)
            for i in range(4):
                m, h = i % 2, i // 2
                sp.wait_ge(residual, 28 + i + 1)
                sp.dma_start(out[0, m * P:(m + 1) * P, h * UN:(h + 1) * UN], X[:, m, h * UN:(h + 1) * UN])\
                    .then_inc(out_done, 16)
            sp.wait_ge(out_done, 64)

        @block.scalar
        def _(act):
            done = [0]
            steps = [0]

            def hi_unit(u):
                act.wait_ge(raw_landed[u % RAW_RING], raw_full(u))
                if u >= SPLIT_RING:
                    act.wait_ge(unit_used, u - SPLIT_RING + 1)
                act.activation(whi[:, u % SPLIT_RING], raw[:, u % RAW_RING], ACT.Copy).then_inc(hi_done, 1)

            def hi_upto(n):
                while done[0] < min(n, UNITS):
                    hi_unit(done[0])
                    done[0] += 1

            def norm(name):
                n = NORM0[TI[name]]
                for q in range(4):
                    if RESIDUALS[name]:
                        act.wait_ge(residual, RESIDUALS[name] - 3 + q)
                    else:
                        act.wait_ge(x_in[q], 16)
                    if q >= 2:
                        act.wait_ge(ss_done, 4 * n + q - 1)
                    m, f = q % 2, q // 2
                    act.activation(JUNK[:, m], X[:, m, f * UN:(f + 1) * UN], ACT.Square,
                                   accum_out=norm_ss[:, m, f:f + 1]).then_inc(ss_done, 1)
                act.wait_ge(ms_done, n + 1)
                act.activation(norm_sd, norm_ms, ACT.Sqrt, scale=1.0 / D, bias=eps_col).then_inc(sd_done, 1)
                act.wait_ge(rstd_done, n + 1)
                act.activation(XN[:, 1], X[:, 1], ACT.Copy, scale=norm_rstd[:, 1:2]).then_inc(xn_act, 1)

            def turn_hi(name, banks=None):
                i = TI[name]
                _, g, kt, _, half = TURNS[i]
                for b in banks or range(kt // 2):
                    act.wait_ge(turned, TURNED0[i] + b + 1)
                    src = bank_kt(4 + b % 4)
                    if g is None:
                        act.activation(XH[:, half * KT + 2 * b:half * KT + 2 * b + 2], src, ACT.Copy)\
                            .then_inc(turned_hi, 1)
                        continue
                    for j in range(2):
                        k = 2 * b + j
                        ins = act.activation(XH[:, half * KT + k], src[:, j], ACT.Copy, scale=gain(g, k))
                    ins.then_inc(turned_hi, 1)

            def read_chunk(name, n, put):
                g, kt = CHUNK0[name] + n, dict((q[0], q[1]) for q in GEMMS)[name]
                ue = U0[name] + (n + 1) * kt // UK
                hi_upto(ue + 1)
                act.wait_ge(unit_used, ue)
                for j in range(2):
                    put(n, j, psum[(g % 2) * 2 + j]).then_inc(acc_read["act"], 1)

            def by_feature(dst):
                return lambda n, j, b: act.activation(
                    dst[:, 4 * n + 2 * j:4 * n + 2 * j + 2], b[:, :].rearrange("p (a t) -> p a t", a=2), ACT.Copy)

            def by_token(dst, func=ACT.Copy):
                return lambda n, j, b: act.activation(dst[:, j, n * UN:(n + 1) * UN], b[:, :], func)

            def mlp(i):
                b, name = U0[f"mlp{i}"], f"mlp{i}"
                s0 = MLP_STEPS * i

                def relu(bank):
                    for m in range(MT):
                        act.activation(RELU[:, m], psum[bank + m][:, :], ACT.Relu).then_inc(relu_done, 1)

                def hidden_hi(q, k0=KT):
                    for k in range(2):
                        act.wait_ge(h_turned, 2 * q + k + 1)
                        act.activation(XH[:, k0 + 2 * k:k0 + 2 * k + 2], bank_kt(6 + k), ACT.Copy).then_inc(h_hi, 1)

                hi_upto(b + 3)
                act.wait_ge(unit_used, b + 2)
                relu(2)
                with act.Fori(1, MLP_STEPS) as j:
                    for n in range(1, UK + 1):
                        slot = (n - 2) % RAW_RING
                        act.wait_ge(raw_landed[slot], (j + (b // RAW_RING + (1 if n >= 2 else 0))) * 16)
                        act.wait_ge(unit_used, j * 4 + (b - 2 + n - SPLIT_RING + 1))
                        act.activation(whi[:, slot % SPLIT_RING], raw[:, slot], ACT.Copy).then_inc(hi_done, 1)
                        if n == 1:
                            hidden_hi(j + (s0 - 1))
                        if n == 3:
                            act.wait_ge(unit_used, j * 4 + b)
                            relu(0)
                done[0] = b + MLP_UNITS - 1
                hidden_hi(s0 + MLP_STEPS - 1, KT + 4)
                hi_upto(b + MLP_UNITS)

            def post_norm(i, u_of, bank0):
                for n in range(2):
                    hi_upto(u_of(n) + 1)
                    act.wait_ge(unit_used, u_of(n))
                    for m in range(MT):
                        if n:
                            act.wait_ge(pss_done, 4 * i + m + 1)
                        act.activation(JUNK[:, m], psum[bank0 + 2 * n + m][:, :], ACT.Square,
                                       accum_out=post_ss[:, m, n:n + 1]).then_inc(pss_done, 1)
                act.wait_ge(pms_done, i + 1)
                act.activation(post_sd, post_ms, ACT.Sqrt, scale=1.0 / D, bias=eps_col).then_inc(psd_done, 1)

            PJUNK = JUNK[:, 0]

            def head_squares(i, src):
                act.activation(KKSQ if i == 0 else fSQ, src, ACT.Square).then_inc(sq_ready, 1)

            def head_roots(i):
                act.wait_ge(sums_ms, i + 1)
                r = rn if i == 0 else frn
                act.activation(r, r, ACT.Sqrt).then_inc(sums_sd, 1)

            def attention(a0, heads, scale, L, E, PT):
                for h in range(heads + 1):
                    if h < heads:
                        act.wait_ge(maxed, a0 + h + 1)
                        if h >= 2:
                            act.wait_ge(e_turned, a0 + h - 1)
                        for m in range(MT):
                            c0, c1 = (0, P) if m == 0 else (P, 3 * P)
                            ins = act.activation(E[:, h % 2, c0:c1], L[:, h % 2, c0:c1], ACT.Exp,
                                                 bias=att_nmax[:, h % 4, m:m + 1],
                                                 accum_out=att_sum[:, h % 16, m:m + 1])
                        ins.then_inc(expd, 1)
                    if h >= 1:
                        g = h - 1
                        act.wait_ge(e_turned, a0 + g + 1)
                        if g >= 2:
                            act.wait_ge(av_prod, a0 + g - 1)
                        act.activation(PT[:, g % 2], psum[2 + g % 2][:, 0:384], ACT.Copy).then_inc(pt_ready, 1)

            act.wait_ge(vecs_in, 16)
            act.wait_ge(eps_ready, 1)
            norm("rwkv")
            hi_upto(1)
            for b in range(4):
                act.wait_ge(turned, b + 1)
                for j in range(2):
                    k = 2 * b + j
                    ins = act.activation(hT[:, k], bank_kt(4 + b)[:, j], ACT.Copy, scale=gain("rwkv_norm_g", k))
                ins.then_inc(hT_ready, 1)
            for b in range(4):
                if b == 2:
                    hi_upto(2)
                act.wait_ge(first_mixed, b + 1)
                act.activation(XH[:, 2 * b:2 * b + 2], XM[0][:, 2 * b:2 * b + 2], ACT.Copy).then_inc(first_hi, 1)

            def mix_to_hi(order, half):
                act.wait_ge(mixed, order)
                act.activation(XH[:, half * KT:(half + 1) * KT], XM[order % 2], ACT.Copy).then_inc(mix_hi, 1)

            hi_upto(3)
            mix_to_hi(2, 1)
            read_chunk("k", 0, by_feature(kT))
            act.wait_ge(lora1, 1)
            act.activation(tw[0:LORA, :], psum[4][0:LORA, 0:T], ACT.Tanh).then_inc(lora1_act, 1)
            read_chunk("k", 1, by_feature(kT))
            mix_to_hi(4, 0)
            act.wait_ge(lora1, 2)
            act.activation(ta[0:LORA, :], psum[5][0:LORA, 0:T], ACT.Copy).then_inc(lora1_act, 1)
            read_chunk("v", 0, by_token(V))
            act.wait_ge(lora1, 3)
            act.activation(sga, psum[6][:, 0:T], ACT.Sigmoid).then_inc(lora1_act, 1)
            act.activation(sgb[0:GATE - P, :], psum[7][0:GATE - P, 0:T], ACT.Sigmoid).then_inc(lora1_act, 1)
            hi_upto(U0["v"] + 4)
            for q, (dst, bias) in enumerate(((sT, "w0"), (aT, "a0"))):
                for b in range(4):
                    act.wait_ge(lora2, 4 * q + b + 1)
                    for j in range(2):
                        ins = act.activation(dst[:, 2 * b + j], bank_kt(4 + b)[:, j], ACT.Sigmoid,
                                             bias=gain(bias, 2 * b + j))
                    ins.then_inc(lora2_read, 1)
                if q == 0:
                    act.wait_ge(lora2_read, 4)
                    act.wait_ge(mix_lo, 2)
                    act.activation(lwT, sT, ACT.Copy, scale=-float(np.exp(-0.5))).then_inc(lw_ready, 1)
            hi_upto(U0["r"] + 1)
            act.wait_ge(centred, 1)
            act.activation(E1, Lx, ACT.Exp).then_inc(exps_ready, 1)
            act.activation(E2, Lx, ACT.Exp, scale=-1.0).then_inc(exps_ready, 1)
            act.activation(state_scale, state_scale, ACT.Exp).then_inc(scale_ready, 1)
            act.wait_ge(prepared, 1)
            head_squares(0, kkT)
            read_chunk("v", 1, by_token(V))
            for b in range(4):
                act.wait_ge(lora2, 8 + b + 1)
                act.activation(G[:, b // 2, (b % 2) * UN:(b % 2 + 1) * UN], psum[4 + b][:, :], ACT.Copy)\
                    .then_inc(lora2_read, 1)
            hi_upto(U0["r"] + 2)
            head_roots(0)
            read_chunk("r", 0, by_feature(rT))
            read_chunk("r", 1, by_feature(rT))
            hi_upto(U0["rwo"] + 2)

            def group_norm(r):
                act.wait_ge(y_centred, r + 1)
                act.activation(YQ, Y[:, r // 2, (r % 2) * UN:(r % 2 + 1) * UN], ACT.Square).then_inc(y_squared, 1)
                act.wait_ge(gn_ms, r + 1)
                act.activation(gn_var, gn_var, ACT.Sqrt).then_inc(gn_sd, 1)

            for r in range(4):
                c = r // 2
                for l in range(2):
                    gi = 2 * r + l
                    act.wait_ge(first_turned, gi + 1)
                    act.activation(TI_[l], psum[2 + l][:, :].rearrange("p (h s) -> p h s", h=4), ACT.Copy)\
                        .then_inc(inv_ready, 1)
                if r >= 1:
                    group_norm(r - 1)
                if r == 0:
                    act.wait_ge(bonus_sum, 1)
                    act.activation(bonus, psum[7][:, 0:32], ACT.Copy).then_inc(bonus_read, 1)
                for l in range(2):
                    act.wait_ge(rhs_prod, 2 * r + l + 1)
                    act.activation(SA[l], psum[6 + l][:, 0:256], ACT.Copy, scale=-1.0).then_inc(rhs_ready, 1)
                for l in range(2):
                    act.wait_ge(sa_prod, 2 * r + l + 1)
                    act.activation(SA[l], psum[6 + l][:, 0:256], ACT.Copy).then_inc(sa_ready, 1)
                for l in range(2):
                    q = (2 * r + l) % 4
                    act.wait_ge(y_prod, 2 * r + l + 1)
                    act.activation(Y[:, c, q * 256:(q + 1) * 256], psum[6 + l][:, 0:256], ACT.Copy)\
                        .then_inc(y_ready, 1)
                if c == 0:
                    for l in range(2):
                        act.wait_ge(keys_turned, 2 * r + l + 1)
                        act.activation(PM[l], psum[l][:, :].rearrange("p (h s) -> p h s", h=4), ACT.Copy)\
                            .then_inc(keys_ready, 1)
            turn_hi("rwo", (0, 1))
            group_norm(3)
            turn_hi("rwo", (2, 3))
            hi_upto(U0["rwo"] + 4 + 1)
            norm("mlp0")
            turn_hi("mlp0")
            mlp(0)
            hi_upto(U0["fk"] + 1)
            norm("kv")
            turn_hi("kv")
            turn_hi("attn")
            read_chunk("fk", 0, by_feature(fK))
            read_chunk("fk", 1, by_feature(fK))
            act.wait_ge(acc_read["act"], READ_COUNT[CHUNK0["fk"] + 1][1])
            head_squares(1, fK)
            read_chunk("fv", 0, by_token(fV))
            act.wait_ge(f_z, 1)
            act.activation(fl[0:NH, :], fz[0:NH, :], ACT.Abs).then_inc(f_abs, 1)
            act.wait_ge(f_abs, 1)
            act.activation(fl[0:NH, :], fl[0:NH, :], ACT.Exp, scale=-1.0).then_inc(f_abs, 1)
            act.wait_ge(f_abs, 2)
            act.activation(fl[0:NH, :], fl[0:NH, :], ACT.Ln, bias=1.0).then_inc(f_ln, 1)
            head_roots(1)
            read_chunk("fv", 1, by_token(fV))
            read_chunk("fq", 0, by_feature(fQ))
            read_chunk("fq", 1, by_feature(fQ))
            act.wait_ge(acc_read["act"], READ_COUNT[CHUNK0["fq"] + 1][1])
            act.wait_ge(sums_ready, 2)
            head_squares(2, fQ)
            head_roots(2)
            attention(0, NH, 1.0 / 8, fL, fE, fPT)
            hi_upto(U0["fo"] + 2)
            turn_hi("fo")
            hi_upto(U0["fo"] + 4 + 1)
            norm("mlp1")
            turn_hi("mlp1")
            mlp(1)
            hi_upto(U0["rq"] + 1)
            norm("ret")
            turn_hi("ret")
            hi_upto(U0["rv"])
            for n in range(4):
                read_chunk("rv", n, by_token(rV))
            for n in range(4):
                read_chunk("rg", n, by_token(rG, ACT.Silu))
            for h in range(RET_H):
                for m in range(MT):
                    act.wait_ge(ret_prod, 2 * h + m + 1)
                    act.activation(PJUNK, psum[4 + (2 * h + m) % 4][:, :], ACT.Square,
                                   accum_out=ret_sums[:, 2 * h + m:2 * h + m + 1]).then_inc(ret_ss, 1)
                    act.wait_ge(ret_ss, 2 * h + m + 1)
                act.wait_ge(ret_ms, h + 1)
                act.activation(ret_sums[:, 2 * h:2 * h + 2], ret_sums[:, 2 * h:2 * h + 2], ACT.Sqrt).then_inc(ret_sd, 1)
            hi_upto(U0["reo"] + 2)
            turn_hi("reo")
            post_norm(0, lambda n: U0["reo"] + 4 * (n + 1), 0)
            norm("mlp2")
            turn_hi("mlp2")
            mlp(2)
            post_norm(1, lambda n: U0["mlp2"] + MLP_UNITS - 1 + n, 2)
            norm("moba")
            turn_hi("moba")
            read_chunk("mq", 0, by_feature(mQ))
            read_chunk("mq", 1, by_feature(mQ))
            read_chunk("mk", 0, by_feature(mK))
            read_chunk("mk", 1, by_feature(mK))
            read_chunk("mv", 0, by_token(mV))
            read_chunk("mv", 1, by_token(mV))
            attention(NH, MOBA_H, MOBA_D ** -0.5, mL, mE, mPT)
            hi_upto(U0["mo"] + 2)
            turn_hi("mo")
            post_norm(2, lambda n: U0["mo"] + 2 * (n + 1), 0)
            norm("mlp3")
            turn_hi("mlp3")
            mlp(3)
            post_norm(3, lambda n: U0["mlp3"] + MLP_UNITS - 1 + n, 2)

        @block.vector
        def _(dve):
            done = [0]
            steps = [0]

            def step(ins):
                steps[0] += 1
                ins.then_inc(dve_step, 1)
                dve.wait_ge(dve_step, steps[0])

            def lo_unit(u):
                dve.wait_ge(hi_done, u + 1)
                dve.tensor_tensor(wlo[:, u % SPLIT_RING], raw[:, u % RAW_RING],
                                  whi[:, u % SPLIT_RING].bitcast(F32), ALU.subtract).then_inc(lo_done, 1)

            def lo_upto(n):
                while done[0] < min(n, UNITS):
                    lo_unit(done[0])
                    done[0] += 1

            def norm(name):
                n = NORM0[TI[name]]
                dve.wait_ge(ss_done, 4 * (n + 1))
                dve.tensor_tensor(norm_ms, norm_ss[:, :, 0], norm_ss[:, :, 1], ALU.add).then_inc(ms_done, 1)
                dve.wait_ge(sd_done, n + 1)
                dve.reciprocal(norm_rstd, norm_sd).then_inc(rstd_done, 1)
                dve.wait_ge(rstd_done, n + 1)
                dve.tensor_scalar(XN[:, 0], X[:, 0], norm_rstd[:, 0:1], None, ALU.mult).then_inc(xn_ready, 1)

            def turn_lo(name, banks=None):
                i = TI[name]
                _, g, kt, _, half = TURNS[i]
                for b in banks or range(kt // 2):
                    dve.wait_ge(turned_hi, SPLIT0[i] + b + 1)
                    src = bank_kt(4 + b % 4)
                    k = half * KT + 2 * b
                    if g is None:
                        dve.tensor_tensor(XL[:, k:k + 2], src, XH[:, k:k + 2].bitcast(F32), ALU.subtract)\
                            .then_inc(turned_lo, 1)
                        continue
                    for j in range(2):
                        ins = dve.scalar_tensor_tensor(XL[:, k + j], src[:, j], gain(g, 2 * b + j),
                                                       XH[:, k + j].bitcast(F32), ALU.mult, ALU.subtract)
                    ins.then_inc(turned_lo, 1)

            def residual_chunks(name):
                for n in range(2):
                    g, kt = CHUNK0[name] + n, 8
                    ue = U0[name] + (n + 1) * kt // UK
                    lo_upto(ue + 1)
                    dve.wait_ge(unit_used, ue)
                    for m in range(MT):
                        x = X[:, m, n * UN:(n + 1) * UN]
                        dve.tensor_tensor(x, x, psum[(g % 2) * 2 + m][:, :], ALU.add).then_inc(residual, 1)

            def mlp(i, before, plain):
                b = U0[f"mlp{i}"]
                s0 = MLP_STEPS * i

                def hidden_lo(q, k0=KT):
                    for k in range(2):
                        dve.wait_ge(h_hi, 2 * q + k + 1)
                        s = slice(k0 + 2 * k, k0 + 2 * k + 2)
                        dve.tensor_tensor(XL[:, s], bank_kt(6 + k), XH[:, s].bitcast(F32), ALU.subtract)\
                            .then_inc(h_lo, 1)

                lo_upto(b + 2)
                with dve.Fori(1, MLP_STEPS) as j:
                    for n in range(UK):
                        slot = (n - 2) % RAW_RING
                        dve.wait_ge(hi_done, j * 4 + (b - 2 + n + 1))
                        dve.tensor_tensor(wlo[:, slot % SPLIT_RING], raw[:, slot],
                                          whi[:, slot % SPLIT_RING].bitcast(F32), ALU.subtract).then_inc(lo_done, 1)
                        if n == 1:
                            hidden_lo(j + (s0 - 1))
                done[0] = b + MLP_UNITS - 2
                lo_upto(b + MLP_UNITS - 1)
                hidden_lo(s0 + MLP_STEPS - 1, KT + 4)
                lo_upto(b + MLP_UNITS)
                if plain:
                    lo_upto(b + MLP_UNITS + 1)
                    for n in range(2):
                        dve.wait_ge(unit_used, b + MLP_UNITS - 1 + n)
                        for m in range(MT):
                            x = X[:, m, n * UN:(n + 1) * UN]
                            dve.tensor_tensor(x, x, psum[2 + 2 * n + m][:, :], ALU.add).then_inc(residual, 1)

            def post_norm(i, ue, bank0, row):
                lo_upto(ue + 1)
                dve.wait_ge(pss_done, 4 * (i + 1))
                dve.tensor_tensor(post_ms, post_ss[:, :, 0], post_ss[:, :, 1], ALU.add).then_inc(pms_done, 1)
                dve.wait_ge(psd_done, i + 1)
                step(dve.reciprocal(post_rstd, post_sd))
                if i % 2 == 0:
                    dve.wait_ge(post_in, 16 * (i + 2))
                for n in range(2):
                    for m in range(MT):
                        ins = dve.scalar_tensor_tensor(PTMP[:, m], psum[bank0 + 2 * n + m][:, :],
                                                       post_rstd[:, m:m + 1], POST[:, row, n * UN:(n + 1) * UN],
                                                       ALU.mult, ALU.mult)
                    step(ins)
                    for m in range(MT):
                        x = X[:, m, n * UN:(n + 1) * UN]
                        dve.tensor_tensor(x, x, PTMP[:, m], ALU.add).then_inc(residual, 1)
                    dve.wait_ge(residual, RESIDUALS_AFTER_POST[i] - 2 + 2 * n)

            def head_sums(i, scale, eps):
                r = rn if i == 0 else frn
                dve.wait_ge(sums_ready, i + 1)
                dve.tensor_scalar(r, psum[4][:, 0:T], scale, eps, ALU.mult, ALU.add).then_inc(sums_ms, 1)
                dve.wait_ge(sums_sd, i + 1)
                if i == 0:
                    step(dve.tensor_scalar(r, r, 1e-12, None, ALU.max))
                dve.reciprocal(r, r).then_inc(rn_ready, 1)

            def attention(a0, heads, scale, L, CAUSAL, V_, dh, O):
                per = 512 // (MT * dh)
                for h in range(heads + 4):
                    if h < heads:
                        dve.wait_ge(logits, a0 + h + 1)
                        if h >= 2:
                            dve.wait_ge(expd, a0 + h - 1)
                        dve.scalar_tensor_tensor(L[:, h % 2], psum[h % 2][:, 0:384], scale, CAUSAL,
                                                 ALU.mult, ALU.add).then_inc(masked, 1)
                        dve.wait_ge(masked, a0 + h + 1)
                        for m in range(MT):
                            c0, c1 = (0, P) if m == 0 else (P, 3 * P)
                            ins = dve.tensor_reduce(att_nmax[:, h % 4, m:m + 1], L[:, h % 2, c0:c1], AXX, ALU.max,
                                                    negate=True)
                        ins.then_inc(maxed, 1)
                    g = h - 4
                    if g >= 0 and g % per == per - 1:
                        h0 = g - per + 1
                        dve.wait_ge(expd, a0 + g + 1)
                        s = att_sum[:, h0:g + 1]
                        step(dve.reciprocal(s, s))
                        dve.wait_ge(av_prod, a0 + g + 1)
                        src = psum[4 + (g // per) % 2][:, :].rearrange("p (h m d) -> p m h d", h=per, m=MT)
                        for m in range(MT):
                            ins = dve.tensor_tensor(
                                O[:, m, h0 * dh:(g + 1) * dh].rearrange("p (h d) -> p h d", h=per), src[:, m],
                                s[:, :, m:m + 1].broadcast_to((P, per, dh)), ALU.mult)
                        ins.then_inc(att_out, 1)

            dve.memset(eps_col, NORM_EPS).then_inc(eps_ready, 1)
            norm("rwkv")
            lo_upto(1)

            def mix_tiles(order, mu, ks):
                for k in ks:
                    ins = dve.scalar_tensor_tensor(XM[order % 2][:, k], xxT[:, k], gain(f"mu{mu}", k), hT[:, k],
                                                   ALU.mult, ALU.add)
                return ins

            def mix(order, mu):
                mix_tiles(order, mu, range(KT)).then_inc(mixed, 1)

            def mix_to_lo(j, order, half):
                dve.wait_ge(mix_hi, j)
                s = slice(half * KT, (half + 1) * KT)
                dve.tensor_tensor(XL[:, s], XM[order % 2], XH[:, s].bitcast(F32), ALU.subtract).then_inc(mix_lo, 1)

            def first_to_lo(b):
                dve.wait_ge(first_hi, b + 1)
                s = slice(2 * b, 2 * b + 2)
                dve.tensor_tensor(XL[:, s], XM[0][:, s], XH[:, s].bitcast(F32), ALU.subtract).then_inc(first_lo, 1)

            for b in range(4):
                s = slice(2 * b, 2 * b + 2)
                dve.wait_ge(hT_ready, b + 1)
                dve.tensor_tensor(xxT[:, s, 1:T], hT[:, s, 0:T - 1], hT[:, s, 1:T], ALU.subtract)
                step(dve.tensor_scalar(xxT[:, s, 0:1], hT[:, s, 0:1], -1.0, None, ALU.mult))
                mix_tiles(0, 2, range(2 * b, 2 * b + 2)).then_inc(first_mixed, 1)
                if b >= 1:
                    first_to_lo(b - 1)
            lo_upto(2)
            first_to_lo(3)
            mix(1, 1)
            lo_upto(3)
            dve.wait_ge(first_lo, 4)
            mix(2, 3)
            mix_to_lo(1, 2, 1)
            lo_upto(4)
            dve.wait_ge(lora1, 1)
            mix(3, 4)
            lo_upto(5)
            dve.wait_ge(mix_lo, 1)
            mix(4, 0)
            lo_upto(6)
            dve.wait_ge(lora1, 2)
            mix(5, 5)
            mix_to_lo(2, 4, 0)
            lo_upto(8)
            dve.wait_ge(mix_lo, 2)
            dve.wait_ge(lw_ready, 1)
            dve.memset(Lx[:, :, 0:1], 0.0)
            step(dve.memset(ones, 1.0))
            lw16 = lwT.rearrange("p k (c t) -> p (k c) t", c=2)
            for q in range(2 * KT):
                ins = dve.tensor_tensor_scan(Lx[:, q, 1:LW], ones, lw16[:, q], 0.0, ALU.mult, ALU.add)
            step(ins)
            Lc = Lx.rearrange("p (k c) t -> p k c t", c=2)
            step(dve.tensor_copy(mids, Lx[:, :, HD:HD + 1]))
            mid2 = mids.rearrange("p (k c) o -> p k (c o)", c=2)
            step(dve.tensor_tensor(state_scale, Lc[:, :, 0, P], mid2[:, :, 0], ALU.subtract))
            step(dve.tensor_tensor(state_scale, state_scale, mid2[:, :, 1], ALU.add))
            dve.tensor_tensor(Lx, Lx, mids.broadcast_to((P, 2 * KT, LW)), ALU.subtract).then_inc(centred, 1)
            dve.wait_ge(lora2, 8)
            for p in range(KT):
                ins = dve.tensor_scalar(kkT[:, p], kT[:, p], gain("k_k", p), None, ALU.mult)
            ins.then_inc(prepared, 1)
            lo_upto(9)
            dve.wait_ge(lora2_read, 8)
            dve.wait_ge(lora2, 12)
            for p in range(KT):
                ins = dve.tensor_scalar(sqT[:, p], aT[:, p], 1.0, gain("k_a", p), ALU.subtract, ALU.mult)
            step(ins)
            lo_upto(10)
            head_sums(0, 1.0, 0.0)
            step(dve.scalar_tensor_tensor(kT, sqT, 1.0, kT, ALU.add, ALU.mult))
            lo_upto(11)
            for b in range(4):
                dve.wait_ge(rn_spread, b + 1)
                k2 = kkT[:, 2 * b:2 * b + 2]
                ins = dve.tensor_tensor(k2, k2, bank_kt(4 + b), ALU.mult)
                ins.then_inc(spread_read, 1)
            dve.wait_ge(spread_read, 4)
            dve.wait_ge(exps_ready, 2)
            kk16 = kkT.rearrange("p k (c t) -> p (k c) t", c=2)
            r16 = rT.rearrange("p k (c t) -> p (k c) t", c=2)
            k16 = kT.rearrange("p k (c t) -> p (k c) t", c=2)
            b16 = BE.rearrange("p k (c t) -> p (k c) t", c=2)
            step(dve.tensor_tensor(aT, kkT, aT, ALU.mult))
            dve.tensor_tensor(b16, b16, E2[:, :, 1:LW], ALU.mult)
            lo_upto(12)
            dve.tensor_tensor(k16, k16, E2[:, :, 1:LW], ALU.mult).then_inc(prepared, 1)
            dve.tensor_tensor(AR[:, :, 0], kk16, E1[:, :, 0:P], ALU.mult)
            dve.wait_ge(acc_read["act"], READ_COUNT[CHUNK0["r"] + 1][1])
            dve.tensor_tensor(AR[:, :, 1], r16, E1[:, :, 1:LW], ALU.mult).then_inc(rho_ready, 1)
            dve.wait_ge(rho_ready, 1)
            for l in range(2):
                for blk in range(4):
                    ins = dve.memset(M[l][HD:P, :, blk * P:blk * P + HD], 0.0)
            step(ins)
            dve.wait_ge(scale_ready, 1)
            dve.wait_ge(const_in, 16 * (len(CONST_KEEP) - 2))
            first4 = keep["first_mask"][:, :].unsqueeze(1).broadcast_to((P, 4, P))
            ident4 = ident[:, :].unsqueeze(1).broadcast_to((P, 4, P))
            pm = keep["pair_masks"]

            def group_norm(r, part):
                y2 = Y[:, r // 2, (r % 2) * UN:(r % 2 + 1) * UN]
                y = y2.rearrange("p (h d) -> p h d", h=8)
                if part == 0:
                    dve.wait_ge(y_ready, 2 * r + 2)
                    step(dve.tensor_reduce(gn_mean, y, AXX, ALU.add))
                    step(dve.tensor_scalar(gn_mean, gn_mean, 1.0 / HD, None, ALU.mult))
                elif part == 1:
                    dve.tensor_tensor(y, y, gn_mean.unsqueeze(2).broadcast_to((P, 8, HD)), ALU.subtract)\
                        .then_inc(y_centred, 1)
                elif part == 2:
                    dve.wait_ge(y_squared, r + 1)
                    step(dve.tensor_reduce(gn_var, YQ.rearrange("p (h d) -> p h d", h=8), AXX, ALU.add))
                    dve.tensor_scalar(gn_var, gn_var, 1.0 / HD, GN_EPS, ALU.mult, ALU.add).then_inc(gn_ms, 1)
                elif part == 3:
                    dve.wait_ge(gn_sd, r + 1)
                    step(dve.reciprocal(gn_var, gn_var))
                    step(dve.tensor_tensor(y, y, gn_var.unsqueeze(2).broadcast_to((P, 8, HD)), ALU.mult))
                elif part == 4:
                    dve.wait_ge(gate_ready, r + 1)
                    step(dve.tensor_tensor(y2, y2, G[:, r // 2, (r % 2) * UN:(r % 2 + 1) * UN], ALU.mult))
                else:
                    dve.tensor_tensor(y2, y2, V[:, r // 2, (r % 2) * UN:(r % 2 + 1) * UN], ALU.add)\
                        .then_inc(y_done, 1)

            for r in range(4):
                c = r // 2
                for l in range(2):
                    gi = 2 * r + l
                    for h in range(4):
                        b = psum[4 * l + h]
                        dve.wait_ge(pair_prod, 4 * gi + h + 1)
                        dve.tensor_tensor(M[l][0:HD, h], b[0:HD, :], pm[0:HD, :], ALU.mult)
                        dve.tensor_tensor(M[l][HD:P, h].rearrange("p (b t) -> p b t", b=4)[:, :, HD:P],
                                          b[HD:P, :].rearrange("p (b t) -> p b t", b=4)[:, :, HD:P],
                                          pm[HD:P, :].rearrange("p (b t) -> p b t", b=4)[:, :, HD:P],
                                          ALU.mult).then_inc(pair_masked, 1)
                    dve.wait_ge(pair_masked, 4 * gi + 4)
                    step(dve.tensor_tensor(TT_[l], M[l][:, :, 0:P], first4, ALU.mult))
                    dve.tensor_tensor(TT_[l], TT_[l], ident4, ALU.add).then_inc(first_ready, 1)
                if r == 0:
                    lo_upto(U0["rwo"] + 2)
                for i in range(6):
                    lm = keep["level_masks"][:, i * P:(i + 1) * P].unsqueeze(1).broadcast_to((P, 4, P))
                    for l in range(2):
                        n = 12 * r + 2 * i + l
                        dve.wait_ge(half_prod, n + 1)
                        dve.tensor_tensor(PM[l], psum[l][:, :].rearrange("p (h s) -> p h s", h=4), lm, ALU.mult)\
                            .then_inc(half_masked, 1)
                    for l in range(2):
                        n = 12 * r + 2 * i + l
                        dve.wait_ge(step_prod, n + 1)
                        if i < 5:
                            dve.tensor_tensor(TI_[l], TI_[l], psum[2 + l][:, :].rearrange("p (h s) -> p h s", h=4),
                                              ALU.subtract)
                        dve.tensor_tensor(TT_[l], TT_[l], psum[4 + l][:, :].rearrange("p (h s) -> p h s", h=4),
                                          ALU.subtract).then_inc(doubled, 1)
                    if r >= 1:
                        group_norm(r - 1, i)
                    elif i == 0:
                        dve.wait_ge(prepared, 2)
                        dve.wait_ge(lo_done, U0["rwo"])
                        for p in range(KT):
                            ins = dve.scalar_tensor_tensor(BONUS[:, p].rearrange("p (c t) -> p c t", c=2),
                                                           AR[:, 2 * p:2 * p + 2, 1], gain("r_k", p),
                                                           k16[:, 2 * p:2 * p + 2], ALU.mult, ALU.mult)
                        ins.then_inc(bonus_prod, 1)
                if c == 0:
                    for l in range(2):
                        p0 = 2 * (2 * r + l)
                        dve.wait_ge(state_prod, 2 * r + l + 1)
                        for pp in range(2):
                            dve.scalar_tensor_tensor(S0[:, p0 + pp], psum[2 + l][:, pp * P:(pp + 1) * P],
                                                     state_scale[:, p0 + pp:p0 + pp + 1], keep["head_blocks"][:, :],
                                                     ALU.mult, ALU.mult).then_inc(state_ready, 1)
            for part in range(3):
                group_norm(3, part)
            turn_lo("rwo", (0, 1))
            for part in range(3, 6):
                group_norm(3, part)
            turn_lo("rwo", (2, 3))
            residual_chunks("rwo")
            norm("mlp0")
            turn_lo("mlp0")
            mlp(0, 4, True)
            norm("kv")
            turn_lo("kv")
            turn_lo("attn")
            lo_upto(U0["fv"] + 1)
            dve.wait_ge(f_prod, 1)
            dve.wait_ge(fox_in, 16 * 3)
            dve.tensor_scalar(fz[0:NH, :], psum[4][0:NH, 0:T], fbias[0:NH, :], None, ALU.add).then_inc(f_z, 1)
            lo_upto(U0["fv"] + 3)
            head_sums(1, 1.0 / HD, NORM_EPS)
            dve.wait_ge(f_ln, 1)
            step(dve.scalar_tensor_tensor(fz[0:NH, :], fz[0:NH, :], 0.0, fl[0:NH, :], ALU.min, ALU.subtract))
            step(dve.memset(fl, 1.0))
            step(dve.tensor_tensor_scan(fc[0:NH, :], fl[0:NH, :], fz[0:NH, :], 0.0, ALU.mult, ALU.add))
            dve.wait_ge(zeroed, 2)
            dve.tensor_scalar(negc[0:NH, :], fc[0:NH, :], -8.0, None, ALU.mult).then_inc(negc_ready, 1)
            lo_upto(U0["fq"] + 1)
            for b in range(4):
                dve.wait_ge(rn_spread, 4 + b + 1)
                for j in range(2):
                    p = 2 * b + j
                    for f in range(2):
                        s = slice(f * HD, (f + 1) * HD)
                        ins = dve.scalar_tensor_tensor(fKP[s, 2 * p + f], bank_kt(4 + b)[s, j],
                                                       gain("k_norm_g", p)[s], fK[s, p], ALU.mult, ALU.mult)
                ins.then_inc(spread_read, 1)
            lo_upto(U0["fo"] + 1)
            head_sums(2, 1.0 / HD, NORM_EPS)
            for b in range(4):
                dve.wait_ge(rn_spread, 8 + b + 1)
                for j in range(2):
                    p = 2 * b + j
                    ins = dve.scalar_tensor_tensor(fQ[:, p], bank_kt(4 + b)[:, j], gain("q_norm_g", p), fQ[:, p],
                                                   ALU.mult, ALU.mult)
                ins.then_inc(spread_read, 1)
            attention(0, NH, 1.0 / 8, fL, fCAUSAL, fV, HD, fO)
            lo_upto(U0["fo"] + 2)
            turn_lo("fo")
            residual_chunks("fo")
            norm("mlp1")
            turn_lo("mlp1")
            mlp(1, 12, True)
            norm("ret")
            turn_lo("ret")
            dve.wait_ge(ret_in, 16 * 3)
            cos2 = rCOS.unsqueeze(1).broadcast_to((P, 2, T))
            sin2 = rSIN.unsqueeze(1).broadcast_to((P, 2, T))
            for i, (name, dst) in enumerate((("rq", rQ), ("rk", rK))):
                for n in range(2):
                    g = CHUNK0[name] + n
                    ue = U0[name] + 2 * (n + 1)
                    lo_upto(ue + 1)
                    dve.wait_ge(unit_used, ue)
                    for j in range(2):
                        h, s = 2 * n + j, j
                        src = bank_kt((g % 2) * 2 + j)
                        dve.tensor_tensor(rA[s], src, cos2, ALU.mult)
                        ins = dve.tensor_tensor(rB[s], src, sin2, ALU.mult)
                        ins.then_inc(acc_read["dve"], 1)
                        dve.wait_ge(acc_read["dve"], READ_COUNT[g][1] - 1 + j)
                        dve.tensor_tensor(dst[:, h, 0], rA[s][:, 0], rB[s][:, 1], ALU.subtract)
                        dve.tensor_tensor(dst[:, h, 1], rB[s][:, 0], rA[s][:, 1], ALU.add).then_inc(rotated, 1)
            lo_upto(U0["reo"])
            for h in range(RET_H):
                dve.wait_ge(scores, h + 1)
                if h >= 2:
                    dve.wait_ge(ret_prod, 2 * (h - 1))
                d = rDEC[:, h]
                dve.tensor_tensor(rPT[:, h % 2, 0:T], psum[h % 2][:, 0:T], d, ALU.mult)
                dve.tensor_tensor(rPT[:, h % 2, T:T + P], psum[h % 2][:, T:T + P], d[:, 0:P], ALU.mult)\
                    .then_inc(decayed, 1)
                dve.wait_ge(ret_ss, 2 * h + 2)
                s = ret_sums[:, 2 * h:2 * h + 2]
                dve.tensor_scalar(s, s, 1.0 / RET_DV, NORM_EPS, ALU.mult, ALU.add).then_inc(ret_ms, 1)
                dve.wait_ge(ret_sd, h + 1)
                step(dve.reciprocal(s, s))
                if h == 0:
                    dve.wait_ge(acc_read["act"], READ_COUNT[CHUNK0["rg"] + 3][1])
                for m in range(MT):
                    gt = rG[:, m, h * RET_DV:(h + 1) * RET_DV]
                    dve.scalar_tensor_tensor(gt, psum[4 + (2 * h + m) % 4][:, :], s[:, m:m + 1], gt, ALU.mult,
                                             ALU.mult).then_inc(ret_out, 1)
            lo_upto(U0["reo"] + 2)
            turn_lo("reo")
            post_norm(0, U0["reo"] + 8, 0, 0)
            norm("mlp2")
            turn_lo("mlp2")
            mlp(2, 20, False)
            post_norm(1, U0["mlp2"] + MLP_UNITS, 2, 1)
            norm("moba")
            turn_lo("moba")
            dve.wait_ge(moba_in, 16 * 4)
            for i, (name, src) in enumerate((("mq", mQ), ("mk", mK))):
                lo_upto(U0["mk"] + 5)
                dve.wait_ge(acc_read["act"], READ_COUNT[CHUNK0[name] + 1][1])
                for b in range(4):
                    s = slice(2 * b, 2 * b + 2)
                    x = src[0:ROPE, s]
                    dve.wait_ge(rope_swapped, 4 * i + b + 1)
                    step(dve.tensor_tensor(mTMP[0:ROPE], bank_kt(4 + b)[0:ROPE],
                                           mSIN[0:ROPE].unsqueeze(1).broadcast_to((ROPE, 2, T)), ALU.mult))
                    step(dve.tensor_tensor(mTMP2[0:ROPE], x, mCOS[0:ROPE].unsqueeze(1).broadcast_to((ROPE, 2, T)),
                                           ALU.mult))
                    dve.tensor_tensor(x, mTMP[0:ROPE], mTMP2[0:ROPE], ALU.add).then_inc(roped, 1)
                    dve.wait_ge(roped, 4 * i + b + 1)
            lo_upto(U0["mo"] + 1)
            attention(NH, MOBA_H, MOBA_D ** -0.5, mL, mCAUSAL, mV, MOBA_D, mO)
            lo_upto(U0["mo"] + 2)
            turn_lo("mo")
            post_norm(2, U0["mo"] + 4, 0, 0)
            norm("mlp3")
            turn_lo("mlp3")
            mlp(3, 28, False)
            post_norm(3, U0["mlp3"] + MLP_UNITS, 2, 1)

        @block.gpsimd
        def _(pool):
            def squares(i):
                s0 = MLP_STEPS * i

                def one(q):
                    for m in range(MT):
                        pool.wait_ge(relu_done, 2 * q + m + 1)
                        pool.tensor_tensor(RELU[:, m], RELU[:, m], RELU[:, m], ALU.mult).then_inc(square_done, 1)

                with pool.Fori(0, MLP_STEPS) as j:
                    one(j + s0)

            pool.wait_ge(const_in, 16 * (len(CONST_KEEP) - 2))
            pool.wait_ge(lora2, 12)
            pool.dma_start(SPREAD.rearrange("p k f -> p (k f)"), a["head_spread"]).then_inc(spread_in, 16)
            pool.wait_ge(prepared, 2)
            def pads(gi):
                c, p0 = gi // 4, 2 * (gi % 4)
                if gi >= 2:
                    pool.wait_ge(pair_prod, 4 * (gi - 1))
                for s, src in enumerate((BE, kT)):
                    for f in range(2):
                        pool.tensor_scalar(PADS[c][gi % 2][:, s].rearrange("p (q f) t -> p f q t", f=2)[:, f],
                                           src[:, p0:p0 + 2, c * P:(c + 1) * P], keep["head_halves"][:, f:f + 1], 1.0,
                                           ALU.mult, ALU.mult).then_inc(padded, 1)

            def gate(r):
                c, cols, n = r // 2, slice((r % 2) * UN, (r % 2 + 1) * UN), 3 * r
                v, gt = V[:, c, cols], G[:, c, cols]
                v3 = v.rearrange("p (h d) -> p h d", h=8)
                bs = bonus[:, c * NH + (r % 2) * 8:c * NH + (r % 2) * 8 + 8]
                pool.wait_ge(y_prod, 2 * r + 2)
                if c == 0:
                    pool.wait_ge(state_prod, 2 * r + 2)
                pool.tensor_tensor(v3, v3, bs.unsqueeze(2).broadcast_to((P, 8, HD)), ALU.mult).then_inc(pool_step, 1)
                pool.wait_ge(pool_step, n + 1)
                pool.tensor_tensor(v, v, LNROW[:, 1, cols], ALU.add).then_inc(pool_step, 1)
                pool.wait_ge(pool_step, n + 2)
                pool.tensor_tensor(v, v, gt, ALU.mult).then_inc(pool_step, 1)
                pool.wait_ge(pool_step, n + 3)
                pool.tensor_tensor(gt, gt, LNROW[:, 0, cols], ALU.mult).then_inc(gate_ready, 1)

            pads(0)
            pool.wait_ge(rho_ready, 1)
            pads(1)
            pool.wait_ge(lo_done, U0["rwo"])
            for i in range(2):
                pool.dma_start(LNROW[:, i], a[ROWS[i]].partition_broadcast(P)).then_inc(lnrow_in, 16)
            pool.wait_ge(bonus_read, 1)
            pool.wait_ge(lnrow_in, 32)
            for r in range(4):
                if r < 3:
                    pads(2 * r + 2)
                    pads(2 * r + 3)
                gate(r)
            squares(0)
            pool.dma_start(wf.rearrange("p k n -> p (k n)"), a["wf"]).then_inc(fox_in, 16)
            pool.dma_start(fbias[0:NH, :], a["f_bias"]).then_inc(fox_in, 16)
            pool.dma_start(fCAUSAL, a["causal"]).then_inc(fox_in, 16)
            pool.dma_start(SPREAD.rearrange("p k f -> p (k f)"), a["head_spread"]).then_inc(spread_in, 16)
            pool.memset(negc, 0.0).then_inc(zeroed, 1)
            pool.wait_ge(h_lo, 2 * MLP_STEPS)
            pool.memset(fKP, 0.0).then_inc(zeroed, 1)
            squares(1)
            for n, dst in (("ret_decay", at(0, RET_H * T)), ("ret_cos", rCOS), ("ret_sin", rSIN)):
                pool.dma_start(dst, a[n]).then_inc(ret_in, 16)
            for i in range(2):
                pool.dma_start(POST[:, i], a[ROWS[2 + i]].partition_broadcast(P)).then_inc(post_in, 16)
            squares(2)
            for n, dst, k in (("rope_cos", mCOS, ROPE), ("rope_sin", mSIN, ROPE), ("rope_swap", mSWAP, P),
                              ("causal", mCAUSAL, P)):
                pool.dma_start(dst[0:k], a[n]).then_inc(moba_in, 16)
            pool.wait_ge(residual, 24)
            for i in range(2):
                pool.dma_start(POST[:, i], a[ROWS[4 + i]].partition_broadcast(P)).then_inc(post_in, 16)
            squares(3)

        @block.tensor
        def _(pe):
            def turn(name, src, banks=None):
                i = TI[name]
                kt = TURNS[i][2]
                for b in banks or range(kt // 2):
                    if b >= 4:
                        pe.wait_ge(turned_lo, SPLIT0[i] + b - 3)
                    for j in range(2):
                        for m in range(MT):
                            k = 2 * b + j
                            ins = pe.transpose(psum[4 + b % 4][:, j * T + m * P:j * T + (m + 1) * P],
                                               src[:, m, k * P:(k + 1) * P], ident[:, :])
                    ins.then_inc(turned, 1)

            def norm_turn(name):
                pe.wait_ge(xn_ready, NORM0[TI[name]] + 1)
                pe.wait_ge(xn_act, NORM0[TI[name]] + 1)
                turn(name, XN)

            def passes(out_, x, w, xs, ws, start, stop_=False):
                (xh, xl), (wh, wl) = x, w
                pe.matmul(out_, xh[xs], wh[ws], start=start, stop=False)
                pe.matmul(out_, xh[xs], wl[ws], start=False, stop=False)
                return pe.matmul(out_, xl[xs], wh[ws], start=False, stop=stop_)

            def chunk(name, n, form, half=0, kts=KT, ready=None):
                g = CHUNK0[name] + n
                if g >= 2 and READ_COUNT[g - 2][0] != "sum":
                    who, c = READ_COUNT[g - 2]
                    pe.wait_ge(acc_read[who], c)
                for kg in range(kts // UK):
                    u = U0[name] + n * (kts // UK) + kg
                    pe.wait_ge(lo_done, u + 1)
                    s = u % SPLIT_RING
                    for k in range(UK):
                        kt = kg * UK + k
                        if ready is not None and n == 0 and kt % 2 == 0:
                            ready(kt // 2)
                        first, last = kt == 0, kt == kts - 1
                        x = half * KT + kt
                        if form == "token":
                            for m in range(MT):
                                ins = passes(psum[(g % 2) * 2 + m][:, :], (XH, XL), (whi, wlo),
                                             (slice(None), x, slice(m * P, (m + 1) * P)),
                                             (slice(None), s, k), first, last)
                        else:
                            for f in range(UK):
                                o = psum[(g % 2) * 2 + f // 2][:, (f % 2) * T:(f % 2 + 1) * T]
                                ins = passes(o, (whi, wlo), (XH, XL),
                                             (slice(None), s, k, slice(f * P, (f + 1) * P)),
                                             (slice(None), x), first and f % 2 == 0, last and f % 2 == 1)
                    ins.then_inc(unit_used, 1)

            def split_ready(name):
                return lambda b: pe.wait_ge(turned_lo, SPLIT0[TI[name]] + b + 1)

            def mlp(i):
                b, name = U0[f"mlp{i}"], f"mlp{i}"
                s0 = MLP_STEPS * i

                def up(u, bank, kg, ready=False):
                    for k in range(UK):
                        kt = kg * UK + k
                        if ready and kt % 2 == 0:
                            pe.wait_ge(turned_lo, SPLIT0[TI[name]] + kt // 2 + 1)
                        for m in range(MT):
                            ins = passes(psum[bank + m][:, :], (XH, XL), (whi, wlo),
                                         (slice(None), kt, slice(m * P, (m + 1) * P)), (slice(None), u, k),
                                         kt == 0, kt == KT - 1)
                    ins.then_inc(unit_used, 1)

                def hidden_turn(q):
                    pe.wait_ge(square_done, q * 2 + 2)
                    for k in range(2):
                        for j in range(2):
                            for m in range(MT):
                                f = 2 * k + j
                                ins = pe.transpose(psum[6 + k][:, j * T + m * P:j * T + (m + 1) * P],
                                                   RELU[:, m, f * P:(f + 1) * P], ident[:, :])
                        ins.then_inc(h_turned, 1)

                def down(u, n, first, last, k0=KT):
                    for k in range(UK):
                        for m in range(MT):
                            ins = passes(psum[2 + 2 * n + m][:, :], (XH, XL), (whi, wlo),
                                         (slice(None), k0 + k, slice(m * P, (m + 1) * P)), (slice(None), u, k),
                                         first and k == 0, last and k == UK - 1)
                    ins.then_inc(unit_used, 1)

                for kg in range(2):
                    pe.wait_ge(lo_done, b + kg + 1)
                    up(kg, 2, kg, True)

                def body(j, first=False, last=False):
                    if not first:
                        pe.wait_ge(relu_done, (j + s0) * 2)
                    pe.wait_ge(lo_done, j * 4 + (b - 1))
                    up(0, 0, 0)
                    hidden_turn(j + (s0 - 1))
                    pe.wait_ge(lo_done, j * 4 + b)
                    up(1, 0, 1)
                    pe.wait_ge(h_lo, (j + s0) * 2)
                    for n in range(2):
                        pe.wait_ge(lo_done, j * 4 + (b + n + 1))
                        if last and n == 1:
                            hidden_turn(q_last)
                        down(n, n, first, False)

                q_last = s0 + MLP_STEPS - 1
                body(1, first=True)
                with pe.Fori(2, MLP_STEPS - 1) as j:
                    body(j)
                body(MLP_STEPS - 1, last=True)
                pe.wait_ge(h_lo, 2 * (q_last + 1))
                for n in range(2):
                    pe.wait_ge(lo_done, b + MLP_UNITS - 1 + n)
                    down(n, n, False, True, KT + 4)

            def head_sums(i, sq):
                pe.wait_ge(sq_ready, i + 1)
                for p in range(KT):
                    ins = pe.matmul(psum[4][:, 0:T], keep["head_window"][:, 14 - 2 * p:14 - 2 * p + P], sq[:, p],
                                    start=(p == 0), stop=(p == KT - 1))
                ins.then_inc(sums_ready, 1)

            def head_spread(i, r):
                pe.wait_ge(rn_ready, i + 1)
                pe.wait_ge(spread_in, 16 if i == 0 else 32)
                for p in range(KT):
                    ins = pe.matmul(psum[4 + p // 2][:, (p % 2) * T:(p % 2 + 1) * T], SPREAD[:, p], r,
                                    start=(p % 2 == 0), stop=(p % 2 == 1))
                    if p % 2:
                        ins.then_inc(rn_spread, 1)

            def attention(a0, heads, dh, q_of, k_of, bias, E, PT, V_):
                per = 512 // (MT * dh)
                for h in range(heads + 3):
                    if h < heads:
                        if h >= 2:
                            pe.wait_ge(masked, a0 + h - 1)
                        for m in range(MT):
                            c0, n = (0, P) if m == 0 else (P, T)
                            o = psum[h % 2][:, c0:c0 + n]
                            ins = pe.matmul(o, q_of(h)[:, m * P:(m + 1) * P], k_of(h)[:, 0:n], start=(m == 0),
                                            stop=(not bias and m == 1))
                            if bias:
                                ins = pe.matmul(o, ident[:, h:h + 1].broadcast_to((P, P)), negc[:, 0:n],
                                                start=False, stop=(m == 1))
                        ins.then_inc(logits, 1)
                    g = h - 1
                    if 0 <= g < heads:
                        pe.wait_ge(expd, a0 + g + 1)
                        if g >= 2:
                            pe.wait_ge(pt_ready, a0 + g - 1)
                        for s in range(3):
                            ins = pe.transpose(psum[2 + g % 2][:, s * P:(s + 1) * P], E[:, g % 2, s * P:(s + 1) * P],
                                               ident[:, :])
                        ins.then_inc(e_turned, 1)
                    g = h - 3
                    if g >= 0:
                        pe.wait_ge(pt_ready, a0 + g + 1)
                        if g % per == 0 and g // per >= 2:
                            pe.wait_ge(att_out, a0 // 4 + g // per - 1)
                        o = psum[4 + (g // per) % 2][:, (g % per) * MT * dh:(g % per + 1) * MT * dh]
                        v = V_[:, :, g * dh:(g + 1) * dh]
                        pt = PT[:, g % 2]
                        pe.matmul(o[:, 0:dh], pt[:, 0:P], v[:, 0], start=(g % per == 0), stop=False)
                        pe.matmul(o[:, dh:2 * dh], pt[:, P:2 * P], v[:, 0], start=False, stop=False)
                        pe.matmul(o[:, dh:2 * dh], pt[:, 2 * P:3 * P], v[:, 1], start=False,
                                  stop=(g % per == per - 1)).then_inc(av_prod, 1)

            pe.wait_ge(ident_in, 16)
            norm_turn("rwkv")

            def lora_in1(order, w, n, bank):
                for k in range(KT):
                    ins = pe.matmul(psum[bank][0:min(n, P), 0:T], w[:, k, 0:min(n, P)], XM[order % 2][:, k],
                                    start=(k == 0), stop=(k == KT - 1))
                if n > P:
                    for k in range(KT):
                        ins = pe.matmul(psum[bank + 1][0:n - P, 0:T], w[:, k, P:n], XM[order % 2][:, k],
                                        start=(k == 0), stop=(k == KT - 1))
                ins.then_inc(lora1, 1)

            chunk("k", 0, "feature", 0, ready=lambda b: pe.wait_ge(first_lo, b + 1))
            pe.wait_ge(lora_in, 16 * 7)
            pe.wait_ge(mixed, 1)
            lora_in1(1, w1s, LORA, 4)
            chunk("k", 1, "feature", 0)
            pe.wait_ge(mixed, 3)
            lora_in1(3, a1s, LORA, 5)
            chunk("v", 0, "token", 1, ready=lambda b: pe.wait_ge(mix_lo, 1))
            pe.wait_ge(mixed, 5)
            lora_in1(5, g1s, GATE, 6)
            for q, (w2, t1) in enumerate(((w2s, tw), (a2s, ta))):
                for b in range(4):
                    if q == 0:
                        pe.wait_ge(lora1_act, b + 1)
                    else:
                        pe.wait_ge(lora2_read, b + 1)
                    for j in range(2):
                        p = 2 * b + j
                        ins = pe.matmul(psum[4 + b][:, j * T:(j + 1) * T], w2[0:LORA, p * P:(p + 1) * P],
                                        t1[0:LORA, :], start=(j == 0), stop=(j == 1))
                    ins.then_inc(lora2, 1)
            chunk("v", 1, "token", 1)
            for b in range(4):
                m, n = b // 2, b % 2
                pe.wait_ge(lora2_read, 4 + b + 1)
                pe.matmul(psum[4 + b][:, :], sga[:, m * P:(m + 1) * P], g2a[:, n * UN:(n + 1) * UN], start=True,
                          stop=False)
                pe.matmul(psum[4 + b][:, :], sgb[0:GATE - P, m * P:(m + 1) * P], g2b[0:GATE - P, n * UN:(n + 1) * UN],
                          start=False, stop=True).then_inc(lora2, 1)
            pe.wait_ge(lora2_read, 9)
            pe.wait_ge(const_in, 16 * (len(CONST_KEEP) - 2))
            head_sums(0, KKSQ)
            chunk("r", 0, "feature", 0, ready=lambda b: pe.wait_ge(mix_lo, 2))
            pe.wait_ge(lora2_read, 12)
            head_spread(0, rn)
            chunk("r", 1, "feature", 0)
            pe.wait_ge(spread_read, 4)
            pe.wait_ge(rho_ready, 1)
            for r in range(4):
                c = r // 2
                if r:
                    pe.wait_ge(y_ready, 2 * r)
                    pe.wait_ge(state_ready, 4 * min(r, 2))
                for l in range(2):
                    gi = 2 * r + l
                    p0 = 2 * (gi % 4)
                    pe.wait_ge(padded, 4 * (gi + 1))
                    for h in range(4):
                        ar = AR[:, (p0 + h // 2) * 2 + c]
                        for s in range(2):
                            ins = pe.matmul(psum[4 * l + h][:, s * T:(s + 1) * T], PADS[c][l][:, s, h], ar, start=(s == 0),
                                            stop=(s == 1))
                        ins.then_inc(pair_prod, 1)
                pe.wait_ge(pair_masked, 4 * (2 * r + 2))
                for l in range(2):
                    gi = 2 * r + l
                    pe.wait_ge(first_ready, gi + 1)
                    for h in range(4):
                        ins = pe.transpose(psum[2 + l][:, h * P:(h + 1) * P], TT_[l][:, h], ident[:, :])
                    ins.then_inc(first_turned, 1)
                for i in range(6):
                    for l in range(2):
                        if i == 0:
                            pe.wait_ge(inv_ready, 2 * r + l + 1)
                        else:
                            pe.wait_ge(doubled, 12 * r + 2 * (i - 1) + l + 1)
                        for h in range(4):
                            ins = pe.matmul(psum[l][:, h * P:(h + 1) * P], M[l][:, h, 0:P], TI_[l][:, h],
                                            start=(h == 0), stop=(h == 3))
                        ins.then_inc(half_prod, 1)
                    if r == 0 and i == 2:
                        pe.wait_ge(bonus_prod, 1)
                        for q in range(2 * KT):
                            cq, p = q // KT, q % KT
                            ins = pe.matmul(psum[7][:, 16 * cq + 2 * p:16 * cq + 2 * p + 2],
                                            BONUS[:, p, cq * P:(cq + 1) * P], keep["head_window"][:, 14:16],
                                            start=(q == 0), stop=(q == 2 * KT - 1))
                        ins.then_inc(bonus_sum, 1)
                    for l in range(2):
                        pe.wait_ge(half_masked, 12 * r + 2 * i + l + 1)
                        if i < 5:
                            for h in range(4):
                                pe.matmul(psum[2 + l][:, h * P:(h + 1) * P], TT_[l][:, h], PM[l][:, h],
                                          start=(h == 0), stop=(h == 3))
                        for h in range(4):
                            ins = pe.matmul(psum[4 + l][:, h * P:(h + 1) * P], PM[l][:, h], TT_[l][:, h],
                                            start=(h == 0), stop=(h == 3))
                        ins.then_inc(step_prod, 1)

                def carried(l, p0, which):
                    for pp in range(2):
                        pe.matmul(psum[6 + l][:, pp * P:(pp + 1) * P], AR[:, (p0 + pp) * 2 + c, which],
                                  S0[:, p0 + pp], start=(pp == 0), stop=False)

                if r == 0:
                    pe.wait_ge(bonus_read, 1)
                for l in range(2):
                    p0 = 2 * ((2 * r + l) % 4)
                    if c:
                        carried(l, p0, 0)
                    for h in range(4):
                        hd = (2 * p0 + h) * HD
                        ins = pe.matmul(psum[6 + l][:, h * HD:(h + 1) * HD], M[l][:, h, 2 * P:3 * P],
                                        V[:, c, hd:hd + HD], start=(c == 0 and h == 0), stop=(h == 3))
                    ins.then_inc(rhs_prod, 1)
                for l in range(2):
                    pe.wait_ge(rhs_ready, 2 * r + l + 1)
                    pe.wait_ge(doubled, 12 * r + 10 + l + 1)
                    for h in range(4):
                        ins = pe.matmul(psum[6 + l][:, h * HD:(h + 1) * HD], TT_[l][:, h],
                                        SA[l][:, h * HD:(h + 1) * HD], start=(h == 0), stop=(h == 3))
                    ins.then_inc(sa_prod, 1)
                for l in range(2):
                    p0 = 2 * ((2 * r + l) % 4)
                    pe.wait_ge(sa_ready, 2 * r + l + 1)
                    if c:
                        carried(l, p0, 1)
                    for h in range(4):
                        hd = (2 * p0 + h) * HD
                        o = psum[6 + l][:, h * HD:(h + 1) * HD]
                        pe.matmul(o, M[l][:, h, P:2 * P], SA[l][:, h * HD:(h + 1) * HD], start=(c == 0 and h == 0),
                                  stop=False)
                        ins = pe.matmul(o, M[l][:, h, 3 * P:4 * P], V[:, c, hd:hd + HD], start=False,
                                        stop=(h == 3))
                    ins.then_inc(y_prod, 1)
                if c == 0:
                    for l in range(2):
                        p0 = 2 * (2 * r + l)
                        for s, src in enumerate((BE, kT)):
                            for pp in range(2):
                                k = (2 * s + pp) * P
                                ins = pe.transpose(psum[l][:, k:k + P], src[:, p0 + pp, 0:P], ident[:, :])
                        ins.then_inc(keys_turned, 1)
                    for l in range(2):
                        p0 = 2 * (2 * r + l)
                        pe.wait_ge(keys_ready, 2 * r + l + 1)
                        for pp in range(2):
                            o = psum[2 + l][:, pp * P:(pp + 1) * P]
                            pe.matmul(o, PM[l][:, pp], SA[l][:, pp * P:(pp + 1) * P], start=(pp == 0), stop=False)
                            ins = pe.matmul(o, PM[l][:, 2 + pp], V[:, 0, (p0 + pp) * P:(p0 + pp + 1) * P],
                                            start=False, stop=(pp == 1))
                        ins.then_inc(state_prod, 1)
            pe.wait_ge(y_done, 3)
            turn("rwo", Y, (0, 1))

            def rwo_ready(b):
                if b == 2:
                    pe.wait_ge(y_done, 4)
                    turn("rwo", Y, (2, 3))
                pe.wait_ge(turned_lo, b + 1)

            for n in range(2):
                chunk("rwo", n, "token", ready=rwo_ready)
            norm_turn("mlp0")
            mlp(0)
            norm_turn("kv")
            pe.wait_ge(turned_lo, SPLIT0[TI["attn"]])
            turn("attn", XN)
            chunk("fk", 0, "feature", ready=split_ready("kv"))
            chunk("fk", 1, "feature")
            pe.wait_ge(fox_in, 16 * 3)
            pe.wait_ge(turned_lo, SPLIT0[TI["fo"]])
            for part in (XH, XL):
                for k in range(KT):
                    ins = pe.matmul(psum[4][0:NH, 0:T], wf[:, k], part[:, k].bitcast(F32),
                                    start=(part is XH and k == 0), stop=(part is XL and k == KT - 1))
            ins.then_inc(f_prod, 1)
            chunk("fv", 0, "token")
            pe.wait_ge(f_z, 1)
            head_sums(1, fSQ)
            chunk("fv", 1, "token")
            head_spread(1, frn)
            chunk("fq", 0, "feature", 1)
            chunk("fq", 1, "feature", 1)
            pe.wait_ge(spread_read, 8)
            head_sums(2, fSQ)
            head_spread(2, frn)
            pe.wait_ge(spread_read, 12)
            pe.wait_ge(negc_ready, 1)
            attention(0, NH, HD, lambda h: fQ[:, h // 2], lambda h: fKP[:, h], True, fE, fPT, fV)
            pe.wait_ge(att_out, 4)
            turn("fo", fO)
            for n in range(2):
                chunk("fo", n, "token", ready=split_ready("fo"))
            norm_turn("mlp1")
            mlp(1)
            norm_turn("ret")
            for name in ("rq", "rk"):
                for n in range(2):
                    chunk(name, n, "feature", ready=split_ready("ret"))
            for name in ("rv", "rg"):
                for n in range(4):
                    chunk(name, n, "token")
            pe.wait_ge(acc_read["act"], READ_COUNT[CHUNK0["rg"] + 3][1])
            pe.wait_ge(rotated, 2 * RET_H)
            for h in range(RET_H + 1):
                if h < RET_H:
                    if h >= 2:
                        pe.wait_ge(decayed, h - 1)
                    for m in range(MT):
                        o = psum[h % 2][:, 0:T] if m == 0 else psum[h % 2][:, T:T + P]
                        for e in range(2):
                            ins = pe.matmul(o, rK[:, h, e, m * P:(m + 1) * P], rQ[:, h, e, m * P:T],
                                            start=(m == 0 and e == 0), stop=(m == 1 and e == 1))
                    ins.then_inc(scores, 1)
                g = h - 1
                if g >= 0:
                    pe.wait_ge(decayed, g + 1)
                    if g >= 2:
                        pe.wait_ge(ret_out, 2 * (g - 1))
                    v = rV[:, :, g * RET_DV:(g + 1) * RET_DV]
                    pt = rPT[:, g % 2]
                    b = 4 + (2 * g) % 4
                    pe.matmul(psum[b][:, :], pt[:, 0:P], v[:, 0], start=True, stop=True).then_inc(ret_prod, 1)
                    pe.matmul(psum[b + 1][:, :], pt[:, P:2 * P], v[:, 0], start=True, stop=False)
                    pe.matmul(psum[b + 1][:, :], pt[:, 2 * P:3 * P], v[:, 1], start=False, stop=True)\
                        .then_inc(ret_prod, 1)
            pe.wait_ge(ret_out, 8)
            turn("reo", rG)
            for n in range(2):
                chunk("reo", n, "token", kts=2 * KT, ready=split_ready("reo"))
            norm_turn("mlp2")
            mlp(2)
            norm_turn("moba")
            for name in ("mq", "mk"):
                for n in range(2):
                    chunk(name, n, "feature", ready=split_ready("moba"))
            for i, (name, src) in enumerate((("mq", mQ), ("mk", mK))):
                pe.wait_ge(acc_read["act"], READ_COUNT[CHUNK0[name] + 1][1])
                pe.wait_ge(moba_in, 16 * 4)
                for b in range(4):
                    if i:
                        pe.wait_ge(roped, b + 1)
                    for j in range(2):
                        ins = pe.matmul(psum[4 + b][0:ROPE, j * T:(j + 1) * T], mSWAP, src[:, 2 * b + j],
                                        start=(j == 0), stop=(j == 1))
                    ins.then_inc(rope_swapped, 1)
            for n in range(2):
                chunk("mv", n, "token")
            pe.wait_ge(acc_read["act"], READ_COUNT[CHUNK0["mv"] + 1][1])
            pe.wait_ge(roped, 8)
            attention(NH, MOBA_H, MOBA_D, lambda h: mQ[:, h], lambda h: mK[:, h], False, mE, mPT, mV)
            pe.wait_ge(att_out, 4 + 4)
            turn("mo", mO)
            for n in range(2):
                chunk("mo", n, "token", ready=split_ready("mo"))
            norm_turn("mlp3")
            mlp(3)


def pack(w):
    k, n = w.shape
    return w.reshape(k // 512, UK, P, n // UN, UN).transpose(3, 0, 2, 1, 4).reshape(-1, P, UK * UN)


def pack_mlp(w_in, w_out):
    up, down = pack(w_in), pack(w_out)
    units = [up[0], up[1]]
    for j in range(1, MLP_STEPS):
        units += [up[2 * j], up[2 * j + 1], down[j - 1], down[MLP_STEPS + j - 1]]
    units += [down[MLP_STEPS - 1], down[2 * MLP_STEPS - 1]]
    return np.stack(units)


def by_partition(w):
    return w.reshape(-1, P, w.shape[1]).transpose(1, 0, 2).reshape(P, -1)


def laid_out(i):
    f = {k: np.asarray(v) for k, v in i.items()}
    o = {"x": f["x"].reshape(MT, P, D).transpose(1, 0, 2)}
    per = {"rwkv_norm_g": f["rwkv_norm_g"][0], "w0": f["rwkv_w0"][0], "a0": f["rwkv_a0"][0],
           "k_k": f["rwkv_k_k"][0], "k_a": f["rwkv_k_a"][0], "r_k": f["rwkv_r_k"][0],
           "kv_norm_g": f["kv_norm_g"], "k_norm_g": f["k_norm_g"], "attn_norm_g": f["attn_norm_g"][0],
           "q_norm_g": f["q_norm_g"][0], "mlp_norm_g0": f["mlp_norm_g"][0], "mlp_norm_g1": f["mlp_norm_g"][1],
           "ln_mix_pre_0": f["ln_mix_pre_0_2"], "ln_mlp_pre_0": f["ln_mlp_pre_0_2"],
           "ln_mix_pre_1": f["ln_mix_pre_1_2"], "ln_mlp_pre_1": f["ln_mlp_pre_1_2"]}
    per |= {f"mu{m}": f["rwkv_mu"][0, m] for m in range(6)}
    o["vecs"] = np.stack([per[n].reshape(KT, P).T for n in VECS], 1).reshape(P, -1)
    rows = {"lnx_w": f["rwkv_lnx_w"][0], "lnx_b": f["rwkv_lnx_b"][0]}
    rows |= {n: f[n + "_2"] for n in ROWS[2:]}
    o |= {n: rows[n].reshape(1, D) for n in ROWS}
    o["w1"], o["a1"], o["g1"] = (by_partition(f[n][0]) for n in ("rwkv_w1", "rwkv_a1", "rwkv_g1"))
    o["w2"], o["a2"] = f["rwkv_w2"][0], f["rwkv_a2"][0]
    o["g2a"], o["g2b"] = f["rwkv_g2"][0, :P], f["rwkv_g2"][0, P:]
    o["wf"] = by_partition(f["kv_w"][:, 2 * D:])
    o["f_bias"] = f["kv_f_bias"].reshape(NH, 1)
    cols = np.arange(D).reshape(RET_H, P, 2).transpose(0, 2, 1).reshape(-1)
    ret, mo = f["w_in_0_2"], f["w_in_1_2"]
    w = {"r": f["rwkv_w_rkv"][0, 0], "k": f["rwkv_w_rkv"][0, 1], "v": f["rwkv_w_rkv"][0, 2],
         "rwo": f["rwkv_w_o"][0], "fk": f["kv_w"][:, :D], "fv": f["kv_w"][:, D:2 * D],
         "fq": f["attn_w_q"][0], "fo": f["attn_w_o"][0],
         "rq": ret[:, :D][:, cols], "rk": ret[:, D:2 * D][:, cols], "rv": ret[:, 2 * D:4 * D], "rg": ret[:, 4 * D:],
         "reo": f["w_out_0_2"], "mq": mo[:, :D], "mk": mo[:, D:2 * D], "mv": mo[:, 2 * D:], "mo": f["w_out_1_2"]}
    o |= {"w_" + n: pack(m) for n, m in w.items()}
    o["w_mlp0"] = pack_mlp(f["mlp_w_in"][0], f["mlp_w_out"][0])
    o["w_mlp1"] = pack_mlp(f["mlp_w_in"][1], f["mlp_w_out"][1])
    o["w_mlp2"] = pack_mlp(f["w_up_0_2"], f["w_down_0_2"])
    o["w_mlp3"] = pack_mlp(f["w_up_1_2"], f["w_down_1_2"])
    o |= constants()
    return {k: np.ascontiguousarray(v) for k, v in o.items()}


def kernel(**inputs):
    import concourse.bacc as bacc
    from concourse.bass_utils import run_bass_kernel_spmd

    nc = bacc.Bacc("TRN2", target_bir_lowering=False, num_devices=1)
    arrays = {f"in_{k}": v for k, v in laid_out(inputs).items()}
    a = {k[3:]: nc.dram_tensor(k, v.shape, mybir.dt.from_np(v.dtype), kind="ExternalInput").ap()
         for k, v in arrays.items()}
    out = nc.dram_tensor("out", (1, T, D), F32, kind="ExternalOutput").ap()
    build(nc, a, out)
    return run_bass_kernel_spmd(nc, [arrays], core_ids=[0]).results[0]["out"]
```

```python
from contextlib import ExitStack

import numpy as np

import concourse.bass as bass
from concourse import mybir

F32 = mybir.dt.float32
F32R = mybir.dt.float32r
ACT = mybir.ActivationFunctionType
ALU = mybir.AluOpType
AXX = mybir.AxisListType.X

P = 128
D = 1024
T = 256
FF = 4096
MT = T // P
KT = D // P
RAW_RING, SPLIT_RING = 4, 2
UK, UN = 4, 512
NH = 16
HD = 64
LORA, GATE = 64, 160
RET_H, RET_DV = 4, 512
MOBA_H, MOBA_D = 8, 128
ROPE = 32
NORM_EPS, GN_EPS = 1e-6, 64e-5
NEG = -1e30

GEMMS = [("k", 8, 2), ("v", 8, 2), ("r", 8, 2), ("rwo", 8, 2), ("mlp0", 0, 0),
         ("fk", 8, 2), ("fq", 8, 2), ("fv", 8, 2), ("fo", 8, 2), ("mlp1", 0, 0),
         ("rq", 8, 2), ("rk", 8, 2), ("rv", 8, 4), ("rg", 8, 4), ("reo", 16, 2), ("mlp2", 0, 0),
         ("mq", 8, 2), ("mk", 8, 2), ("mv", 8, 2), ("mo", 8, 2), ("mlp3", 0, 0)]
READER = {"r": "act", "k": "act", "v": "act", "rwo": "sum", "fk": "act", "fv": "act", "fq": "act",
          "fo": "sum", "rq": "dve", "rk": "dve", "rv": "act", "rg": "act", "reo": "sum",
          "mq": "act", "mk": "act", "mv": "act", "mo": "sum"}
MLP_STEPS = FF // UN
MLP_UNITS = 4 * MLP_STEPS


def plan():
    u0, chunk0, u, g = {}, {}, 0, 0
    readers = []
    for name, kt, nn in GEMMS:
        u0[name], chunk0[name] = u, g
        if kt == 0:
            u += MLP_UNITS
            continue
        readers += [READER[name]] * nn
        u += nn * kt // UK
        g += nn
    read_count, counts = [], {"act": 0, "dve": 0, "sum": 0}
    for r in readers:
        counts[r] += 2
        read_count.append((r, counts[r]))
    return u0, chunk0, read_count, u


U0, CHUNK0, READ_COUNT, UNITS = plan()

VECS = ["rwkv_norm_g", "mu0", "mu1", "mu2", "mu3", "mu4", "mu5", "w0", "a0", "k_k", "k_a", "r_k",
        "kv_norm_g", "k_norm_g", "attn_norm_g", "q_norm_g", "mlp_norm_g0", "mlp_norm_g1",
        "ln_mix_pre_0", "ln_mlp_pre_0", "ln_mix_pre_1", "ln_mlp_pre_1"]
ROWS = ["lnx_w", "lnx_b", "ln_mix_post_0", "ln_mlp_post_0", "ln_mix_post_1", "ln_mlp_post_1"]

TURNS = [("rwkv", "rwkv_norm_g", 8, True, 0), ("rwo", None, 8, False, 0), ("mlp0", "mlp_norm_g0", 8, True, 0),
         ("kv", "kv_norm_g", 8, True, 0), ("attn", "attn_norm_g", 8, False, 1), ("fo", None, 8, False, 0),
         ("mlp1", "mlp_norm_g1", 8, True, 0), ("ret", "ln_mix_pre_0", 8, True, 0), ("reo", None, 16, False, 0),
         ("mlp2", "ln_mlp_pre_0", 8, True, 0), ("moba", "ln_mix_pre_1", 8, True, 0), ("mo", None, 8, False, 0),
         ("mlp3", "ln_mlp_pre_1", 8, True, 0)]
TI = {t[0]: i for i, t in enumerate(TURNS)}


def turn_counts():
    turned, split, normed, b, s, n = [], [], [], 0, 0, 0
    for name, _, kt, norm, _ in TURNS:
        turned.append(b)
        split.append(s)
        normed.append(n)
        b += kt // 2
        s += kt // 2 if name != "rwkv" else 0
        n += 1 if norm else 0
    return turned, split, normed


TURNED0, SPLIT0, NORM0 = turn_counts()
RESIDUALS = {"rwkv": 0, "mlp0": 4, "kv": 8, "mlp1": 12, "ret": 16, "mlp2": 20, "moba": 24, "mlp3": 28}

RESIDUALS_AFTER_POST = [20, 24, 28, 32]


def constants():
    f = np.float32
    i = np.arange(P)
    c = {"ident": np.eye(P, dtype=f)}
    strict = (i[:, None] < i[None, :]).astype(f)
    incl = (i[:, None] <= i[None, :]).astype(f)
    c["pair_masks"] = np.concatenate([strict, incl, strict, incl], 1)
    lm = []
    for m in (1, 2, 4, 8, 16, 32, 64):
        b = i // m
        lm.append(((b[:, None] % 2 == 1) & (b[None, :] == b[:, None] - 1)).astype(f))
    c["first_mask"] = -lm[0].T
    c["level_masks"] = np.concatenate(lm[1:], 1)
    c["head_window"] = np.zeros((P, 142), f)
    c["head_window"][i, 14 + i // HD] = 1.0
    c["head_spread"] = (i[:, None] == np.arange(D)[None, :] // HD).astype(f)
    c["head_blocks"] = (i[:, None] // HD == i[None, :] // HD).astype(f)
    c["head_halves"] = np.stack([(i // HD == 0), (i // HD == 1)], 1).astype(f)
    c["ones_row"] = np.ones((1, KT * T), f)
    causal = np.where(i[:, None] >= i[None, :], 0.0, NEG).astype(f)
    c["causal"] = np.concatenate([causal, np.zeros((P, P), f), causal], 1)
    h = np.arange(RET_H, dtype=f)
    lg = np.log(1.0 - 2.0 ** (-5.0 - h.astype(np.float64)))
    t = np.arange(T)
    diff = t[None, None, :] - i[:, None, None]
    dec = np.where(diff >= 0, np.exp(lg[None, :, None] * np.maximum(diff, 0)) / 16.0, 0.0)
    c["ret_decay"] = dec.reshape(P, RET_H * T).astype(f)
    freq = (1.0 / (f(10000.0) ** np.linspace(0.0, 1.0, P, dtype=f))).astype(f)
    ang = (np.arange(T, dtype=f)[None, :] * freq[:, None]).astype(f).astype(np.float64)
    c["ret_cos"], c["ret_sin"] = np.cos(ang).astype(f), np.sin(ang).astype(f)
    inv = (f(500000.0) ** (-np.arange(0, ROPE, 2, dtype=f) / f(ROPE))).astype(f)
    a2 = (np.arange(T, dtype=f)[None, :] * inv[:, None]).astype(f).astype(np.float64)
    c["rope_cos"] = np.concatenate([np.cos(a2), np.cos(a2)], 0).astype(f)
    c["rope_sin"] = np.concatenate([-np.sin(a2), np.sin(a2)], 0).astype(f)
    perm = np.zeros((P, ROPE), f)
    j = np.arange(ROPE)
    perm[(j + ROPE // 2) % ROPE, j] = 1.0
    c["rope_swap"] = perm
    return c


CONST_KEEP = ["ident", "pair_masks", "first_mask", "level_masks", "head_window", "head_blocks", "head_halves", "causal"]


def build(nc, a, out):
    with ExitStack() as ctx:
        def sb(name, shape, dt=F32):
            return ctx.enter_context(nc.sbuf_tensor(name, shape, dt))

        def sem(name):
            return ctx.enter_context(nc.semaphore(name))

        X = sb("X", [P, MT, D])
        raw = sb("raw", [P, RAW_RING, UK, UN])
        whi = sb("whi", [P, SPLIT_RING, UK, UN], F32R)
        wlo = sb("wlo", [P, SPLIT_RING, UK, UN], F32R)
        XH = sb("XH", [P, 2 * KT, T], F32R)
        XL = sb("XL", [P, 2 * KT, T], F32R)
        vecs = sb("vecs", [P, len(VECS), KT])
        keep = {n: sb(f"c_{n}", list(a[n].shape)) for n in CONST_KEEP if n != "causal"}
        ident = keep["ident"]
        small = sb("small", [P, 128])
        att_nmax = sb("att_nmax", [P, 4, MT])
        att_sum = sb("att_sum", [P, NH, MT])
        ret_sums = sb("ret_sums", [P, RET_H * MT])
        NA = 24320
        arena = sb("arena", [P, NA])
        psum = [ctx.enter_context(nc.psum_tensor(f"bank{i}", [P, 512], F32)) for i in range(8)]

        def at(off, *dims):
            n = int(np.prod(dims))
            assert off + n <= NA, (off, dims)
            v = arena[:, off:off + n]
            names = "abcd"[:len(dims)]
            if len(dims) == 1:
                return v
            return v.rearrange(f"p ({' '.join(names)}) -> p {' '.join(names)}", **dict(zip(names, dims)))

        def gain(name, k):
            i = VECS.index(name)
            return vecs[:, i, k:k + 1]

        def bank_kt(b):
            return psum[b][:, :].rearrange("p (a t) -> p a t", a=2)

        norm_ss = small[:, 18:22].rearrange("p (m n) -> p m n", m=2)
        norm_ms, norm_rstd = small[:, 2:4], small[:, 4:6]
        norm_sd = small[:, 6:8]
        post_ss = small[:, 8:12].rearrange("p (m n) -> p m n", m=2)
        post_ms, post_sd, post_rstd = small[:, 12:14], small[:, 14:16], small[:, 16:18]
        eps_col = small[:, 22:23]
        bonus = small[:, 32:64]
        state_scale = small[:, 64:72]
        gn_mean, gn_var = small[:, 72:80], small[:, 88:96]

        XN, JUNK = at(4096, MT, D), at(6144, 2, UN)
        RELU = at(8240, MT, UN)
        hT, xxT = at(0, KT, T), at(2048, KT, T)
        XM = [at(6144, KT, T), at(4096, KT, T)]
        w1s, a1s, g1s = at(8192, KT, LORA), at(8704, KT, LORA), at(9216, KT, GATE)
        w2s, a2s, g2a, g2b = at(10496, D), at(11520, D), at(12544, D), at(13568, D)
        rT, kT, V, G = at(14592, KT, T), at(16640, KT, T), at(18688, MT, D), at(20736, MT, D)
        tw, ta, sga, sgb = at(22784, T), at(23040, T), at(23296, T), at(23552, T)
        k16 = kT.rearrange("p k (c t) -> p (k c) t", c=2)
        sT, aT, lwT = at(0, KT, T), at(2080, KT, T), at(4128, KT, T)
        LW = P + 1
        Lx = at(6176, KT * 2, LW)
        E1, E2 = at(8240, KT * 2, LW), at(0, KT * 2, LW)
        kkT, sqT, rn = at(10496, KT, T), at(12544, KT, T), at(22784, T)
        AR = at(4128, KT * 2, 2, P)
        BE = aT
        Y = at(0, MT, D)
        M = [at(8240 + 2048 * l, 4, 512) for l in range(2)]
        TI_ = [at(12336 + 512 * l, 4, P) for l in range(2)]
        TT_ = [at(13360 + 512 * l, 4, P) for l in range(2)]
        PM = [at(14384 + 512 * l, 4, P) for l in range(2)]
        PADS = [[at(1024, 2, 4, P), at(15408, 2, 4, P)],
                [raw[:, 2].rearrange("p (a s) (h t) -> p a s h t", a=2, h=4)[:, 1], at(15408, 2, 4, P)]]
        KKSQ = at(14592, KT, T)
        SA = [at(22784 + 256 * l, 256) for l in range(2)]
        S0 = at(23296, KT, P)
        BONUS = raw[:, 2].rearrange("p k (a t) -> p (k a) t", a=2)
        YQ = raw[:, 2, 0]
        LNROW = raw[:, 3].rearrange("p (i k) n -> p i (k n)", i=2)
        ones, mids = at(24064, P), small[:, 104:120].unsqueeze(2)
        SPREAD = at(23040, KT, P)
        fK, fKP, fV, fQ = at(0, KT, T), at(8240, NH, T), at(12336, MT, D), at(14384, KT, T)
        fSQ, negc, frn = at(16432, KT, T), at(18480, T), at(18736, T)
        fQ2 = [fQ, fSQ]
        wf, fz, fl = at(18992, KT, NH), at(19120, T), at(19376, T)
        fc, fbias = at(19632, T), at(7600, 1)
        fL, fE, fPT = at(19888, 2, 384), at(20656, 2, 384), at(21424, 2, 384)
        fO, fCAUSAL = at(22192, MT, D), at(7200, 384)
        rDEC, rCOS, rSIN = at(0, RET_H, T), at(1024, T), at(1280, T)
        rQ, rK = at(1536, RET_H, 2, T), at(7168, RET_H, 2, T)
        rV, rG = at(9216, MT, 2 * D), at(13312, MT, 2 * D)
        rA, rB = [at(17408 + 512 * i, 2, T) for i in range(2)], [at(18432 + 512 * i, 2, T) for i in range(2)]
        rPT = at(19456, 2, 384)
        RET_BANK = [4, 6, 0, 2]
        POST = at(20224, 2, D)
        PTMP = at(22272, 2, MT, UN)
        mQ, mCOS, mSIN, mSWAP, mCAUSAL = at(0, KT, T), at(2048, T), at(2304, T), at(2560, ROPE), at(2592, 384)
        mTMP, mTMP2 = at(2976, 2, T), at(3488, 2, T)
        mK, mV = at(7168, KT, T), at(9216, MT, D)
        mL, mE, mPT = at(11264, 2, 384), at(12032, 2, 384), at(12800, 2, 384)
        mO = at(13568, MT, D)

        raw_landed = [sem(f"raw_landed{i}") for i in range(RAW_RING)]
        hi_done, lo_done, unit_used = sem("hi_done"), sem("lo_done"), sem("unit_used")
        acc_read = {"act": sem("acc_read_act"), "dve": sem("acc_read_dve")}
        spread_in = sem("spread_in")
        x_in = [sem(f"x_in{i}") for i in range(4)]
        ident_in, const_in, vecs_in, lora_in = sem("ident_in"), sem("const_in"), sem("vecs_in"), sem("lora_in")
        lnrow_in, fox_in, ret_in, moba_in = sem("lnrow_in"), sem("fox_in"), sem("ret_in"), sem("moba_in")
        post_in, out_done = sem("post_in"), sem("out_done")
        ss_done, ms_done, sd_done, rstd_done, xn_ready = (sem(n) for n in (
            "ss_done", "ms_done", "sd_done", "rstd_done", "xn_ready"))
        xn_act = sem("xn_act")
        turned, turned_hi, turned_lo, hT_ready = sem("turned"), sem("turned_hi"), sem("turned_lo"), sem("hT_ready")
        residual, eps_ready = sem("residual"), sem("eps_ready")
        pss_done, pms_done, psd_done, ptmp_done = (sem(n) for n in (
            "pss_done", "pms_done", "psd_done", "ptmp_done"))
        relu_done, square_done, h_turned, h_hi, h_lo = (sem(n) for n in (
            "relu_done", "square_done", "h_turned", "h_hi", "h_lo"))
        dve_step, pool_step = sem("dve_step"), sem("pool_step")
        first_mixed, first_hi, first_lo, mixed, mix_hi, mix_lo, lora1, lora1_act, lora2, lora2_read = (sem(n) for n in (
            "first_mixed", "first_hi", "first_lo", "mixed", "mix_hi", "mix_lo", "lora1", "lora1_act", "lora2", "lora2_read"))
        lw_ready, centred, exps_ready, sq_ready, sums_ready, sums_ms, sums_sd, rn_ready, rn_spread, spread_read = (
            sem(n) for n in ("lw_ready", "centred", "exps_ready", "sq_ready", "sums_ready", "sums_ms", "sums_sd",
                             "rn_ready", "rn_spread", "spread_read"))
        bonus_prod, bonus_sum, bonus_read, prepared, rho_ready, scale_ready = (sem(n) for n in (
            "bonus_prod", "bonus_sum", "bonus_read", "prepared", "rho_ready", "scale_ready"))
        padded, pair_prod, pair_masked, first_ready, first_turned, inv_ready, half_prod, half_masked, step_prod, \
            rhs_prod, rhs_ready, sa_prod, sa_ready, y_prod, y_ready, keys_turned, keys_ready, state_prod, \
            state_ready = (sem(n) for n in (
                "padded", "pair_prod", "pair_masked", "first_ready", "first_turned", "inv_ready", "half_prod",
                "half_masked", "step_prod", "rhs_prod", "rhs_ready", "sa_prod", "sa_ready", "y_prod", "y_ready",
                "keys_turned", "keys_ready", "state_prod", "state_ready"))
        kappa_ready, cleared = sem("kappa_ready"), sem("cleared")
        doubled, inv_prod, inv_doubled = sem("doubled"), sem("inv_prod"), sem("inv_doubled")
        y_centred, y_squared, gn_ms, gn_sd, y_done, gate_ready = (sem(n) for n in (
            "y_centred", "y_squared", "gn_ms", "gn_sd", "y_done", "gate_ready"))
        f_prod, f_z, f_abs, f_ln, negc_ready, zeroed, bias_in = (sem(n) for n in (
            "f_prod", "f_z", "f_abs", "f_ln", "negc_ready", "zeroed", "bias_in"))
        logits, masked, maxed, expd, e_turned, pt_ready, av_prod, att_out = (sem(n) for n in (
            "logits", "masked", "maxed", "expd", "e_turned", "pt_ready", "av_prod", "att_out"))
        rope_swapped, rope_cos, roped = sem("rope_swapped"), sem("rope_cos"), sem("roped")
        rotated, scores, decayed, ret_prod, ret_ss, ret_ms, ret_sd, ret_out = (sem(n) for n in (
            "rotated", "scores", "decayed", "ret_prod", "ret_ss", "ret_ms", "ret_sd", "ret_out"))

        block = ctx.enter_context(nc.Block())

        def raw_full(u):
            return 16 * (u // RAW_RING + 1)

        @block.sync
        def _(sp):
            def load_unit(name, u, row):
                if u >= RAW_RING:
                    sp.wait_ge(lo_done, u - RAW_RING + 1)
                sp.dma_start(raw[:, u % RAW_RING].rearrange("p k n -> p (k n)"), a["w_" + name][row])\
                    .then_inc(raw_landed[u % RAW_RING], 16)

            for q in range(4):
                m, f = q % 2, q // 2
                sp.dma_start(X[:, m, f * UN:(f + 1) * UN], a["x"][:, m, f * UN:(f + 1) * UN]).then_inc(x_in[q], 16)
            sp.dma_start(vecs[:, :, :].rearrange("p v k -> p (v k)"), a["vecs"]).then_inc(vecs_in, 16)
            sp.dma_start(ident[:, :], a["ident"]).then_inc(ident_in, 16)
            load_unit("k", 0, 0)
            load_unit("k", 1, 1)
            for n, dst in (("w1", w1s), ("a1", a1s), ("g1", g1s)):
                sp.dma_start(dst.rearrange("p k n -> p (k n)"), a[n]).then_inc(lora_in, 16)
            for n, dst, k in (("w2", w2s, LORA), ("a2", a2s, LORA), ("g2a", g2a, P), ("g2b", g2b, GATE - P)):
                sp.dma_start(dst[0:k, :], a[n]).then_inc(lora_in, 16)
            for n in CONST_KEEP[1:-1]:
                sp.dma_start(keep[n][:, :], a[n]).then_inc(const_in, 16)
            for name, kt, nn in GEMMS:
                if kt:
                    for i in range(nn * kt // UK):
                        u = U0[name] + i
                        if name == "rwo" and i == 2:
                            sp.wait_ge(gn_ms, 4)
                        if name == "rwo" and i == 3:
                            sp.wait_ge(gate_ready, 4)
                        if u >= 2:
                            load_unit(name, u, i)
                    continue
                b = U0[name]
                for i in range(2):
                    load_unit(name, b + i, i)
                with sp.Fori(1, MLP_STEPS) as j:
                    for i in range(UK):
                        slot = (i - 2) % RAW_RING
                        sp.wait_ge(lo_done, j * 4 + (b - 2 + i - RAW_RING + 1))
                        sp.dma_start(raw[:, slot].rearrange("p k n -> p (k n)"),
                                     a["w_" + name][bass.ds(j * 4 + (i - 2), 1)].rearrange("u p n -> (u p) n"))\
                            .then_inc(raw_landed[slot], 16)
                for i in range(MLP_UNITS - 2, MLP_UNITS):
                    load_unit(name, b + i, i)
            for i in range(4):
                m, h = i % 2, i // 2
                sp.wait_ge(residual, 28 + i + 1)
                sp.dma_start(out[0, m * P:(m + 1) * P, h * UN:(h + 1) * UN], X[:, m, h * UN:(h + 1) * UN])\
                    .then_inc(out_done, 16)
            sp.wait_ge(out_done, 64)

        @block.scalar
        def _(act):
            done = [0]

            def hi_unit(u):
                act.wait_ge(raw_landed[u % RAW_RING], raw_full(u))
                if u >= SPLIT_RING:
                    act.wait_ge(unit_used, u - SPLIT_RING + 1)
                act.activation(whi[:, u % SPLIT_RING], raw[:, u % RAW_RING], ACT.Copy).then_inc(hi_done, 1)

            def hi_upto(n):
                while done[0] < min(n, UNITS):
                    hi_unit(done[0])
                    done[0] += 1

            def norm(name):
                n = NORM0[TI[name]]
                for q in range(4):
                    if RESIDUALS[name]:
                        act.wait_ge(residual, RESIDUALS[name] - 3 + q)
                    else:
                        act.wait_ge(x_in[q], 16)
                    if q >= 2:
                        act.wait_ge(ss_done, 4 * n + q - 1)
                    m, f = q % 2, q // 2
                    act.activation(JUNK[:, m], X[:, m, f * UN:(f + 1) * UN], ACT.Square,
                                   accum_out=norm_ss[:, m, f:f + 1]).then_inc(ss_done, 1)
                act.wait_ge(ms_done, n + 1)
                act.activation(norm_sd, norm_ms, ACT.Sqrt, scale=1.0 / D, bias=eps_col).then_inc(sd_done, 1)
                act.wait_ge(rstd_done, n + 1)
                for f in range(2):
                    s = slice(f * UN, (f + 1) * UN)
                    act.activation(XN[:, 1, s], X[:, 1, s], ACT.Copy, scale=norm_rstd[:, 1:2]).then_inc(xn_act, 1)

            def fetch(func):
                act.activation(small[:, 0:1], eps_col, func)

            def turn_hi(name, banks=None):
                i = TI[name]
                _, g, kt, _, half = TURNS[i]
                for b in banks or range(kt // 2):
                    act.wait_ge(turned, TURNED0[i] + b + 1)
                    src = bank_kt(4 + b % 4)
                    if g is None:
                        act.activation(XH[:, half * KT + 2 * b:half * KT + 2 * b + 2], src, ACT.Copy)\
                            .then_inc(turned_hi, 1)
                        continue
                    for j in range(2):
                        k = 2 * b + j
                        ins = act.activation(XH[:, half * KT + k], src[:, j], ACT.Copy, scale=gain(g, k))
                    ins.then_inc(turned_hi, 1)

            def read_chunk(name, n, put, ahead=False):
                g, kt = CHUNK0[name] + n, dict((q[0], q[1]) for q in GEMMS)[name]
                ue = U0[name] + (n + 1) * kt // UK
                hi_upto(ue + 1)
                act.wait_ge(unit_used, ue)
                if ahead:
                    hi_upto(ue + 2)
                for j in range(2):
                    put(n, j, psum[(g % 2) * 2 + j]).then_inc(acc_read["act"], 1)

            def by_feature(dst):
                return lambda n, j, b: act.activation(
                    dst[:, 4 * n + 2 * j:4 * n + 2 * j + 2], b[:, :].rearrange("p (a t) -> p a t", a=2), ACT.Copy)

            def by_token(dst, func=ACT.Copy):
                return lambda n, j, b: act.activation(dst[:, j, n * UN:(n + 1) * UN], b[:, :], func)

            def mlp(i):
                b, name = U0[f"mlp{i}"], f"mlp{i}"
                s0 = MLP_STEPS * i

                def relu(bank):
                    for m in range(MT):
                        act.activation(RELU[:, m], psum[bank + m][:, :], ACT.Relu).then_inc(relu_done, 1)

                def hidden_hi(q, k0=KT):
                    for k in range(2):
                        act.wait_ge(h_turned, 2 * q + k + 1)
                        act.activation(XH[:, k0 + 2 * k:k0 + 2 * k + 2], bank_kt(6 + k), ACT.Copy).then_inc(h_hi, 1)

                hi_upto(b + 3)
                act.wait_ge(unit_used, b + 2)
                relu(2)
                with act.Fori(1, MLP_STEPS) as j:
                    for n in range(1, UK + 1):
                        slot = (n - 2) % RAW_RING
                        act.wait_ge(raw_landed[slot], (j + (b // RAW_RING + (1 if n >= 2 else 0))) * 16)
                        act.wait_ge(unit_used, j * 4 + (b - 2 + n - SPLIT_RING + 1))
                        act.activation(whi[:, slot % SPLIT_RING], raw[:, slot], ACT.Copy).then_inc(hi_done, 1)
                        if n == 1:
                            hidden_hi(j + (s0 - 1))
                        if n == 3:
                            act.wait_ge(unit_used, j * 4 + b)
                            relu(0)
                done[0] = b + MLP_UNITS - 1
                hidden_hi(s0 + MLP_STEPS - 1, KT + 4)
                hi_upto(b + MLP_UNITS)

            def post_norm(i, u_of, bank0):
                for n in range(2):
                    if i == 2 and n == 1:
                        fetch(ACT.Sqrt)
                    hi_upto(u_of(n) + 1)
                    act.wait_ge(unit_used, u_of(n))
                    for m in range(MT):
                        if n:
                            act.wait_ge(pss_done, 4 * i + m + 1)
                        act.activation(JUNK[:, m], psum[bank0 + 2 * n + m][:, :], ACT.Square,
                                       accum_out=post_ss[:, m, n:n + 1]).then_inc(pss_done, 1)
                act.wait_ge(pms_done, i + 1)
                act.activation(post_sd, post_ms, ACT.Sqrt, scale=1.0 / D, bias=eps_col).then_inc(psd_done, 1)

            def head_squares(i, src):
                act.activation(KKSQ if i == 0 else fSQ, src, ACT.Square).then_inc(sq_ready, 1)

            def head_roots(i):
                act.wait_ge(sums_ms, i + 1)
                r = rn if i == 0 else frn
                act.activation(r, r, ACT.Sqrt).then_inc(sums_sd, 1)

            def attention(a0, heads, L, E, PT, name):
                for h in range(heads + 1):
                    if h < heads:
                        act.wait_ge(maxed, a0 + h + 1)
                        if h >= 2:
                            act.wait_ge(e_turned, a0 + h - 1)
                        for m in range(MT):
                            c0, c1 = (0, P) if m == 0 else (P, 3 * P)
                            ins = act.activation(E[:, h % 2, c0:c1], L[:, h % 2, c0:c1], ACT.Exp,
                                                 bias=att_nmax[:, h % 4, m:m + 1],
                                                 accum_out=att_sum[:, h % 16, m:m + 1])
                        ins.then_inc(expd, 1)
                    if h == 4:
                        hi_upto(U0[name] + 2)
                    if h >= 1:
                        g = h - 1
                        act.wait_ge(e_turned, a0 + g + 1)
                        if g >= 2:
                            act.wait_ge(av_prod, a0 + g - 1)
                        act.activation(PT[:, g % 2], psum[2 + g % 2][:, 0:384], ACT.Copy).then_inc(pt_ready, 1)

            act.wait_ge(vecs_in, 16)
            act.wait_ge(eps_ready, 1)
            norm("rwkv")
            hi_upto(1)
            for b in range(4):
                act.wait_ge(turned, b + 1)
                for j in range(2):
                    k = 2 * b + j
                    ins = act.activation(hT[:, k], bank_kt(4 + b)[:, j], ACT.Copy, scale=gain("rwkv_norm_g", k))
                ins.then_inc(hT_ready, 1)
            for b in range(4):
                if b == 2:
                    hi_upto(2)
                act.wait_ge(first_mixed, b + 1)
                act.activation(XH[:, 2 * b:2 * b + 2], XM[0][:, 2 * b:2 * b + 2], ACT.Copy).then_inc(first_hi, 1)

            def mix_to_hi(order, half):
                act.wait_ge(mixed, order)
                act.activation(XH[:, half * KT:(half + 1) * KT], XM[order % 2], ACT.Copy).then_inc(mix_hi, 1)

            hi_upto(3)
            mix_to_hi(2, 1)
            read_chunk("k", 0, by_feature(kT))
            act.wait_ge(lora1, 1)
            act.activation(tw[0:LORA, :], psum[4][0:LORA, 0:T], ACT.Tanh).then_inc(lora1_act, 1)
            read_chunk("k", 1, by_feature(kT))
            mix_to_hi(4, 0)
            act.wait_ge(lora1, 2)
            act.activation(ta[0:LORA, :], psum[5][0:LORA, 0:T], ACT.Copy).then_inc(lora1_act, 1)
            read_chunk("v", 0, by_token(V))
            act.wait_ge(lora1, 3)
            act.activation(sga, psum[6][:, 0:T], ACT.Sigmoid).then_inc(lora1_act, 1)
            act.activation(sgb[0:GATE - P, :], psum[7][0:GATE - P, 0:T], ACT.Sigmoid).then_inc(lora1_act, 1)
            hi_upto(U0["v"] + 4)
            for q, (dst, bias) in enumerate(((sT, "w0"), (aT, "a0"))):
                for b in range(4):
                    act.wait_ge(lora2, 4 * q + b + 1)
                    for j in range(2):
                        ins = act.activation(dst[:, 2 * b + j], bank_kt(4 + b)[:, j], ACT.Sigmoid,
                                             bias=gain(bias, 2 * b + j))
                    ins.then_inc(lora2_read, 1)
                if q == 0:
                    act.wait_ge(lora2_read, 4)
                    act.wait_ge(mix_lo, 2)
                    act.activation(lwT, sT, ACT.Copy, scale=-float(np.exp(-0.5))).then_inc(lw_ready, 1)
            hi_upto(U0["r"] + 1)
            act.wait_ge(centred, 1)
            act.activation(E1, Lx, ACT.Exp).then_inc(exps_ready, 1)
            act.activation(E2, Lx, ACT.Exp, scale=-1.0).then_inc(exps_ready, 1)
            act.activation(state_scale, state_scale, ACT.Exp).then_inc(scale_ready, 1)
            act.wait_ge(prepared, 1)
            head_squares(0, kkT)
            read_chunk("v", 1, by_token(V))
            for b in range(4):
                act.wait_ge(lora2, 8 + b + 1)
                act.activation(G[:, b // 2, (b % 2) * UN:(b % 2 + 1) * UN], psum[4 + b][:, :], ACT.Copy)\
                    .then_inc(lora2_read, 1)
            hi_upto(U0["r"] + 2)
            head_roots(0)
            read_chunk("r", 0, by_feature(rT))
            read_chunk("r", 1, by_feature(rT))
            hi_upto(U0["rwo"] + 2)

            def group_norm(r):
                act.wait_ge(y_centred, r + 1)
                act.activation(YQ, Y[:, r // 2, (r % 2) * UN:(r % 2 + 1) * UN], ACT.Square).then_inc(y_squared, 1)
                act.wait_ge(gn_ms, r + 1)
                act.activation(gn_var, gn_var, ACT.Sqrt).then_inc(gn_sd, 1)

            for r in range(4):
                c = r // 2
                for l in range(2):
                    gi = 2 * r + l
                    act.wait_ge(first_turned, gi + 1)
                    act.activation(TI_[l], psum[2 + l][:, :].rearrange("p (h s) -> p h s", h=4), ACT.Copy)\
                        .then_inc(inv_ready, 1)
                if r >= 1:
                    group_norm(r - 1)
                if r == 0:
                    act.wait_ge(bonus_sum, 1)
                    act.activation(bonus, psum[7][:, 0:32], ACT.Copy).then_inc(bonus_read, 1)
                for l in range(2):
                    act.wait_ge(rhs_prod, 2 * r + l + 1)
                    act.activation(SA[l], psum[6 + l][:, 0:256], ACT.Copy, scale=-1.0).then_inc(rhs_ready, 1)
                for l in range(2):
                    act.wait_ge(sa_prod, 2 * r + l + 1)
                    act.activation(SA[l], psum[6 + l][:, 0:256], ACT.Copy).then_inc(sa_ready, 1)
                for l in range(2):
                    q = (2 * r + l) % 4
                    act.wait_ge(y_prod, 2 * r + l + 1)
                    act.activation(Y[:, c, q * 256:(q + 1) * 256], psum[6 + l][:, 0:256], ACT.Copy)\
                        .then_inc(y_ready, 1)
                if c == 0:
                    for l in range(2):
                        act.wait_ge(keys_turned, 2 * r + l + 1)
                        act.activation(PM[l], psum[l][:, :].rearrange("p (h s) -> p h s", h=4), ACT.Copy)\
                            .then_inc(keys_ready, 1)
            turn_hi("rwo", (0, 1))
            group_norm(3)
            turn_hi("rwo", (2, 3))
            hi_upto(U0["rwo"] + 4 + 1)
            norm("mlp0")
            turn_hi("mlp0")
            mlp(0)
            hi_upto(U0["fk"] + 1)
            norm("kv")
            turn_hi("kv")
            turn_hi("attn")
            read_chunk("fk", 0, by_feature(fK))
            read_chunk("fk", 1, by_feature(fK))
            act.wait_ge(acc_read["act"], READ_COUNT[CHUNK0["fk"] + 1][1])
            head_squares(1, fK)
            read_chunk("fq", 0, by_feature(fQ))
            hi_upto(U0["fq"] + 4)
            head_roots(1)
            read_chunk("fq", 1, by_feature(fQ))
            act.wait_ge(acc_read["act"], READ_COUNT[CHUNK0["fq"] + 1][1])
            act.wait_ge(sums_ready, 2)
            head_squares(2, fQ)
            hi_upto(U0["fv"] + 2)
            read_chunk("fv", 0, by_token(fV))
            hi_upto(U0["fv"] + 4)
            head_roots(2)
            act.wait_ge(f_abs, 1)
            act.activation(fl[0:NH, :], fl[0:NH, :], ACT.Exp, scale=-1.0).then_inc(f_abs, 1)
            act.wait_ge(f_abs, 2)
            act.activation(fl[0:NH, :], fl[0:NH, :], ACT.Ln, bias=1.0).then_inc(f_ln, 1)
            fetch(ACT.Exp)
            read_chunk("fv", 1, by_token(fV))
            attention(0, NH, fL, fE, fPT, "fo")
            turn_hi("fo")
            hi_upto(U0["fo"] + 4 + 1)
            fetch(ACT.Sqrt)
            norm("mlp1")
            turn_hi("mlp1")
            mlp(1)
            hi_upto(U0["rq"] + 1)
            norm("ret")
            turn_hi("ret")
            hi_upto(U0["rv"])
            for n in range(4):
                read_chunk("rv", n, by_token(rV), True)
            for n in range(4):
                read_chunk("rg", n, by_token(rG, ACT.Silu), True)

            def head_rms(h):
                for m in range(MT):
                    act.wait_ge(ret_prod, 2 * h + m + 1)
                    act.activation(JUNK[:, m], psum[RET_BANK[h] + m][:, :], ACT.Square,
                                   accum_out=ret_sums[:, 2 * h + m:2 * h + m + 1]).then_inc(ret_ss, 1)
                act.wait_ge(ret_ms, h + 1)
                act.activation(ret_sums[:, 2 * h:2 * h + 2], ret_sums[:, 2 * h:2 * h + 2], ACT.Sqrt).then_inc(ret_sd, 1)

            fetch(ACT.Sqrt)
            hi_upto(U0["reo"] + 2)
            for h in range(3):
                head_rms(h)
            turn_hi("reo", (0, 1))
            head_rms(3)
            turn_hi("reo", range(2, 6))
            hi_upto(U0["reo"] + 3)
            turn_hi("reo", (6, 7))
            post_norm(0, lambda n: U0["reo"] + 4 * (n + 1), 0)
            norm("mlp2")
            turn_hi("mlp2")
            mlp(2)
            post_norm(1, lambda n: U0["mlp2"] + MLP_UNITS - 1 + n, 2)
            norm("moba")
            turn_hi("moba")
            read_chunk("mq", 0, by_feature(mQ))
            read_chunk("mq", 1, by_feature(mQ))
            read_chunk("mk", 0, by_feature(mK))
            read_chunk("mk", 1, by_feature(mK))
            read_chunk("mv", 0, by_token(mV))
            fetch(ACT.Exp)
            read_chunk("mv", 1, by_token(mV))
            attention(NH, MOBA_H, mL, mE, mPT, "mo")
            turn_hi("mo")
            post_norm(2, lambda n: U0["mo"] + 2 * (n + 1), 0)
            norm("mlp3")
            turn_hi("mlp3")
            mlp(3)
            post_norm(3, lambda n: U0["mlp3"] + MLP_UNITS - 1 + n, 2)

        @block.vector
        def _(dve):
            done = [0]
            steps = [0]

            def step(ins):
                steps[0] += 1
                ins.then_inc(dve_step, 1)
                dve.wait_ge(dve_step, steps[0])

            def lo_unit(u):
                dve.wait_ge(hi_done, u + 1)
                dve.tensor_tensor(wlo[:, u % SPLIT_RING], raw[:, u % RAW_RING],
                                  whi[:, u % SPLIT_RING].bitcast(F32), ALU.subtract).then_inc(lo_done, 1)

            def lo_upto(n):
                while done[0] < min(n, UNITS):
                    lo_unit(done[0])
                    done[0] += 1

            def norm(name):
                n = NORM0[TI[name]]
                dve.wait_ge(ss_done, 4 * (n + 1))
                dve.tensor_tensor(norm_ms, norm_ss[:, :, 0], norm_ss[:, :, 1], ALU.add).then_inc(ms_done, 1)
                dve.wait_ge(sd_done, n + 1)
                dve.reciprocal(norm_rstd, norm_sd).then_inc(rstd_done, 1)
                dve.wait_ge(rstd_done, n + 1)
                for f in range(2):
                    s = slice(f * UN, (f + 1) * UN)
                    dve.tensor_scalar(XN[:, 0, s], X[:, 0, s], norm_rstd[:, 0:1], None, ALU.mult).then_inc(xn_ready, 1)

            def turn_lo(name, banks=None):
                i = TI[name]
                _, g, kt, _, half = TURNS[i]
                for b in banks or range(kt // 2):
                    dve.wait_ge(turned_hi, SPLIT0[i] + b + 1)
                    src = bank_kt(4 + b % 4)
                    k = half * KT + 2 * b
                    if g is None:
                        dve.tensor_tensor(XL[:, k:k + 2], src, XH[:, k:k + 2].bitcast(F32), ALU.subtract)\
                            .then_inc(turned_lo, 1)
                        continue
                    for j in range(2):
                        ins = dve.scalar_tensor_tensor(XL[:, k + j], src[:, j], gain(g, 2 * b + j),
                                                       XH[:, k + j].bitcast(F32), ALU.mult, ALU.subtract)
                    ins.then_inc(turned_lo, 1)

            def residual_chunks(name):
                for n in range(2):
                    g, kt = CHUNK0[name] + n, 8
                    ue = U0[name] + (n + 1) * kt // UK
                    lo_upto(ue + 1)
                    dve.wait_ge(unit_used, ue)
                    for m in range(MT):
                        x = X[:, m, n * UN:(n + 1) * UN]
                        dve.tensor_tensor(x, x, psum[(g % 2) * 2 + m][:, :], ALU.add).then_inc(residual, 1)

            def mlp(i, plain):
                b = U0[f"mlp{i}"]
                s0 = MLP_STEPS * i

                def hidden_lo(q, k0=KT):
                    for k in range(2):
                        dve.wait_ge(h_hi, 2 * q + k + 1)
                        s = slice(k0 + 2 * k, k0 + 2 * k + 2)
                        dve.tensor_tensor(XL[:, s], bank_kt(6 + k), XH[:, s].bitcast(F32), ALU.subtract)\
                            .then_inc(h_lo, 1)

                lo_upto(b + 2)
                with dve.Fori(1, MLP_STEPS) as j:
                    for n in range(UK):
                        slot = (n - 2) % RAW_RING
                        dve.wait_ge(hi_done, j * 4 + (b - 2 + n + 1))
                        dve.tensor_tensor(wlo[:, slot % SPLIT_RING], raw[:, slot],
                                          whi[:, slot % SPLIT_RING].bitcast(F32), ALU.subtract).then_inc(lo_done, 1)
                        if n == 1:
                            hidden_lo(j + (s0 - 1))
                done[0] = b + MLP_UNITS - 2
                lo_upto(b + MLP_UNITS - 1)
                hidden_lo(s0 + MLP_STEPS - 1, KT + 4)
                lo_upto(b + MLP_UNITS)
                if plain:
                    lo_upto(b + MLP_UNITS + 1)
                    for n in range(2):
                        dve.wait_ge(unit_used, b + MLP_UNITS - 1 + n)
                        for m in range(MT):
                            x = X[:, m, n * UN:(n + 1) * UN]
                            dve.tensor_tensor(x, x, psum[2 + 2 * n + m][:, :], ALU.add).then_inc(residual, 1)

            def post_norm(i, ue, bank0, row):
                if i % 2 == 0:
                    dve.wait_ge(post_in, 16 * (i + 2))

                def gained(n, m):
                    dve.wait_ge(pss_done, 4 * i + 2 * n + m + 1)
                    dve.tensor_tensor(PTMP[:, n, m], psum[bank0 + 2 * n + m][:, :], POST[:, row, n * UN:(n + 1) * UN],
                                      ALU.mult).then_inc(ptmp_done, 1)

                lo_upto(ue)
                gained(0, 0)
                gained(0, 1)
                lo_upto(ue + 1)
                gained(1, 0)
                dve.wait_ge(pss_done, 4 * (i + 1))
                dve.tensor_tensor(post_ms, post_ss[:, :, 0], post_ss[:, :, 1], ALU.add).then_inc(pms_done, 1)
                gained(1, 1)
                dve.wait_ge(psd_done, i + 1)
                step(dve.reciprocal(post_rstd, post_sd))
                dve.wait_ge(ptmp_done, 4 * (i + 1))
                for n in range(2):
                    for m in range(MT):
                        x = X[:, m, n * UN:(n + 1) * UN]
                        dve.scalar_tensor_tensor(x, PTMP[:, n, m], post_rstd[:, m:m + 1], x, ALU.mult, ALU.add)\
                            .then_inc(residual, 1)
                dve.wait_ge(residual, RESIDUALS_AFTER_POST[i])

            def head_sums(i, scale, eps):
                r = rn if i == 0 else frn
                dve.wait_ge(sums_ready, i + 1)
                dve.tensor_scalar(r, psum[4][:, 0:T], scale, eps, ALU.mult, ALU.add).then_inc(sums_ms, 1)
                dve.wait_ge(sums_sd, i + 1)
                if i == 0:
                    step(dve.tensor_scalar(r, r, 1e-12, None, ALU.max))
                dve.reciprocal(r, r).then_inc(rn_ready, 1)

            def att_norm(a0, g, dh, O):
                per = 512 // (MT * dh)
                h0, h1 = g * per, (g + 1) * per
                dve.wait_ge(expd, a0 + h1)
                s = att_sum[:, h0:h1]
                step(dve.reciprocal(s, s))
                dve.wait_ge(av_prod, a0 + h1)
                src = psum[6 + g % 2][:, :].rearrange("p (h m d) -> p m h d", h=per, m=MT)
                for m in range(MT):
                    ins = dve.tensor_tensor(
                        O[:, m, h0 * dh:h1 * dh].rearrange("p (h d) -> p h d", h=per), src[:, m],
                        s[:, :, m:m + 1].broadcast_to((P, per, dh)), ALU.mult)
                ins.then_inc(att_out, 1)

            def attention(a0, heads, scale, L, CAUSAL, dh, O, name):
                per = 512 // (MT * dh)
                for h in range(heads + 4):
                    if h < heads:
                        dve.wait_ge(logits, a0 + h + 1)
                        if h >= 2:
                            dve.wait_ge(expd, a0 + h - 1)
                        dve.scalar_tensor_tensor(L[:, h % 2], psum[h % 2][:, 0:384], scale, CAUSAL,
                                                 ALU.mult, ALU.add).then_inc(masked, 1)
                        dve.wait_ge(masked, a0 + h + 1)
                        for m in range(MT):
                            c0, c1 = (0, P) if m == 0 else (P, 3 * P)
                            ins = dve.tensor_reduce(att_nmax[:, h % 4, m:m + 1], L[:, h % 2, c0:c1], AXX, ALU.max,
                                                    negate=True)
                        ins.then_inc(maxed, 1)
                    if h == 5:
                        lo_upto(U0[name] + 2)
                    g = h - 4
                    if 0 <= g < heads - 1 and g % per == per - 1:
                        att_norm(a0, g // per, dh, O)
                turn_lo(name, (0, 1))
                att_norm(a0, 3, dh, O)
                turn_lo(name, (2, 3))

            dve.memset(eps_col, NORM_EPS).then_inc(eps_ready, 1)
            norm("rwkv")
            lo_upto(1)

            def mix_tiles(order, mu, ks):
                for k in ks:
                    ins = dve.scalar_tensor_tensor(XM[order % 2][:, k], xxT[:, k], gain(f"mu{mu}", k), hT[:, k],
                                                   ALU.mult, ALU.add)
                return ins

            def mix(order, mu):
                mix_tiles(order, mu, range(KT)).then_inc(mixed, 1)

            def mix_to_lo(j, order, half):
                dve.wait_ge(mix_hi, j)
                s = slice(half * KT, (half + 1) * KT)
                dve.tensor_tensor(XL[:, s], XM[order % 2], XH[:, s].bitcast(F32), ALU.subtract).then_inc(mix_lo, 1)

            def first_to_lo(b):
                dve.wait_ge(first_hi, b + 1)
                s = slice(2 * b, 2 * b + 2)
                dve.tensor_tensor(XL[:, s], XM[0][:, s], XH[:, s].bitcast(F32), ALU.subtract).then_inc(first_lo, 1)

            for b in range(4):
                s = slice(2 * b, 2 * b + 2)
                dve.wait_ge(hT_ready, b + 1)
                dve.tensor_tensor(xxT[:, s, 1:T], hT[:, s, 0:T - 1], hT[:, s, 1:T], ALU.subtract)
                step(dve.tensor_scalar(xxT[:, s, 0:1], hT[:, s, 0:1], -1.0, None, ALU.mult))
                mix_tiles(0, 2, range(2 * b, 2 * b + 2)).then_inc(first_mixed, 1)
                if b >= 1:
                    first_to_lo(b - 1)
            lo_upto(2)
            first_to_lo(3)
            mix(1, 1)
            lo_upto(3)
            dve.wait_ge(first_lo, 4)
            mix(2, 3)
            mix_to_lo(1, 2, 1)
            lo_upto(4)
            dve.wait_ge(lora1, 1)
            mix(3, 4)
            lo_upto(5)
            dve.wait_ge(mix_lo, 1)
            mix(4, 0)
            lo_upto(6)
            dve.wait_ge(lora1, 2)
            mix(5, 5)
            mix_to_lo(2, 4, 0)
            lo_upto(8)
            dve.wait_ge(mix_lo, 2)
            dve.wait_ge(lw_ready, 1)
            dve.memset(Lx[:, :, 0:1], 0.0)
            step(dve.memset(ones, 1.0))
            lw16 = lwT.rearrange("p k (c t) -> p (k c) t", c=2)
            for q in range(2 * KT):
                ins = dve.tensor_tensor_scan(Lx[:, q, 1:LW], ones, lw16[:, q], 0.0, ALU.mult, ALU.add)
            step(ins)
            Lc = Lx.rearrange("p (k c) t -> p k c t", c=2)
            step(dve.tensor_copy(mids, Lx[:, :, HD:HD + 1]))
            mid2 = mids.rearrange("p (k c) o -> p k (c o)", c=2)
            step(dve.tensor_tensor(state_scale, Lc[:, :, 0, P], mid2[:, :, 0], ALU.subtract))
            step(dve.tensor_tensor(state_scale, state_scale, mid2[:, :, 1], ALU.add))
            dve.tensor_tensor(Lx, Lx, mids.broadcast_to((P, 2 * KT, LW)), ALU.subtract).then_inc(centred, 1)
            dve.wait_ge(lora2, 8)
            for p in range(KT):
                ins = dve.tensor_scalar(kkT[:, p], kT[:, p], gain("k_k", p), None, ALU.mult)
            ins.then_inc(prepared, 1)
            lo_upto(9)
            dve.wait_ge(lora2_read, 8)
            dve.wait_ge(lora2, 12)
            for p in range(KT):
                ins = dve.tensor_scalar(sqT[:, p], aT[:, p], 1.0, gain("k_a", p), ALU.subtract, ALU.mult)
            step(ins)
            lo_upto(10)
            head_sums(0, 1.0, 0.0)
            dve.scalar_tensor_tensor(kT, sqT, 1.0, kT, ALU.add, ALU.mult).then_inc(prepared, 1)
            lo_upto(11)
            for b in range(4):
                dve.wait_ge(rn_spread, b + 1)
                k2 = kkT[:, 2 * b:2 * b + 2]
                ins = dve.tensor_tensor(k2, k2, bank_kt(4 + b), ALU.mult)
                ins.then_inc(spread_read, 1)
            dve.wait_ge(spread_read, 4)
            lo_upto(12)
            dve.wait_ge(exps_ready, 2)
            kk16 = kkT.rearrange("p k (c t) -> p (k c) t", c=2)
            r16 = rT.rearrange("p k (c t) -> p (k c) t", c=2)
            b16 = BE.rearrange("p k (c t) -> p (k c) t", c=2)
            step(dve.tensor_tensor(aT, kkT, aT, ALU.mult))
            dve.tensor_tensor(b16, b16, E2[:, :, 1:LW], ALU.mult).then_inc(prepared, 1)
            dve.tensor_tensor(AR[:, :, 0], kk16, E1[:, :, 0:P], ALU.mult)
            for n in range(2):
                dve.wait_ge(acc_read["act"], READ_COUNT[CHUNK0["r"] + n][1])
                q = slice(n * KT, (n + 1) * KT)
                dve.tensor_tensor(AR[:, q, 1], r16[:, q], E1[:, q, 1:LW], ALU.mult).then_inc(rho_ready, 1)
            dve.wait_ge(rho_ready, 2)
            for blk in range(4):
                ins = dve.memset(M[0][HD:P, :, blk * P:blk * P + HD], 0.0)
            step(ins)
            dve.wait_ge(scale_ready, 1)
            dve.wait_ge(const_in, 16 * (len(CONST_KEEP) - 2))
            first4 = keep["first_mask"][:, :].unsqueeze(1).broadcast_to((P, 4, P))
            ident4 = ident[:, :].unsqueeze(1).broadcast_to((P, 4, P))
            pm = keep["pair_masks"]

            def group_norm(r, part):
                y2 = Y[:, r // 2, (r % 2) * UN:(r % 2 + 1) * UN]
                y = y2.rearrange("p (h d) -> p h d", h=8)
                if part == 0:
                    dve.wait_ge(y_ready, 2 * r + 2)
                    step(dve.tensor_reduce(gn_mean, y, AXX, ALU.add))
                    step(dve.tensor_scalar(gn_mean, gn_mean, 1.0 / HD, None, ALU.mult))
                elif part == 1:
                    dve.tensor_tensor(y, y, gn_mean.unsqueeze(2).broadcast_to((P, 8, HD)), ALU.subtract)\
                        .then_inc(y_centred, 1)
                elif part == 2:
                    dve.wait_ge(y_squared, r + 1)
                    step(dve.tensor_reduce(gn_var, YQ.rearrange("p (h d) -> p h d", h=8), AXX, ALU.add))
                    dve.tensor_scalar(gn_var, gn_var, 1.0 / HD, GN_EPS, ALU.mult, ALU.add).then_inc(gn_ms, 1)
                elif part == 3:
                    dve.wait_ge(gn_sd, r + 1)
                    step(dve.reciprocal(gn_var, gn_var))
                    step(dve.tensor_tensor(y, y, gn_var.unsqueeze(2).broadcast_to((P, 8, HD)), ALU.mult))
                elif part == 4:
                    dve.wait_ge(gate_ready, r + 1)
                    step(dve.tensor_tensor(y2, y2, G[:, r // 2, (r % 2) * UN:(r % 2 + 1) * UN], ALU.mult))
                else:
                    dve.tensor_tensor(y2, y2, V[:, r // 2, (r % 2) * UN:(r % 2 + 1) * UN], ALU.add)\
                        .then_inc(y_done, 1)

            for r in range(4):
                c = r // 2
                for l in range(2):
                    gi = 2 * r + l
                    if gi == 1:
                        dve.wait_ge(cleared, 4)
                    for h in range(4):
                        b = psum[4 * l + h]
                        dve.wait_ge(pair_prod, 4 * gi + h + 1)
                        dve.tensor_tensor(M[l][0:HD, h], b[0:HD, :], pm[0:HD, :], ALU.mult)
                        dve.tensor_tensor(M[l][HD:P, h].rearrange("p (b t) -> p b t", b=4)[:, :, HD:P],
                                          b[HD:P, :].rearrange("p (b t) -> p b t", b=4)[:, :, HD:P],
                                          pm[HD:P, :].rearrange("p (b t) -> p b t", b=4)[:, :, HD:P],
                                          ALU.mult).then_inc(pair_masked, 1)
                    dve.wait_ge(pair_masked, 4 * gi + 4)
                    step(dve.tensor_tensor(TT_[l], M[l][:, :, 0:P], first4, ALU.mult))
                    dve.tensor_tensor(TT_[l], TT_[l], ident4, ALU.add).then_inc(first_ready, 1)
                if r == 0:
                    lo_upto(U0["rwo"] + 2)
                for i in range(6):
                    lm = keep["level_masks"][:, i * P:(i + 1) * P].unsqueeze(1).broadcast_to((P, 4, P))
                    for l in range(2):
                        n = 12 * r + 2 * i + l
                        dve.wait_ge(half_prod, n + 1)
                        dve.tensor_tensor(PM[l], psum[l][:, :].rearrange("p (h s) -> p h s", h=4), lm, ALU.mult)\
                            .then_inc(half_masked, 1)
                    if r >= 1:
                        group_norm(r - 1, i)
                    elif i == 0:
                        dve.wait_ge(kappa_ready, 1)
                        dve.wait_ge(lo_done, U0["rwo"])
                        for p in range(KT):
                            ins = dve.scalar_tensor_tensor(BONUS[:, p].rearrange("p (c t) -> p c t", c=2),
                                                           AR[:, 2 * p:2 * p + 2, 1], gain("r_k", p),
                                                           k16[:, 2 * p:2 * p + 2], ALU.mult, ALU.mult)
                        ins.then_inc(bonus_prod, 1)
                    for l in range(2):
                        n = 12 * r + 2 * i + l
                        if i < 5:
                            dve.wait_ge(inv_prod, 10 * r + 2 * i + l + 1)
                            dve.tensor_tensor(TI_[l], TI_[l], psum[2 + l][:, :].rearrange("p (h s) -> p h s", h=4),
                                              ALU.subtract).then_inc(inv_doubled, 1)
                        dve.wait_ge(step_prod, n + 1)
                        dve.tensor_tensor(TT_[l], TT_[l], psum[4 + l][:, :].rearrange("p (h s) -> p h s", h=4),
                                          ALU.subtract).then_inc(doubled, 1)
                if c == 0:
                    for l in range(2):
                        p0 = 2 * (2 * r + l)
                        dve.wait_ge(state_prod, 2 * r + l + 1)
                        for pp in range(2):
                            dve.scalar_tensor_tensor(S0[:, p0 + pp], psum[2 + l][:, pp * P:(pp + 1) * P],
                                                     state_scale[:, p0 + pp:p0 + pp + 1], keep["head_blocks"][:, :],
                                                     ALU.mult, ALU.mult).then_inc(state_ready, 1)
            for part in range(3):
                group_norm(3, part)
            turn_lo("rwo", (0, 1))
            for part in range(3, 6):
                group_norm(3, part)
            turn_lo("rwo", (2, 3))
            residual_chunks("rwo")
            norm("mlp0")
            turn_lo("mlp0")
            mlp(0, True)
            norm("kv")
            turn_lo("kv")
            turn_lo("attn")
            lo_upto(U0["fq"] + 4)
            head_sums(1, 1.0 / HD, NORM_EPS)
            lo_upto(U0["fv"] + 2)
            dve.wait_ge(zeroed, 1)
            for b in range(4):
                dve.wait_ge(rn_spread, 4 + b + 1)
                for j in range(2):
                    p = 2 * b + j
                    for f in range(2):
                        s = slice(f * HD, (f + 1) * HD)
                        ins = dve.scalar_tensor_tensor(fKP[s, 2 * p + f], bank_kt(4 + b)[s, j],
                                                       gain("k_norm_g", p)[s], fK[s, p], ALU.mult, ALU.mult)
                ins.then_inc(spread_read, 1)
            lo_upto(U0["fv"] + 4)
            head_sums(2, 1.0 / HD, NORM_EPS)
            dve.wait_ge(f_prod, 1)
            dve.wait_ge(fox_in, 16 * 3)
            dve.tensor_scalar(fz[0:NH, :], psum[5][0:NH, 0:T], fbias[0:NH, :], None, ALU.add).then_inc(f_z, 1)
            dve.wait_ge(f_z, 1)
            dve.scalar_tensor_tensor(fl[0:NH, :], fz[0:NH, :], -1.0, fz[0:NH, :], ALU.mult, ALU.max)\
                .then_inc(f_abs, 1)
            for b in range(4):
                dve.wait_ge(rn_spread, 8 + b + 1)
                for j in range(2):
                    p = 2 * b + j
                    for f in (1, 0):
                        s = slice(f * HD, (f + 1) * HD)
                        ins = dve.scalar_tensor_tensor(fQ2[f][s, p], bank_kt(4 + b)[s, j],
                                                       gain("q_norm_g", p)[s], fQ[s, p], ALU.mult, ALU.mult)
                ins.then_inc(spread_read, 1)
            dve.wait_ge(f_ln, 1)
            step(dve.scalar_tensor_tensor(fz[0:NH, :], fz[0:NH, :], 0.0, fl[0:NH, :], ALU.min, ALU.subtract))
            step(dve.memset(fl, 1.0))
            step(dve.tensor_tensor_scan(fc[0:NH, :], fl[0:NH, :], fz[0:NH, :], 0.0, ALU.mult, ALU.add))
            dve.tensor_scalar(negc[0:NH, :], fc[0:NH, :], -8.0, None, ALU.mult).then_inc(negc_ready, 1)
            lo_upto(U0["fo"] + 1)
            attention(0, NH, 1.0 / 8, fL, fCAUSAL, HD, fO, "fo")
            residual_chunks("fo")
            norm("mlp1")
            turn_lo("mlp1")
            mlp(1, True)
            norm("ret")
            turn_lo("ret")
            dve.wait_ge(ret_in, 16 * 3)
            cos2 = rCOS.unsqueeze(1).broadcast_to((P, 2, T))
            sin2 = rSIN.unsqueeze(1).broadcast_to((P, 2, T))
            for i, (name, dst) in enumerate((("rq", rQ), ("rk", rK))):
                for n in range(2):
                    g = CHUNK0[name] + n
                    ue = U0[name] + 2 * (n + 1)
                    lo_upto(ue + 1)
                    dve.wait_ge(unit_used, ue)
                    for j in range(2):
                        h, s = 2 * n + j, j
                        src = bank_kt((g % 2) * 2 + j)
                        dve.tensor_tensor(rA[s], src, cos2, ALU.mult)
                        ins = dve.tensor_tensor(rB[s], src, sin2, ALU.mult)
                        ins.then_inc(acc_read["dve"], 1)
                        dve.wait_ge(acc_read["dve"], READ_COUNT[g][1] - 1 + j)
                        dve.tensor_tensor(dst[:, h, 0], rA[s][:, 0], rB[s][:, 1], ALU.subtract)
                        dve.tensor_tensor(dst[:, h, 1], rB[s][:, 0], rA[s][:, 1], ALU.add).then_inc(rotated, 1)
                        if j == 0:
                            lo_upto(ue + 2)
            lo_upto(U0["reo"])

            def decay(h):
                dve.wait_ge(scores, h + 1)
                if h >= 2:
                    dve.wait_ge(ret_prod, 2 * (h - 1))
                d = rDEC[:, h]
                dve.tensor_tensor(rPT[:, h % 2, 0:T], psum[h][:, 0:T], d, ALU.mult)
                dve.tensor_tensor(rPT[:, h % 2, T:T + P], psum[h][:, T:T + P], d[:, 0:P], ALU.mult)\
                    .then_inc(decayed, 1)

            def head_norm(h):
                dve.wait_ge(ret_ss, 2 * h + 2)
                s = ret_sums[:, 2 * h:2 * h + 2]
                dve.tensor_scalar(s, s, 1.0 / RET_DV, NORM_EPS, ALU.mult, ALU.add).then_inc(ret_ms, 1)
                dve.wait_ge(ret_sd, h + 1)
                step(dve.reciprocal(s, s))
                if h == 0:
                    dve.wait_ge(acc_read["act"], READ_COUNT[CHUNK0["rg"] + 3][1])
                for m in range(MT):
                    gt = rG[:, m, h * RET_DV:(h + 1) * RET_DV]
                    dve.scalar_tensor_tensor(gt, psum[RET_BANK[h] + m][:, :], s[:, m:m + 1], gt, ALU.mult,
                                             ALU.mult).then_inc(ret_out, 1)

            decay(0)
            for h in range(3):
                decay(h + 1)
                if h == 0:
                    lo_upto(U0["reo"] + 2)
                head_norm(h)
            turn_lo("reo", (0, 1))
            head_norm(3)
            turn_lo("reo", range(2, 6))
            lo_upto(U0["reo"] + 3)
            turn_lo("reo", (6, 7))
            post_norm(0, U0["reo"] + 8, 0, 0)
            norm("mlp2")
            turn_lo("mlp2")
            mlp(2, False)
            post_norm(1, U0["mlp2"] + MLP_UNITS, 2, 1)
            norm("moba")
            turn_lo("moba")
            dve.wait_ge(moba_in, 16 * 4)

            def rope(i, name, src, b):
                s = slice(2 * b, 2 * b + 2)
                x = src[0:ROPE, s]
                dve.wait_ge(acc_read["act"], READ_COUNT[CHUNK0[name] + 1][1])
                dve.wait_ge(rope_swapped, 4 * i + b + 1)
                step(dve.tensor_tensor(mTMP[0:ROPE], bank_kt(4 + b)[0:ROPE],
                                       mSIN[0:ROPE].unsqueeze(1).broadcast_to((ROPE, 2, T)), ALU.mult))
                step(dve.tensor_tensor(mTMP2[0:ROPE], x, mCOS[0:ROPE].unsqueeze(1).broadcast_to((ROPE, 2, T)),
                                       ALU.mult))
                dve.tensor_tensor(x, mTMP[0:ROPE], mTMP2[0:ROPE], ALU.add).then_inc(roped, 1)
                dve.wait_ge(roped, 4 * i + b + 1)

            for i, (name, src, after) in enumerate((("mq", mQ, "mk"), ("mk", mK, "mv"))):
                lo_upto(U0[after] + 3)
                rope(i, name, src, 0)
                rope(i, name, src, 1)
                lo_upto(U0[after] + 4)
                rope(i, name, src, 2)
                rope(i, name, src, 3)
            lo_upto(U0["mo"] + 1)
            attention(NH, MOBA_H, MOBA_D ** -0.5, mL, mCAUSAL, MOBA_D, mO, "mo")
            post_norm(2, U0["mo"] + 4, 0, 0)
            norm("mlp3")
            turn_lo("mlp3")
            mlp(3, False)
            post_norm(3, U0["mlp3"] + MLP_UNITS, 2, 1)

        @block.gpsimd
        def _(pool):
            def squares(i):
                s0 = MLP_STEPS * i

                def one(q):
                    for m in range(MT):
                        pool.wait_ge(relu_done, 2 * q + m + 1)
                        pool.tensor_tensor(RELU[:, m], RELU[:, m], RELU[:, m], ALU.mult).then_inc(square_done, 1)

                with pool.Fori(0, MLP_STEPS) as j:
                    one(j + s0)

            pool.wait_ge(const_in, 16 * (len(CONST_KEEP) - 2))
            pool.wait_ge(lora2, 12)
            pool.dma_start(SPREAD.rearrange("p k f -> p (k f)"), a["head_spread"]).then_inc(spread_in, 16)
            pool.wait_ge(prepared, 2)
            pool.wait_ge(exps_ready, 2)
            pool.tensor_tensor(k16, k16, E2[:, :, 1:LW], ALU.mult).then_inc(kappa_ready, 1)
            pool.wait_ge(kappa_ready, 1)
            pool.wait_ge(prepared, 3)
            def pads(gi):
                c, p0 = gi // 4, 2 * (gi % 4)
                if gi >= 2:
                    pool.wait_ge(pair_prod, 4 * (gi - 1))
                for s, src in enumerate((BE, kT)):
                    for f in range(2):
                        pool.tensor_scalar(PADS[c][gi % 2][:, s].rearrange("p (q f) t -> p f q t", f=2)[:, f],
                                           src[:, p0:p0 + 2, c * P:(c + 1) * P], keep["head_halves"][:, f:f + 1], 1.0,
                                           ALU.mult, ALU.mult).then_inc(padded, 1)

            def gate(r):
                c, cols, n = r // 2, slice((r % 2) * UN, (r % 2 + 1) * UN), 3 * r
                v, gt = V[:, c, cols], G[:, c, cols]
                v3 = v.rearrange("p (h d) -> p h d", h=8)
                bs = bonus[:, c * NH + (r % 2) * 8:c * NH + (r % 2) * 8 + 8]
                pool.wait_ge(y_prod, 2 * r + 2)
                if c == 0:
                    pool.wait_ge(state_prod, 2 * r + 2)
                pool.tensor_tensor(v3, v3, bs.unsqueeze(2).broadcast_to((P, 8, HD)), ALU.mult).then_inc(pool_step, 1)
                pool.wait_ge(pool_step, n + 1)
                pool.tensor_tensor(v, v, LNROW[:, 1, cols], ALU.add).then_inc(pool_step, 1)
                pool.wait_ge(pool_step, n + 2)
                pool.tensor_tensor(v, v, gt, ALU.mult).then_inc(pool_step, 1)
                pool.wait_ge(pool_step, n + 3)
                pool.tensor_tensor(gt, gt, LNROW[:, 0, cols], ALU.mult).then_inc(gate_ready, 1)

            pads(0)
            pool.wait_ge(rho_ready, 2)
            pads(1)
            for blk in range(4):
                pool.memset(M[1][:, :, blk * P:blk * P + HD], 0.0).then_inc(cleared, 1)
            pool.wait_ge(lo_done, U0["rwo"])
            for i in range(2):
                pool.dma_start(LNROW[:, i], a[ROWS[i]].partition_broadcast(P)).then_inc(lnrow_in, 16)
            pool.wait_ge(bonus_read, 1)
            pool.wait_ge(lnrow_in, 32)
            for r in range(4):
                if r < 3:
                    pads(2 * r + 2)
                    pads(2 * r + 3)
                gate(r)
            squares(0)
            pool.dma_start(wf.rearrange("p k n -> p (k n)"), a["wf"]).then_inc(fox_in, 16)
            pool.dma_start(fbias[0:NH, :], a["f_bias"]).then_inc(fox_in, 16)
            pool.dma_start(fCAUSAL, a["causal"]).then_inc(fox_in, 16)
            pool.dma_start(SPREAD.rearrange("p k f -> p (k f)"), a["head_spread"]).then_inc(spread_in, 16)
            pool.wait_ge(h_lo, 2 * MLP_STEPS)
            pool.memset(fKP, 0.0).then_inc(zeroed, 1)
            pool.wait_ge(spread_read, 12)
            for f in range(2):
                pool.dma_start(fQ2[f][HD * (1 - f):HD * (1 - f) + 1].rearrange("p k t -> p (k t)"), a["ones_row"])\
                    .then_inc(bias_in, 16)
            pool.wait_ge(negc_ready, 1)
            for f in range(2):
                pool.dma_start(fKP[HD * (1 - f):HD * (1 - f) + 1, f:NH:2, :], negc[8 * f:8 * f + 8, :])\
                    .then_inc(bias_in, 16)
            squares(1)
            for n, dst in (("ret_decay", at(0, RET_H * T)), ("ret_cos", rCOS), ("ret_sin", rSIN)):
                pool.dma_start(dst, a[n]).then_inc(ret_in, 16)
            for i in range(2):
                pool.dma_start(POST[:, i], a[ROWS[2 + i]].partition_broadcast(P)).then_inc(post_in, 16)
            squares(2)
            for n, dst, k in (("rope_cos", mCOS, ROPE), ("rope_sin", mSIN, ROPE), ("rope_swap", mSWAP, P),
                              ("causal", mCAUSAL, P)):
                pool.dma_start(dst[0:k], a[n]).then_inc(moba_in, 16)
            pool.wait_ge(residual, 24)
            for i in range(2):
                pool.dma_start(POST[:, i], a[ROWS[4 + i]].partition_broadcast(P)).then_inc(post_in, 16)
            squares(3)

        @block.tensor
        def _(pe):
            def turn(name, src, banks=None):
                i = TI[name]
                kt = TURNS[i][2]
                for b in banks or range(kt // 2):
                    if b >= 4:
                        pe.wait_ge(turned_lo, SPLIT0[i] + b - 3)
                    for j in range(2):
                        for m in range(MT):
                            k = 2 * b + j
                            ins = pe.transpose(psum[4 + b % 4][:, j * T + m * P:j * T + (m + 1) * P],
                                               src[:, m, k * P:(k + 1) * P], ident[:, :])
                    ins.then_inc(turned, 1)

            def norm_turn(name):
                for f in range(2):
                    pe.wait_ge(xn_ready, 2 * NORM0[TI[name]] + f + 1)
                    pe.wait_ge(xn_act, 2 * NORM0[TI[name]] + f + 1)
                    turn(name, XN, (2 * f, 2 * f + 1))

            def passes(out_, x, w, xs, ws, start, stop_=False):
                (xh, xl), (wh, wl) = x, w
                pe.matmul(out_, xh[xs], wh[ws], start=start, stop=False)
                pe.matmul(out_, xh[xs], wl[ws], start=False, stop=False)
                return pe.matmul(out_, xl[xs], wh[ws], start=False, stop=stop_)

            def chunk(name, n, form, half=0, kts=KT, ready=None):
                g = CHUNK0[name] + n
                if g >= 2 and READ_COUNT[g - 2][0] != "sum":
                    who, c = READ_COUNT[g - 2]
                    pe.wait_ge(acc_read[who], c)
                for kg in range(kts // UK):
                    u = U0[name] + n * (kts // UK) + kg
                    pe.wait_ge(lo_done, u + 1)
                    s = u % SPLIT_RING
                    for k in range(UK):
                        kt = kg * UK + k
                        if ready is not None and n == 0 and kt % 2 == 0:
                            ready(kt // 2)
                        first, last = kt == 0, kt == kts - 1
                        x = half * KT + kt
                        if form == "token":
                            for m in range(MT):
                                ins = passes(psum[(g % 2) * 2 + m][:, :], (XH, XL), (whi, wlo),
                                             (slice(None), x, slice(m * P, (m + 1) * P)),
                                             (slice(None), s, k), first, last)
                        else:
                            for f in range(UK):
                                o = psum[(g % 2) * 2 + f // 2][:, (f % 2) * T:(f % 2 + 1) * T]
                                ins = passes(o, (whi, wlo), (XH, XL),
                                             (slice(None), s, k, slice(f * P, (f + 1) * P)),
                                             (slice(None), x), first and f % 2 == 0, last and f % 2 == 1)
                    ins.then_inc(unit_used, 1)

            def split_ready(name):
                return lambda b: pe.wait_ge(turned_lo, SPLIT0[TI[name]] + b + 1)

            def mlp(i):
                b, name = U0[f"mlp{i}"], f"mlp{i}"
                s0 = MLP_STEPS * i

                def up(u, bank, kg, ready=False):
                    for k in range(UK):
                        kt = kg * UK + k
                        if ready and kt % 2 == 0:
                            pe.wait_ge(turned_lo, SPLIT0[TI[name]] + kt // 2 + 1)
                        for m in range(MT):
                            ins = passes(psum[bank + m][:, :], (XH, XL), (whi, wlo),
                                         (slice(None), kt, slice(m * P, (m + 1) * P)), (slice(None), u, k),
                                         kt == 0, kt == KT - 1)
                    ins.then_inc(unit_used, 1)

                def hidden_turn(q):
                    pe.wait_ge(square_done, q * 2 + 2)
                    for k in range(2):
                        for j in range(2):
                            for m in range(MT):
                                f = 2 * k + j
                                ins = pe.transpose(psum[6 + k][:, j * T + m * P:j * T + (m + 1) * P],
                                                   RELU[:, m, f * P:(f + 1) * P], ident[:, :])
                        ins.then_inc(h_turned, 1)

                def down(u, n, first, last, k0=KT):
                    for k in range(UK):
                        for m in range(MT):
                            ins = passes(psum[2 + 2 * n + m][:, :], (XH, XL), (whi, wlo),
                                         (slice(None), k0 + k, slice(m * P, (m + 1) * P)), (slice(None), u, k),
                                         first and k == 0, last and k == UK - 1)
                    ins.then_inc(unit_used, 1)

                for kg in range(2):
                    pe.wait_ge(lo_done, b + kg + 1)
                    up(kg, 2, kg, True)

                def body(j, first=False, last=False):
                    if not first:
                        pe.wait_ge(relu_done, (j + s0) * 2)
                    pe.wait_ge(lo_done, j * 4 + (b - 1))
                    up(0, 0, 0)
                    hidden_turn(j + (s0 - 1))
                    pe.wait_ge(lo_done, j * 4 + b)
                    up(1, 0, 1)
                    pe.wait_ge(h_lo, (j + s0) * 2)
                    for n in range(2):
                        pe.wait_ge(lo_done, j * 4 + (b + n + 1))
                        if last and n == 1:
                            hidden_turn(q_last)
                        down(n, n, first, False)

                q_last = s0 + MLP_STEPS - 1
                body(1, first=True)
                with pe.Fori(2, MLP_STEPS - 1) as j:
                    body(j)
                body(MLP_STEPS - 1, last=True)
                pe.wait_ge(h_lo, 2 * (q_last + 1))
                for n in range(2):
                    pe.wait_ge(lo_done, b + MLP_UNITS - 1 + n)
                    down(n, n, False, True, KT + 4)

            def head_sums(i, sq):
                pe.wait_ge(sq_ready, i + 1)
                for p in range(KT):
                    ins = pe.matmul(psum[4][:, 0:T], keep["head_window"][:, 14 - 2 * p:14 - 2 * p + P], sq[:, p],
                                    start=(p == 0), stop=(p == KT - 1))
                ins.then_inc(sums_ready, 1)

            def head_spread(i, r):
                pe.wait_ge(rn_ready, i + 1)
                pe.wait_ge(spread_in, 16 if i == 0 else 32)
                for p in range(KT):
                    ins = pe.matmul(psum[4 + p // 2][:, (p % 2) * T:(p % 2 + 1) * T], SPREAD[:, p], r,
                                    start=(p % 2 == 0), stop=(p % 2 == 1))
                    if p % 2:
                        ins.then_inc(rn_spread, 1)

            def attention(a0, heads, dh, q_of, k_of, E, PT, V_, name, O):
                per = 512 // (MT * dh)

                def head_logits(h):
                    if h >= 2:
                        pe.wait_ge(masked, a0 + h - 1)
                    for m in range(MT):
                        c0, n = (0, P) if m == 0 else (P, T)
                        ins = pe.matmul(psum[h % 2][:, c0:c0 + n], q_of(h)[:, m * P:(m + 1) * P], k_of(h)[:, 0:n],
                                        start=(m == 0), stop=(m == 1))
                    ins.then_inc(logits, 1)

                head_logits(0)
                for h in range(heads + 3):
                    if h + 1 < heads:
                        head_logits(h + 1)
                    g = h - 1
                    if 0 <= g < heads:
                        pe.wait_ge(expd, a0 + g + 1)
                        if g >= 2:
                            pe.wait_ge(pt_ready, a0 + g - 1)
                        for s in range(3):
                            ins = pe.transpose(psum[2 + g % 2][:, s * P:(s + 1) * P], E[:, g % 2, s * P:(s + 1) * P],
                                               ident[:, :])
                        ins.then_inc(e_turned, 1)
                    if h == heads + 1:
                        pe.wait_ge(att_out, a0 // 4 + 2)
                        turn(name, O, (0, 1))
                    g = h - 3
                    if g >= 0:
                        pe.wait_ge(pt_ready, a0 + g + 1)
                        if g % per == 0 and g // per >= 2:
                            pe.wait_ge(att_out, a0 // 4 + g // per - 1)
                        o = psum[6 + (g // per) % 2][:, (g % per) * MT * dh:(g % per + 1) * MT * dh]
                        v = V_[:, :, g * dh:(g + 1) * dh]
                        pt = PT[:, g % 2]
                        pe.matmul(o[:, 0:dh], pt[:, 0:P], v[:, 0], start=(g % per == 0), stop=False)
                        pe.matmul(o[:, dh:2 * dh], pt[:, P:2 * P], v[:, 0], start=False, stop=False)
                        pe.matmul(o[:, dh:2 * dh], pt[:, 2 * P:3 * P], v[:, 1], start=False,
                                  stop=(g % per == per - 1)).then_inc(av_prod, 1)
                pe.wait_ge(att_out, a0 // 4 + 3)
                turn(name, O, (2,))

            def att_ready(a0, name, O):
                def ready(b):
                    if b == 3:
                        pe.wait_ge(att_out, a0 // 4 + 4)
                        turn(name, O, (3,))
                    pe.wait_ge(turned_lo, SPLIT0[TI[name]] + b + 1)
                return ready

            pe.wait_ge(ident_in, 16)
            norm_turn("rwkv")

            def lora_in1(order, w, n, bank):
                for k in range(KT):
                    ins = pe.matmul(psum[bank][0:min(n, P), 0:T], w[:, k, 0:min(n, P)], XM[order % 2][:, k],
                                    start=(k == 0), stop=(k == KT - 1))
                if n > P:
                    for k in range(KT):
                        ins = pe.matmul(psum[bank + 1][0:n - P, 0:T], w[:, k, P:n], XM[order % 2][:, k],
                                        start=(k == 0), stop=(k == KT - 1))
                ins.then_inc(lora1, 1)

            chunk("k", 0, "feature", 0, ready=lambda b: pe.wait_ge(first_lo, b + 1))
            pe.wait_ge(lora_in, 16 * 7)
            pe.wait_ge(mixed, 1)
            lora_in1(1, w1s, LORA, 4)
            chunk("k", 1, "feature", 0)
            pe.wait_ge(mixed, 3)
            lora_in1(3, a1s, LORA, 5)
            chunk("v", 0, "token", 1, ready=lambda b: pe.wait_ge(mix_lo, 1))
            pe.wait_ge(mixed, 5)
            lora_in1(5, g1s, GATE, 6)
            for q, (w2, t1) in enumerate(((w2s, tw), (a2s, ta))):
                for b in range(4):
                    if q == 0:
                        pe.wait_ge(lora1_act, b + 1)
                    else:
                        pe.wait_ge(lora2_read, b + 1)
                    for j in range(2):
                        p = 2 * b + j
                        ins = pe.matmul(psum[4 + b][:, j * T:(j + 1) * T], w2[0:LORA, p * P:(p + 1) * P],
                                        t1[0:LORA, :], start=(j == 0), stop=(j == 1))
                    ins.then_inc(lora2, 1)
            chunk("v", 1, "token", 1)
            for b in range(4):
                m, n = b // 2, b % 2
                pe.wait_ge(lora2_read, 4 + b + 1)
                pe.matmul(psum[4 + b][:, :], sga[:, m * P:(m + 1) * P], g2a[:, n * UN:(n + 1) * UN], start=True,
                          stop=False)
                pe.matmul(psum[4 + b][:, :], sgb[0:GATE - P, m * P:(m + 1) * P], g2b[0:GATE - P, n * UN:(n + 1) * UN],
                          start=False, stop=True).then_inc(lora2, 1)
            pe.wait_ge(lora2_read, 9)
            pe.wait_ge(const_in, 16 * (len(CONST_KEEP) - 2))
            head_sums(0, KKSQ)
            chunk("r", 0, "feature", 0, ready=lambda b: pe.wait_ge(mix_lo, 2))
            pe.wait_ge(lora2_read, 12)
            head_spread(0, rn)
            chunk("r", 1, "feature", 0)
            pe.wait_ge(spread_read, 4)
            pe.wait_ge(rho_ready, 1)
            for r in range(4):
                c = r // 2
                if r:
                    pe.wait_ge(rho_ready, 2)
                    pe.wait_ge(y_ready, 2 * r)
                    pe.wait_ge(state_ready, 4 * min(r, 2))
                for l in range(2):
                    gi = 2 * r + l
                    p0 = 2 * (gi % 4)
                    pe.wait_ge(padded, 4 * (gi + 1))
                    for h in range(4):
                        if gi == 0 and h == 2:
                            pe.wait_ge(acc_read["act"], READ_COUNT[CHUNK0["r"] + 1][1])
                        ar = AR[:, (p0 + h // 2) * 2 + c]
                        for s in range(2):
                            ins = pe.matmul(psum[4 * l + h][:, s * T:(s + 1) * T], PADS[c][l][:, s, h], ar, start=(s == 0),
                                            stop=(s == 1))
                        ins.then_inc(pair_prod, 1)
                for i in range(6):
                    for l in range(2):
                        if i == 0:
                            pe.wait_ge(first_ready, 2 * r + l + 1)
                            for h in range(4):
                                ins = pe.transpose(psum[2 + l][:, h * P:(h + 1) * P], TT_[l][:, h], ident[:, :])
                            ins.then_inc(first_turned, 1)
                            pe.wait_ge(inv_ready, 2 * r + l + 1)
                        else:
                            pe.wait_ge(inv_doubled, 10 * r + 2 * (i - 1) + l + 1)
                        for h in range(4):
                            ins = pe.matmul(psum[l][:, h * P:(h + 1) * P], M[l][:, h, 0:P], TI_[l][:, h],
                                            start=(h == 0), stop=(h == 3))
                        ins.then_inc(half_prod, 1)
                    if r == 0 and i == 2:
                        pe.wait_ge(bonus_prod, 1)
                        for q in range(2 * KT):
                            cq, p = q // KT, q % KT
                            ins = pe.matmul(psum[7][:, 16 * cq + 2 * p:16 * cq + 2 * p + 2],
                                            BONUS[:, p, cq * P:(cq + 1) * P], keep["head_window"][:, 14:16],
                                            start=(q == 0), stop=(q == 2 * KT - 1))
                        ins.then_inc(bonus_sum, 1)
                    for l in range(2):
                        pe.wait_ge(half_masked, 12 * r + 2 * i + l + 1)
                        if i:
                            pe.wait_ge(doubled, 12 * r + 2 * (i - 1) + l + 1)
                        if i < 5:
                            for h in range(4):
                                ins = pe.matmul(psum[2 + l][:, h * P:(h + 1) * P], TT_[l][:, h], PM[l][:, h],
                                                start=(h == 0), stop=(h == 3))
                            ins.then_inc(inv_prod, 1)
                        for h in range(4):
                            ins = pe.matmul(psum[4 + l][:, h * P:(h + 1) * P], PM[l][:, h], TT_[l][:, h],
                                            start=(h == 0), stop=(h == 3))
                        ins.then_inc(step_prod, 1)

                def carried(l, p0, which):
                    for pp in range(2):
                        pe.matmul(psum[6 + l][:, pp * P:(pp + 1) * P], AR[:, (p0 + pp) * 2 + c, which],
                                  S0[:, p0 + pp], start=(pp == 0), stop=False)

                if r == 0:
                    pe.wait_ge(bonus_read, 1)
                for l in range(2):
                    p0 = 2 * ((2 * r + l) % 4)
                    if c:
                        carried(l, p0, 0)
                    for h in range(4):
                        hd = (2 * p0 + h) * HD
                        ins = pe.matmul(psum[6 + l][:, h * HD:(h + 1) * HD], M[l][:, h, 2 * P:3 * P],
                                        V[:, c, hd:hd + HD], start=(c == 0 and h == 0), stop=(h == 3))
                    ins.then_inc(rhs_prod, 1)
                for l in range(2):
                    pe.wait_ge(rhs_ready, 2 * r + l + 1)
                    pe.wait_ge(doubled, 12 * r + 10 + l + 1)
                    for h in range(4):
                        ins = pe.matmul(psum[6 + l][:, h * HD:(h + 1) * HD], TT_[l][:, h],
                                        SA[l][:, h * HD:(h + 1) * HD], start=(h == 0), stop=(h == 3))
                    ins.then_inc(sa_prod, 1)
                for l in range(2):
                    p0 = 2 * ((2 * r + l) % 4)
                    pe.wait_ge(sa_ready, 2 * r + l + 1)
                    if c:
                        carried(l, p0, 1)
                    for h in range(4):
                        hd = (2 * p0 + h) * HD
                        o = psum[6 + l][:, h * HD:(h + 1) * HD]
                        pe.matmul(o, M[l][:, h, P:2 * P], SA[l][:, h * HD:(h + 1) * HD], start=(c == 0 and h == 0),
                                  stop=False)
                        ins = pe.matmul(o, M[l][:, h, 3 * P:4 * P], V[:, c, hd:hd + HD], start=False,
                                        stop=(h == 3))
                    ins.then_inc(y_prod, 1)
                if c == 0:
                    for l in range(2):
                        p0 = 2 * (2 * r + l)
                        for s, src in enumerate((BE, kT)):
                            for pp in range(2):
                                k = (2 * s + pp) * P
                                ins = pe.transpose(psum[l][:, k:k + P], src[:, p0 + pp, 0:P], ident[:, :])
                        ins.then_inc(keys_turned, 1)
                    for l in range(2):
                        p0 = 2 * (2 * r + l)
                        pe.wait_ge(keys_ready, 2 * r + l + 1)
                        for pp in range(2):
                            o = psum[2 + l][:, pp * P:(pp + 1) * P]
                            pe.matmul(o, PM[l][:, pp], SA[l][:, pp * P:(pp + 1) * P], start=(pp == 0), stop=False)
                            ins = pe.matmul(o, PM[l][:, 2 + pp], V[:, 0, (p0 + pp) * P:(p0 + pp + 1) * P],
                                            start=False, stop=(pp == 1))
                        ins.then_inc(state_prod, 1)
            pe.wait_ge(y_done, 3)
            turn("rwo", Y, (0, 1))

            def rwo_ready(b):
                if b == 2:
                    pe.wait_ge(y_done, 4)
                    turn("rwo", Y, (2, 3))
                pe.wait_ge(turned_lo, b + 1)

            for n in range(2):
                chunk("rwo", n, "token", ready=rwo_ready)
            norm_turn("mlp0")
            mlp(0)
            norm_turn("kv")
            pe.wait_ge(turned_lo, SPLIT0[TI["attn"]])
            turn("attn", XN)
            chunk("fk", 0, "feature", ready=split_ready("kv"))
            chunk("fk", 1, "feature")
            chunk("fq", 0, "feature", 1, ready=lambda b: pe.wait_ge(turned_lo, SPLIT0[TI["fo"]]))
            head_sums(1, fSQ)
            chunk("fq", 1, "feature", 1)
            head_spread(1, frn)
            chunk("fv", 0, "token")
            pe.wait_ge(spread_read, 8)
            head_sums(2, fSQ)
            pe.wait_ge(fox_in, 16 * 3)
            for part in (XH, XL):
                for k in range(KT):
                    ins = pe.matmul(psum[5][0:NH, 0:T], wf[:, k], part[:, k].bitcast(F32),
                                    start=(part is XH and k == 0), stop=(part is XL and k == KT - 1))
            ins.then_inc(f_prod, 1)
            pe.wait_ge(f_z, 1)
            head_spread(2, frn)
            chunk("fv", 1, "token")
            pe.wait_ge(spread_read, 12)
            pe.wait_ge(bias_in, 16 * 4)
            attention(0, NH, HD, lambda h: fQ2[h % 2][:, h // 2], lambda h: fKP[:, h], fE, fPT, fV, "fo", fO)
            for n in range(2):
                chunk("fo", n, "token", ready=att_ready(0, "fo", fO))
            norm_turn("mlp1")
            mlp(1)
            norm_turn("ret")
            for name in ("rq", "rk"):
                for n in range(2):
                    chunk(name, n, "feature", ready=split_ready("ret"))
            for name in ("rv", "rg"):
                for n in range(4):
                    chunk(name, n, "token")
            pe.wait_ge(acc_read["act"], READ_COUNT[CHUNK0["rg"] + 3][1])
            pe.wait_ge(rotated, 2 * RET_H)

            def ret_scores(h):
                for m in range(MT):
                    o = psum[h][:, 0:T] if m == 0 else psum[h][:, T:T + P]
                    for e in range(2):
                        ins = pe.matmul(o, rK[:, h, e, m * P:(m + 1) * P], rQ[:, h, e, m * P:T],
                                        start=(m == 0 and e == 0), stop=(m == 1 and e == 1))
                ins.then_inc(scores, 1)

            def ret_values(h):
                pe.wait_ge(decayed, h + 1)
                v = rV[:, :, h * RET_DV:(h + 1) * RET_DV]
                pt, b = rPT[:, h % 2], RET_BANK[h]
                pe.matmul(psum[b][:, :], pt[:, 0:P], v[:, 0], start=True, stop=True).then_inc(ret_prod, 1)
                pe.matmul(psum[b + 1][:, :], pt[:, P:2 * P], v[:, 0], start=True, stop=False)
                pe.matmul(psum[b + 1][:, :], pt[:, 2 * P:3 * P], v[:, 1], start=False, stop=True)\
                    .then_inc(ret_prod, 1)

            ret_scores(0)
            for h in range(3):
                ret_scores(h + 1)
                ret_values(h)
            ret_values(3)
            pe.wait_ge(ret_out, 4)
            turn("reo", rG, range(4))

            def reo_ready(b):
                if b in (2, 4):
                    pe.wait_ge(ret_out, 6 if b == 2 else 8)
                    turn("reo", rG, range(b + 2, b + 4))
                pe.wait_ge(turned_lo, SPLIT0[TI["reo"]] + b + 1)

            for n in range(2):
                chunk("reo", n, "token", kts=2 * KT, ready=reo_ready)
            norm_turn("mlp2")
            mlp(2)
            norm_turn("moba")

            def rope_swap(i, name, src):
                pe.wait_ge(acc_read["act"], READ_COUNT[CHUNK0[name] + 1][1])
                pe.wait_ge(moba_in, 16 * 4)
                for b in range(4):
                    if i:
                        pe.wait_ge(roped, b + 1)
                    for j in range(2):
                        ins = pe.matmul(psum[4 + b][0:ROPE, j * T:(j + 1) * T], mSWAP, src[:, 2 * b + j],
                                        start=(j == 0), stop=(j == 1))
                    ins.then_inc(rope_swapped, 1)

            chunk("mq", 0, "feature", ready=split_ready("moba"))
            chunk("mq", 1, "feature")
            chunk("mk", 0, "feature")
            rope_swap(0, "mq", mQ)
            chunk("mk", 1, "feature")
            chunk("mv", 0, "token")
            rope_swap(1, "mk", mK)
            chunk("mv", 1, "token")
            pe.wait_ge(acc_read["act"], READ_COUNT[CHUNK0["mv"]][1])
            pe.wait_ge(roped, 8)
            attention(NH, MOBA_H, MOBA_D, lambda h: mQ[:, h], lambda h: mK[:, h], mE, mPT, mV, "mo", mO)
            for n in range(2):
                chunk("mo", n, "token", ready=att_ready(NH, "mo", mO))
            norm_turn("mlp3")
            mlp(3)


def pack(w):
    k, n = w.shape
    return w.reshape(k // 512, UK, P, n // UN, UN).transpose(3, 0, 2, 1, 4).reshape(-1, P, UK * UN)


def pack_mlp(w_in, w_out):
    up, down = pack(w_in), pack(w_out)
    units = [up[0], up[1]]
    for j in range(1, MLP_STEPS):
        units += [up[2 * j], up[2 * j + 1], down[j - 1], down[MLP_STEPS + j - 1]]
    units += [down[MLP_STEPS - 1], down[2 * MLP_STEPS - 1]]
    return np.stack(units)


def by_partition(w):
    return w.reshape(-1, P, w.shape[1]).transpose(1, 0, 2).reshape(P, -1)


def laid_out(i):
    f = {k: np.asarray(v) for k, v in i.items()}
    o = {"x": f["x"].reshape(MT, P, D).transpose(1, 0, 2)}
    per = {"rwkv_norm_g": f["rwkv_norm_g"][0], "w0": f["rwkv_w0"][0], "a0": f["rwkv_a0"][0],
           "k_k": f["rwkv_k_k"][0], "k_a": f["rwkv_k_a"][0], "r_k": f["rwkv_r_k"][0],
           "kv_norm_g": f["kv_norm_g"], "k_norm_g": f["k_norm_g"], "attn_norm_g": f["attn_norm_g"][0],
           "q_norm_g": f["q_norm_g"][0], "mlp_norm_g0": f["mlp_norm_g"][0], "mlp_norm_g1": f["mlp_norm_g"][1],
           "ln_mix_pre_0": f["ln_mix_pre_0_2"], "ln_mlp_pre_0": f["ln_mlp_pre_0_2"],
           "ln_mix_pre_1": f["ln_mix_pre_1_2"], "ln_mlp_pre_1": f["ln_mlp_pre_1_2"]}
    per |= {f"mu{m}": f["rwkv_mu"][0, m] for m in range(6)}
    o["vecs"] = np.stack([per[n].reshape(KT, P).T for n in VECS], 1).reshape(P, -1)
    rows = {"lnx_w": f["rwkv_lnx_w"][0], "lnx_b": f["rwkv_lnx_b"][0]}
    rows |= {n: f[n + "_2"] for n in ROWS[2:]}
    o |= {n: rows[n].reshape(1, D) for n in ROWS}
    o["w1"], o["a1"], o["g1"] = (by_partition(f[n][0]) for n in ("rwkv_w1", "rwkv_a1", "rwkv_g1"))
    o["w2"], o["a2"] = f["rwkv_w2"][0], f["rwkv_a2"][0]
    o["g2a"], o["g2b"] = f["rwkv_g2"][0, :P], f["rwkv_g2"][0, P:]
    o["wf"] = by_partition(np.concatenate([f["kv_w"][:, 2 * D::2], f["kv_w"][:, 2 * D + 1::2]], 1))
    o["f_bias"] = np.concatenate([f["kv_f_bias"].reshape(-1)[::2], f["kv_f_bias"].reshape(-1)[1::2]]).reshape(NH, 1)
    cols = np.arange(D).reshape(RET_H, P, 2).transpose(0, 2, 1).reshape(-1)
    ret, mo = f["w_in_0_2"], f["w_in_1_2"]
    w = {"r": f["rwkv_w_rkv"][0, 0], "k": f["rwkv_w_rkv"][0, 1], "v": f["rwkv_w_rkv"][0, 2],
         "rwo": f["rwkv_w_o"][0], "fk": f["kv_w"][:, :D], "fv": f["kv_w"][:, D:2 * D],
         "fq": f["attn_w_q"][0], "fo": f["attn_w_o"][0],
         "rq": ret[:, :D][:, cols], "rk": ret[:, D:2 * D][:, cols], "rv": ret[:, 2 * D:4 * D], "rg": ret[:, 4 * D:],
         "reo": f["w_out_0_2"], "mq": mo[:, :D], "mk": mo[:, D:2 * D], "mv": mo[:, 2 * D:], "mo": f["w_out_1_2"]}
    o |= {"w_" + n: pack(m) for n, m in w.items()}
    o["w_mlp0"] = pack_mlp(f["mlp_w_in"][0], f["mlp_w_out"][0])
    o["w_mlp1"] = pack_mlp(f["mlp_w_in"][1], f["mlp_w_out"][1])
    o["w_mlp2"] = pack_mlp(f["w_up_0_2"], f["w_down_0_2"])
    o["w_mlp3"] = pack_mlp(f["w_up_1_2"], f["w_down_1_2"])
    o |= constants()
    return {k: np.ascontiguousarray(v) for k, v in o.items()}


def kernel(**inputs):
    import concourse.bacc as bacc
    from concourse.bass_utils import run_bass_kernel_spmd

    nc = bacc.Bacc("TRN2", target_bir_lowering=False, num_devices=1)
    arrays = {f"in_{k}": v for k, v in laid_out(inputs).items()}
    a = {k[3:]: nc.dram_tensor(k, v.shape, mybir.dt.from_np(v.dtype), kind="ExternalInput").ap()
         for k, v in arrays.items()}
    out = nc.dram_tensor("out", (1, T, D), F32, kind="ExternalOutput").ap()
    build(nc, a, out)
    return run_bass_kernel_spmd(nc, [arrays], core_ids=[0]).results[0]["out"]
```
